# Optimizing a Trainium2 kernel written in Bass

```python
import math
import jax, jax.numpy as jnp
from jax import lax
import numpy as np

D_MODEL = 1024
BATCH = 1
SEQ = 1024
DEPTH = 1

CTX_LEN = 256
GRID_W = 64
D_MIX = D_MODEL
D_CONV = D_MIX // 2
D_RWKV = D_MIX - D_CONV
RWKV_HEAD = 64
RWKV_HEADS = D_RWKV // RWKV_HEAD
W_LORA = 64
A_LORA = 64
G_LORA = 128
N_DIR = 2
D_FF = ((8 * D_MODEL // 3 + 127) // 128) * 128
PROJ = 3 * D_CONV + 3 * D_RWKV + W_LORA + A_LORA + G_LORA
RMS_EPS = 1e-6
GN_EPS = 64e-5
DECAY_SCALE = math.exp(-0.5)


def rms_norm(x, g):
    xf = x.astype(jnp.float32)
    y = xf * lax.rsqrt(jnp.mean(xf * xf, axis=-1, keepdims=True) + RMS_EPS)
    return (y * g.astype(jnp.float32)).astype(x.dtype)

def modulate(h, shift, scale):
    return h * (1 + scale) + shift

def split_proj(p):
    sizes = (D_CONV, D_CONV, D_CONV, D_RWKV, D_RWKV, D_RWKV, W_LORA, A_LORA, G_LORA)
    idx = [int(i) for i in np.cumsum(sizes)[:-1]]
    return jnp.split(p, idx, axis=-1)

def shortconv1d(u, w):
    up = jnp.pad(u, ((0, 0), (1, 1), (0, 0)))
    return up[:, :-2] * w[0] + up[:, 1:-1] * w[1] + up[:, 2:] * w[2]

def dwconv_grid(u, w, b, rows, cols):
    bsz, t, ch = u.shape
    img = u.reshape(bsz, rows, cols, ch)
    out = lax.conv_general_dilated(img, w[:, :, None, :].astype(u.dtype), (1, 1), "SAME",
                                   dimension_numbers=("NHWC", "HWIO", "NHWC"),
                                   feature_group_count=ch)
    return out.reshape(bsz, t, ch) + b

def to_heads(t):
    return t.astype(jnp.float32).reshape(t.shape[0], t.shape[1], RWKV_HEADS, RWKV_HEAD)

def wkv_scan(state0, r, decay, kk, b, v, k, reverse):
    def step(S, inp):
        r_t, w_t, kk_t, b_t, v_t, k_t = inp
        sa = jnp.einsum("bhvk,bhk->bhv", S, kk_t)
        S = (S * w_t[:, :, None, :] - sa[..., None] * b_t[:, :, None, :]
             + v_t[..., None] * k_t[:, :, None, :])
        return S, jnp.einsum("bhvk,bhk->bhv", S, r_t)
    xs = tuple(jnp.swapaxes(t, 0, 1) for t in (r, decay, kk, b, v, k))
    S, ys = lax.scan(step, state0, xs, reverse=reverse)
    return S, jnp.swapaxes(ys, 0, 1)

def rwkv_scans(r, k, v, w_lo, a_lo, lp, init):
    kk = to_heads(k * lp["k_k"])
    kk = kk * lax.rsqrt(jnp.maximum(jnp.sum(kk * kk, axis=-1, keepdims=True), 1e-24))
    rh, vh = to_heads(r), to_heads(v)
    y_sum = None
    finals = []
    for d in range(N_DIR):
        decay = jnp.exp(-DECAY_SCALE * jax.nn.sigmoid(lp["w0"][d] + jnp.tanh(w_lo) @ lp["w_up"][d]))
        a = jax.nn.sigmoid(lp["a0"][d] + a_lo @ lp["a_up"][d])
        k_d = k * (1 + (a - 1) * lp["k_a"])
        state, y = wkv_scan(init[d], rh, to_heads(decay), kk, kk * to_heads(a), vh, to_heads(k_d),
                            reverse=(d == 1))
        y_sum = y if y_sum is None else y_sum + y
        finals.append(state)
    return y_sum, finals

def rwkv_output(y, r, k, v, g_lo, lp):
    bsz, t = y.shape[:2]
    mu = jnp.mean(y, axis=-1, keepdims=True)
    var = jnp.mean(jnp.square(y - mu), axis=-1, keepdims=True)
    yn = ((y - mu) * lax.rsqrt(var + GN_EPS)).reshape(bsz, t, D_RWKV) * lp["ln_g"] + lp["ln_b"]
    bonus = jnp.sum(to_heads(r) * to_heads(k) * lp["r_k"].astype(jnp.float32), axis=-1, keepdims=True) * to_heads(v)
    gate = jax.nn.sigmoid(g_lo) @ lp["g_up"]
    return ((yn + bonus.reshape(bsz, t, D_RWKV)) * gate).astype(r.dtype)

def mixer_block(h, lp, init, need_output):
    cb, cc, cx, r, k, v, w_lo, a_lo, g_lo = split_proj(h @ lp["w_in"])
    y, finals = rwkv_scans(r, k, v, w_lo, a_lo, lp, init)
    if not need_output:
        return None, finals
    y_conv = cb * shortconv1d(cc * cx, lp["conv_a_w"])
    y_rwkv = rwkv_output(y, r, k, v, g_lo, lp)
    return jnp.concatenate([y_conv, y_rwkv], axis=-1) @ lp["w_out"], finals

def conv_ffn(h, lp, rows, cols):
    gate, val = jnp.split(h @ lp["ffn_w_up"], 2, axis=-1)
    gate = dwconv_grid(gate, lp["ffn_conv_w"], lp["ffn_conv_b"], rows, cols)
    return (jax.nn.silu(gate) * val) @ lp["ffn_w_down"]

def first_inputs(seed: int = 0) -> dict:
    key = jax.random.key(seed)
    ks = jax.random.split(key, 32)
    L, D = DEPTH, D_MODEL

    def nrm(k, shape, s):
        return jax.random.normal(k, shape, jnp.float32) * s

    return {
        "x": nrm(ks[0], (BATCH, SEQ, D), 1.0),
        "c": nrm(ks[1], (BATCH, D), 1.0),
        "ctx": nrm(ks[2], (BATCH, CTX_LEN, D), 1.0),
        "c_ctx": nrm(ks[3], (D,), 1.0),
        "ada_w": nrm(ks[4], (L, D, 6 * D), 0.5 * D ** -0.5),
        "ada_b": nrm(ks[5], (L, 6 * D), 0.01),
        "norm1_g": 1.0 + nrm(ks[6], (L, D), 0.1),
        "norm2_g": 1.0 + nrm(ks[7], (L, D), 0.1),
        "w_in": nrm(ks[8], (L, D, PROJ), D ** -0.5),
        "conv_a_w": nrm(ks[9], (L, 3, D_CONV), 3 ** -0.5),
        "rw_w0": nrm(ks[10], (L, N_DIR, D_RWKV), 0.5),
        "rw_w_up": nrm(ks[11], (L, N_DIR, W_LORA, D_RWKV), 0.5 * W_LORA ** -0.5),
        "rw_a0": nrm(ks[12], (L, N_DIR, D_RWKV), 0.5),
        "rw_a_up": nrm(ks[13], (L, N_DIR, A_LORA, D_RWKV), 0.5 * A_LORA ** -0.5),
        "rw_k_k": 0.85 + nrm(ks[14], (L, D_RWKV), 0.05),
        "rw_k_a": 1.0 + nrm(ks[15], (L, D_RWKV), 0.05),
        "rw_r_k": nrm(ks[16], (L, RWKV_HEADS, RWKV_HEAD), 0.1),
        "rw_g_up": nrm(ks[17], (L, G_LORA, D_RWKV), G_LORA ** -0.5),
        "rw_ln_g": 1.0 + nrm(ks[18], (L, D_RWKV), 0.1),
        "rw_ln_b": nrm(ks[19], (L, D_RWKV), 0.01),
        "w_out": nrm(ks[20], (L, D_MIX, D), D_MIX ** -0.5),
        "ffn_w_up": nrm(ks[21], (L, D, 2 * D_FF), D ** -0.5),
        "ffn_conv_w": nrm(ks[22], (L, 3, 3, D_FF), 1.0 / 3.0),
        "ffn_conv_b": nrm(ks[23], (L, D_FF), 0.01),
        "ffn_w_down": nrm(ks[24], (L, D_FF, D), D_FF ** -0.5),
        "final_g": 1.0 + nrm(ks[25], (D,), 0.1),
    }

def first_block(x, c, ctx, c_ctx, ada_w, ada_b, norm1_g, norm2_g, w_in, conv_a_w,
              rw_w0, rw_w_up, rw_a0, rw_a_up, rw_k_k, rw_k_a, rw_r_k, rw_g_up, rw_ln_g, rw_ln_b,
              w_out, ffn_w_up, ffn_conv_w, ffn_conv_b, ffn_w_down, final_g):
    bsz = x.shape[0]
    rows = x.shape[1] // GRID_W
    zero_state = jnp.zeros((bsz, RWKV_HEADS, RWKV_HEAD, RWKV_HEAD), jnp.float32)
    for l in range(DEPTH):
        last = l == DEPTH - 1
        lp = {
            "w_in": w_in[l], "conv_a_w": conv_a_w[l], "w0": rw_w0[l], "w_up": rw_w_up[l],
            "a0": rw_a0[l], "a_up": rw_a_up[l], "k_k": rw_k_k[l], "k_a": rw_k_a[l],
            "r_k": rw_r_k[l], "g_up": rw_g_up[l], "ln_g": rw_ln_g[l], "ln_b": rw_ln_b[l],
            "w_out": w_out[l], "ffn_w_up": ffn_w_up[l], "ffn_conv_w": ffn_conv_w[l],
            "ffn_conv_b": ffn_conv_b[l], "ffn_w_down": ffn_w_down[l],
        }
        mod = jax.nn.silu(c) @ ada_w[l] + ada_b[l]
        sh1, sc1, g1, sh2, sc2, g2 = [m[:, None, :] for m in jnp.split(mod, 6, axis=-1)]
        csh1, csc1, cg1, csh2, csc2, cg2 = jnp.split(jax.nn.silu(c_ctx) @ ada_w[l] + ada_b[l], 6, axis=-1)

        hc = modulate(rms_norm(ctx, norm1_g[l]), csh1, csc1)
        out_c, ctx_states = mixer_block(hc, lp, (zero_state, zero_state), not last)

        hx = modulate(rms_norm(x, norm1_g[l]), sh1, sc1)
        out_x, _ = mixer_block(hx, lp, ctx_states, True)
        x = x + g1 * out_x
        hx = modulate(rms_norm(x, norm2_g[l]), sh2, sc2)
        x = x + g2 * conv_ffn(hx, lp, rows, GRID_W)

        if not last:
            ctx = ctx + cg1 * out_c
            hc = modulate(rms_norm(ctx, norm2_g[l]), csh2, csc2)
            ctx = ctx + cg2 * conv_ffn(hc, lp, 1, ctx.shape[1])
    return rms_norm(x, final_g)


HEAD_DIM = 64
FOX_HEADS = 8
SB_HEADS = 4
POOL_GROUPS = 4
POOL_WINDOWS = (2, 4, 8, 16)
POOL_GROUP_DIM = 64
FOX_W = FOX_HEADS * HEAD_DIM
SB_W = SB_HEADS * HEAD_DIM
POOL_W = POOL_GROUPS * POOL_GROUP_DIM
D_MIX_2 = FOX_W + POOL_W + SB_W
Q_BLOCK = 128
EPS = 1e-6
NEG = -1e30

IN_SPLITS = (
    FOX_W, FOX_W, FOX_W, FOX_W,
    FOX_HEADS,
    POOL_W, POOL_W,
    SB_W, SB_W, SB_W, SB_W,
)
D_IN = sum(IN_SPLITS)


def rms_norm_2(x, g):
    xf = x.astype(jnp.float32)
    y = xf * lax.rsqrt(jnp.mean(xf * xf, axis=-1, keepdims=True) + EPS)
    return (y * g.astype(jnp.float32)).astype(x.dtype)

def to_heads_2(t, n_heads):
    b, s, _ = t.shape
    return t.reshape(b, s, n_heads, HEAD_DIM).transpose(0, 2, 1, 3)

def from_heads(t):
    b, h, s, d = t.shape
    return t.transpose(0, 2, 1, 3).reshape(b, s, h * d)

def split_blocks(t):
    b, h, s = t.shape[:3]
    nb = s // Q_BLOCK
    t = t.reshape((b, h, nb, Q_BLOCK) + t.shape[3:])
    return jnp.moveaxis(t, 2, 0)

def merge_blocks(o):
    nb, b, h, qb, d = o.shape
    return jnp.moveaxis(o, 0, 2).reshape(b, h, nb * qb, d)

def forgetting_attention(q, k, v, log_f):
    s_len, d = q.shape[2], q.shape[3]
    c = jnp.cumsum(log_f, axis=-1)
    kpos = jnp.arange(s_len)
    scale = d ** -0.5

    def one_block(args):
        qi, ci, i = args
        qpos = i * Q_BLOCK + jnp.arange(Q_BLOCK)
        sc = jnp.einsum('bhqd,bhkd->bhqk', qi, k).astype(jnp.float32) * scale
        sc = sc + (ci[..., :, None] - c[..., None, :])
        sc = jnp.where(kpos[None, :] <= qpos[:, None], sc, NEG)
        p = jax.nn.softmax(sc, axis=-1)
        return jnp.einsum('bhqk,bhkd->bhqd', p.astype(v.dtype), v)

    nb = s_len // Q_BLOCK
    o = lax.map(one_block, (split_blocks(q), split_blocks(c), jnp.arange(nb)))
    return merge_blocks(o)

def stick_breaking_attention(q, k, v):
    s_len, d = q.shape[2], q.shape[3]
    kpos = jnp.arange(s_len)
    scale = d ** -0.5

    def one_block(args):
        qi, i = args
        qpos = i * Q_BLOCK + jnp.arange(Q_BLOCK)
        z = jnp.einsum('bhqd,bhkd->bhqk', qi, k).astype(jnp.float32) * scale
        causal = kpos[None, :] < qpos[:, None]
        log_1m_beta = jnp.where(causal, -jax.nn.softplus(z), 0.0)
        rest = lax.cumsum(log_1m_beta, axis=3, reverse=True) - log_1m_beta
        a = jnp.where(causal, jnp.exp(jax.nn.log_sigmoid(z) + rest), 0.0)
        return jnp.einsum('bhqk,bhkd->bhqd', a.astype(v.dtype), v)

    nb = s_len // Q_BLOCK
    o = lax.map(one_block, (split_blocks(q), jnp.arange(nb)))
    return merge_blocks(o)

def causal_window_mean(x, w):
    s_len = x.shape[1]
    xf = x.astype(jnp.float32)
    cs = jnp.cumsum(xf, axis=1)
    cs_prev = jnp.pad(cs, ((0, 0), (w, 0), (0, 0)))[:, :s_len]
    count = jnp.minimum(jnp.arange(s_len) + 1, w).astype(jnp.float32)
    return ((cs - cs_prev) / count[None, :, None]).astype(x.dtype)

def multiscale_pool(x, w_pool, scale):
    b, s_len, _ = x.shape
    groups = jnp.split(x, POOL_GROUPS, axis=-1)
    pooled = jnp.stack([causal_window_mean(g, w) - g for g, w in zip(groups, POOL_WINDOWS)], axis=2)
    y = jnp.einsum('bsgc,gcd->bsgd', pooled, w_pool).reshape(b, s_len, POOL_W)
    return y * scale

def hybrid_layer(x, norm_g, w_in, b_f, q_norm_g, k_norm_g, w_pool, pool_scale, w_out):
    h = rms_norm_2(x, norm_g)
    proj = jnp.einsum('bsd,de->bse', h, w_in)
    idx = np.cumsum(IN_SPLITS)[:-1].tolist()
    (fq, fk, fv, fg, ff, px, pg, sq, sk, sv, sg) = jnp.split(proj, idx, axis=-1)

    fq = rms_norm_2(to_heads_2(fq, FOX_HEADS), q_norm_g)
    fk = rms_norm_2(to_heads_2(fk, FOX_HEADS), k_norm_g)
    fv = to_heads_2(fv, FOX_HEADS)
    log_f = jax.nn.log_sigmoid((ff + b_f).astype(jnp.float32)).transpose(0, 2, 1)
    fox_out = from_heads(forgetting_attention(fq, fk, fv, log_f)) * jax.nn.silu(fg)

    pool_out = multiscale_pool(px, w_pool, pool_scale) * jax.nn.silu(pg)

    sb = stick_breaking_attention(to_heads_2(sq, SB_HEADS), to_heads_2(sk, SB_HEADS), to_heads_2(sv, SB_HEADS))
    sb_out = from_heads(sb) * jax.nn.silu(sg)

    mixed = jnp.concatenate([fox_out, pool_out, sb_out], axis=-1)
    return x + jnp.einsum('bse,ed->bsd', mixed, w_out)

def second_inputs(seed: int = 0) -> dict:
    key = jax.random.key(seed)
    ks = jax.random.split(key, 10)
    x = jax.random.normal(ks[0], (BATCH, SEQ, D_MODEL), jnp.float32)
    norm_g = 1.0 + 0.02 * jax.random.normal(ks[1], (DEPTH, D_MODEL), jnp.float32)
    w_in = jax.random.normal(ks[2], (DEPTH, D_MODEL, D_IN), jnp.float32) * D_MODEL ** -0.5
    b_f = jax.random.uniform(ks[3], (DEPTH, FOX_HEADS), jnp.float32, 1.0, 4.0)
    q_norm_g = 1.0 + 0.02 * jax.random.normal(ks[4], (DEPTH, HEAD_DIM), jnp.float32)
    k_norm_g = 1.0 + 0.02 * jax.random.normal(ks[5], (DEPTH, HEAD_DIM), jnp.float32)
    w_pool = jax.random.normal(ks[6], (DEPTH, POOL_GROUPS, POOL_GROUP_DIM, POOL_GROUP_DIM), jnp.float32) * POOL_GROUP_DIM ** -0.5
    pool_scale = 1.0 + 0.02 * jax.random.normal(ks[7], (DEPTH, POOL_W), jnp.float32)
    w_out = jax.random.normal(ks[8], (DEPTH, D_MIX_2, D_MODEL), jnp.float32) * D_MIX_2 ** -0.5
    return {"x": x, "norm_g": norm_g, "w_in": w_in, "b_f": b_f, "q_norm_g": q_norm_g,
            "k_norm_g": k_norm_g, "w_pool": w_pool, "pool_scale": pool_scale, "w_out": w_out}

def second_block(x, norm_g, w_in, b_f, q_norm_g, k_norm_g, w_pool, pool_scale, w_out):
    for l in range(DEPTH):
        x = hybrid_layer(x, norm_g[l], w_in[l], b_f[l], q_norm_g[l], k_norm_g[l],
                         w_pool[l], pool_scale[l], w_out[l])
    return x


def setup_inputs(seed=0):
    out = dict(first_inputs(seed))
    for name, value in second_inputs(seed + 1).items():
        if name != "x":
            out[name + "_2"] = value
    return out


def reference(
    x, c, ctx, c_ctx, ada_w, ada_b, norm1_g, norm2_g, w_in, conv_a_w, rw_w0, rw_w_up, rw_a0,
    rw_a_up, rw_k_k, rw_k_a, rw_r_k, rw_g_up, rw_ln_g, rw_ln_b, w_out, ffn_w_up, ffn_conv_w,
    ffn_conv_b, ffn_w_down, final_g, norm_g_2, w_in_2, b_f_2, q_norm_g_2, k_norm_g_2, w_pool_2,
    pool_scale_2, w_out_2,
):
    x = first_block(
        x, c, ctx, c_ctx, ada_w, ada_b, norm1_g, norm2_g, w_in, conv_a_w, rw_w0, rw_w_up, rw_a0,
        rw_a_up, rw_k_k, rw_k_a, rw_r_k, rw_g_up, rw_ln_g, rw_ln_b, w_out, ffn_w_up, ffn_conv_w,
        ffn_conv_b, ffn_w_down, final_g,
    )
    return second_block(
        x, norm_g_2, w_in_2, b_f_2, q_norm_g_2, k_norm_g_2, w_pool_2, pool_scale_2, w_out_2,
    )


_drawn_inputs = setup_inputs


def setup_inputs(seed=0):
    import zlib

    import numpy as np

    out = dict(_drawn_inputs(seed))
    spreads = {}
    factors = {'ctx': 8.0,
     'c_ctx': 8.0,
     'ada_b': 3.484,
     'rw_w0': 2.736,
     'rw_w_up': 7.157,
     'rw_k_k': 8.0,
     'rw_k_a': 7.414,
     'rw_ln_g': 4.995,
     'rw_ln_b': 8.0,
     'ffn_conv_b': 8.0,
     'norm_g_2': 5.069,
     'q_norm_g_2': 8.0,
     'k_norm_g_2': 8.0,
     'pool_scale_2': 8.0}
    for name, (base, spread) in spreads.items():
        noise = np.random.default_rng([zlib.crc32(name.encode()), seed]).standard_normal(out[name].shape)
        drawn = base * np.exp(spread * noise) if base else spread * noise
        out[name] = __import__('jax').numpy.asarray(drawn.astype(out[name].dtype))
    for name, factor in factors.items():
        out[name] = (out[name] * factor).astype(out[name].dtype)
    return out
```

```python
import numpy as np
import concourse.bass as bass
import concourse.mybir as mybir
from contextlib import ExitStack

F32 = mybir.dt.float32
F32R = mybir.dt.float32r
ALU = mybir.AluOpType
ACT = mybir.ActivationFunctionType

P = 128
D = 1024
KD = D // P
SEQ, CTX = 1024, 256
TOK = CTX + SEQ
HEAD = 64
CH = 512
PAIRS = CH // P
NFF = 22
GRID_W = 64
GRID_H = SEQ // GRID_W
C = 64
NCTX, NSEQ = CTX // C, SEQ // C
STEPS = NCTX + NSEQ
SLOTS = STEPS + NCTX
LEVELS = 5
DECAY_SCALE = float(np.exp(-0.5))
RMS_EPS, GN_EPS = 1e-6, 64e-5
BANK = 512

VECS = {}
_at = 0
for _name, _n in (("norm1_g", 8), ("norm2_g", 8), ("final_g", 8), ("norm_g_2", 8), ("ada_b", 48),
                  ("conv_a_w", 12), ("w0a0", 16), ("k_k", 4), ("k_a", 4), ("r_k", 4), ("ln_g", 4),
                  ("ln_b", 4), ("ffn_conv_w", 9 * NFF), ("ffn_conv_b", NFF), ("pool_scale", 2),
                  ("cc", 16), ("qg", 1), ("kg", 1), ("b_f", 1)):
    VECS[_name] = (_at, _n)
    _at += _n
NVEC = _at

CONS = {}
_at = 0
for _name, _n in (("ident", P), ("ones", P), ("headones", P), ("identc", C), ("negcausal", P),
                  ("negstrict", P), ("mask_ll", 2 * 2 * C), ("mask_mm", 2 * 2 * C), ("mask_l1", 2 * C),
                  ("mask_u1", 2 * C), ("mask_lev", 2 * LEVELS * C), ("reset", 2 * PAIRS * C),
                  ("headsel", 8), ("invcount", 2 * 16), ("invwin", 2)):
    CONS[_name] = (_at, _n)
    _at += _n
NCON = _at


def bc(ap, axis, n):
    shape = list(ap.shape)
    return ap.unsqueeze(axis).broadcast_to(shape[:axis] + [n] + shape[axis:])


class Sems:

    def __init__(self, nc, stack, prefix):
        self.nc, self.prefix, self.known = nc, prefix, {}
        stack.callback(self.close)

    def __call__(self, name):
        if name not in self.known:
            self.known[name] = self.nc.alloc_semaphore(name=self.prefix + name)
        return self.known[name]

    def close(self):
        self.nc.clear_and_free_semaphores(list(self.known.values()))
        self.nc.all_engine_barrier()


def hold(eng, gate, sem, value):
    eng.wait_ge(sem, value)
    if not isinstance(value, int):
        eng.sem_inc(gate, 1)


def held(eng, value):
    return value if isinstance(value, int) else eng.snap(value)


def product(nc, out, w_hi, w_lo, x_hi, x_lo, nk, cols):
    for k in range(nk):
        for n, (w, x) in enumerate(((w_hi, x_hi), (w_hi, x_lo), (w_lo, x_hi))):
            last = nc.tensor.matmul(out, w[:, k, :], x[:, k, cols], start=(k == 0 and n == 0),
                                    stop=(k == nk - 1 and n == 2))
    return last


def prologue(nc, d, t):
    groups = [(0, CTX, 1), (CTX, BANK, 0), (CTX + BANK, BANK, 0)]
    NADA = 2
    GADA = 16 // NADA
    with ExitStack() as st:
        sem = Sems(nc, st, "a_")
        sb = lambda n, s, dt=F32: st.enter_context(nc.sbuf_tensor("a_" + n, s, dt))
        xin = sb("xin", [P, KD, TOK])
        tmp = sb("tmp", [P, KD, TOK])
        rstd = sb("rstd", [P, TOK])
        adaw = sb("adaw", [P, 2, NADA, KD, P])
        silu_c = t["silu_c"]
        gain = sb("gain", [P, 2, KD])
        ps = [st.enter_context(nc.psum_tensor(f"a_ps{n}", [P, BANK], F32)) for n in range(4)]
        modps = ps[3][:, 0:32].rearrange("p (n c) -> p n c", c=2)
        vec, con = t["vec"], t["con"]
        block = st.enter_context(nc.Block())

        @block.sync
        def _(sp):
            sp.dma_start(vec, d["vecs"]).then_inc(sem("vecs"), 16)
            sp.dma_start(con, d["consts"]).then_inc(sem("consts"), 16)
            sp.dma_start(xin[:, :, 0:CTX], d["ctxT"]).then_inc(sem("x0"), 16)
            for n in range(2):
                sp.dma_start(adaw[:, n], d["ada"][n]).then_inc(sem(f"ada{n}"), 16)
            for g in (1, 2):
                sp.dma_start(xin[:, :, CTX + BANK * (g - 1):CTX + BANK * g],
                             d["xT"][:, :, BANK * (g - 1):BANK * g]).then_inc(sem(f"x{g}"), 16)
            for i in range(1, GADA // 2):
                for n in range(2):
                    sp.wait_ge(sem(f"ada_used{n}"), i)
                    sp.dma_start(adaw[:, n], d["ada"][2 * i + n]).then_inc(sem(f"ada{n}"), 16)

        @block.tensor
        def _(pe):
            pe.wait_ge(sem("consts"), 16)
            for g, (at, n, _) in enumerate(groups):
                pe.wait_ge(sem("squares"), g + 1)
                for k in range(KD):
                    mm = nc.tensor.matmul(ps[g][:, 0:n], t["c_ones"], tmp[:, k, at:at + n],
                                          start=(k == 0), stop=(k == KD - 1))
                mm.then_inc(sem("sumsq"), 1)
            pe.wait_ge(sem("silu_c"), 1)
            for i in range(GADA // 2):
                for s in range(2):
                    pe.wait_ge(sem(f"ada{s}"), 16 * (i + 1))
                    for m in range(NADA):
                        for k in range(KD):
                            mm = nc.tensor.matmul(modps[:, (2 * i + s) * NADA + m, :], adaw[:, s, m, k, :],
                                                  silu_c[:, k, :], start=(k == 0), stop=(k == KD - 1))
                    mm.then_inc(sem(f"ada_used{s}"), 1)

        @block.scalar
        def _(act):
            act.wait_ge(sem("vecs"), 16)
            nc.scalar.activation(silu_c, t["v_cc"].rearrange("p (k c) -> p k c", c=2),
                                 ACT.Silu).then_inc(sem("silu_c"), 1)
            for g, (at, n, _) in enumerate(groups):
                act.wait_ge(sem(f"x{g}"), 16)
                nc.scalar.activation(tmp[:, :, at:at + n], xin[:, :, at:at + n],
                                     ACT.Square).then_inc(sem("squares"), 1)
            act.wait_ge(sem("eps"), 2)
            for g, (at, n, _) in enumerate(groups):
                act.wait_ge(sem("sumsq"), g + 1)
                nc.scalar.activation(rstd[:, at:at + n], ps[g][:, 0:n], ACT.Sqrt, scale=1.0 / D,
                                     bias=t["c_eps"]).then_inc(sem("std"), 1)
            act.wait_ge(sem("gain"), 1)
            for g, (at, n, c) in enumerate(groups):
                act.wait_ge(sem("normed"), g + 1)
                for k in range(KD):
                    a = nc.scalar.activation(tmp[:, k, at:at + n], tmp[:, k, at:at + n], ACT.Identity,
                                             scale=gain[:, c, k:k + 1], bias=t["mod"][:, c, k:k + 1])
                a.then_inc(sem("full"), 1)
                act.wait_ge(sem("full"), g + 1)
                nc.scalar.activation(t["h_hi"][:, :, at:at + n], tmp[:, :, at:at + n],
                                     ACT.Copy).then_inc(sem("hi"), 1)

        @block.vector
        def _(dve):
            nc.vector.memset(t["c_eps"], RMS_EPS).then_inc(sem("eps"), 1)
            nc.vector.memset(t["c_gneps"], GN_EPS).then_inc(sem("eps"), 1)
            for g, (at, n, _) in enumerate(groups):
                dve.wait_ge(sem("std"), g + 1)
                nc.vector.reciprocal(rstd[:, at:at + n], rstd[:, at:at + n]).then_inc(sem("rstd"), 1)
                dve.wait_ge(sem("rstd"), g + 1)
                nc.vector.tensor_tensor(tmp[:, :, at:at + n], xin[:, :, at:at + n], bc(rstd[:, at:at + n], 1, KD),
                                        ALU.mult).then_inc(sem("normed"), 1)
            dve.wait_ge(sem("ada_used1"), GADA // 2)
            for c in range(2):
                nc.vector.tensor_tensor(t["mod"][:, c, 0:16], modps[:, :, c], t["v_ada_b"][:, 0:16],
                                        ALU.add).then_inc(sem("mod"), 1)
            dve.wait_ge(sem("mod"), 2)
            for c in range(2):
                g = nc.vector.scalar_tensor_tensor(out=gain[:, c], in0=t["mod"][:, c, 8:16], scalar=1.0,
                                                   in1=t["v_norm1_g"], op0=ALU.add, op1=ALU.mult)
            g.then_inc(sem("gain"), 1)
            for g, (at, n, _) in enumerate(groups):
                dve.wait_ge(sem("hi"), g + 1)
                nc.vector.tensor_tensor(t["h_lo"][:, :, at:at + n], tmp[:, :, at:at + n],
                                        t["h_hi"][:, :, at:at + n].bitcast(F32), ALU.subtract).then_inc(sem("lo"), 1)


def projections(nc, d, t):
    TILES, NADA = 3, 2
    G_X = [(CTX, BANK), (CTX + BANK, BANK)]
    G_ALL = [(0, CTX)] + G_X
    with ExitStack() as st:
        sem = Sems(nc, st, "b_")
        sb = lambda n, s, dt=F32: st.enter_context(nc.sbuf_tensor("b_" + n, s, dt))
        raw = sb("raw", [P, TILES, KD, P])
        w_hi = sb("w_hi", [P, TILES, KD, P], F32R)
        w_lo = sb("w_lo", [P, TILES, KD, P], F32R)
        adaw = sb("adaw", [P, NADA, KD, P])
        r = sb("r", [P, SEQ])
        k = sb("k", [P, TOK])
        v = sb("v", [P, TOK])
        kk = sb("kk", [P, TOK])
        sq = sb("sq", [P, TOK])
        rn = sq
        rkk = sb("rkk", [P, SEQ])
        gcc = kk[:, 0:SEQ]
        u = sq[:, 0:SEQ + 2]
        y = rkk
        zero = sb("zero", [P, PAIRS * C])
        ps = [st.enter_context(nc.psum_tensor(f"b_ps{n}", [P, BANK], F32)) for n in range(8)]
        full = [sem(f"psum_full{b}") for b in range(8)]
        free = [sem(f"psum_free{b}") for b in range(8)]
        gate = {n: sem("passed_" + n) for n in ("pe", "sp", "act", "dve", "pool")}
        h_hi, h_lo, mix = t["h_hi"], t["h_lo"], t["mix"]
        conv_w, k_k, r_k = t["v_conv_a_w"], t["v_k_k"], t["v_r_k"]
        block = st.enter_context(nc.Block())

        @block.sync
        def _(sp):
            def wait(s, value):
                hold(sp, gate["sp"], s, value)

            def load_weights(n):
                for tl in range(TILES):
                    wait(sem(f"lo{tl}"), n)
                sp.dma_start(raw[:], d["w1"][n]).then_inc(sem("raw"), 16)

            def load_ada(n):
                wait(sem("ada_used"), n)
                sp.dma_start(adaw[:], d["ada"][n + 8]).then_inc(sem("ada"), 16)

            def store_rkv(i):
                by_chunk = lambda buf, at, n: buf[:, at:at + n].rearrange("p (s c) -> p s c", c=C)
                to = lambda s0, s1, a: d["rkv"][s0:s1, :, a, i, :].rearrange("s p c -> p s c")
                w = nc.sync.snap(i + 1) if not isinstance(i, int) else i + 1
                for a, name, buf, ready in ((0, "r", r, 2), (1, "k", k, 3), (2, "v", v, 3), (3, "kk", kk, 1)):
                    wait(sem(name + "_ready"), w * ready)
                    if name == "r":
                        sp.dma_start(to(NCTX, STEPS, a), by_chunk(buf, 0, SEQ)).then_inc(sem("stored_r"), 16)
                    else:
                        sp.dma_start(to(0, STEPS, a), by_chunk(buf, 0, TOK)).then_inc(sem("stored_" + name), 16)
                        sp.dma_start(to(STEPS, SLOTS, a), by_chunk(buf, 0, CTX)).then_inc(sem("stored_" + name), 16)

            sp.dma_start(raw[:], d["w1"][0]).then_inc(sem("raw"), 16)
            sp.dma_start(adaw[:], d["ada"][8]).then_inc(sem("ada"), 16)
            sp.wait_ge(sem("zero"), 1)
            for s in list(range(NCTX)) + list(range(STEPS, SLOTS)):
                sp.dma_start(d["rkv"][s, :, 0], zero[:].rearrange("p (a c) -> p a c", a=PAIRS)).then_inc(sem("stored_0"), 16)
            with nc.sync.Fori(0, 4) as i:
                load_ada(nc.sync.snap(i * 2 + 1))
                load_weights(nc.sync.snap(i + 1))
                load_ada(nc.sync.snap(i * 2 + 2))
            with nc.sync.Fori(0, 3) as i:
                load_ada(nc.sync.snap(i * 2 + 9))
                load_weights(nc.sync.snap(i + 5))
                store_rkv(i)
                load_ada(nc.sync.snap(i * 2 + 10))
            load_ada(15)
            load_weights(8)
            store_rkv(3)
            sp.wait_ge(sem("stored_0"), 16 * 2 * NCTX)
            sp.wait_ge(sem("stored_r"), 16 * 4)
            for name in ("k", "v", "kk"):
                sp.wait_ge(sem("stored_" + name), 32 * 4)

        @block.tensor
        def _(pe):
            def wait(s, value):
                hold(pe, gate["pe"], s, value)

            def tile(n, tl, groups, uses):
                wait(sem(f"hi{tl}"), n + 1)
                wait(sem(f"lo{tl}"), n + 1)
                for (at, m), (b, read, value) in zip(groups, uses):
                    wait(read, value)
                    product(nc, ps[b][:, 0:m], w_hi[:, tl], w_lo[:, tl], h_hi, h_lo, KD,
                            slice(at, at + m)).then_inc(full[b], 1)

            def modulation(n):
                wait(sem("ada"), n * 16 + 16)
                wait(free[7], n)
                for m in range(NADA):
                    for q in range(KD):
                        mm = nc.tensor.matmul(ps[7][:, 2 * m:2 * m + 2], adaw[:, m, q, :], t["silu_c"][:, q, :],
                                              start=(q == 0), stop=(q == KD - 1))
                mm.then_inc(sem("ada_used"), 1)

            with nc.tensor.Fori(0, 4) as i:
                n = nc.tensor.snap(i + 0)
                tile(n, 0, G_X, [(b, free[b], n) for b in (0, 1)])
                modulation(nc.tensor.snap(i * 2))
                tile(n, 1, G_X, [(b, free[b], n) for b in (3, 4)])
                tile(n, 2, G_X, [(b, free[b], n) for b in (5, 6)])
                modulation(nc.tensor.snap(i * 2 + 1))
            for b in (0, 3, 4, 5, 6):
                pe.wait_ge(free[b], 4)
            r_read, k_read, v_read = sem("r_ready"), sem("k_ready"), sem("v_ready")
            with nc.tensor.Fori(0, 4) as i:
                n = nc.tensor.snap(i + 4)
                b1, i3, r0 = nc.tensor.snap(i * 5 + 4), nc.tensor.snap(i * 3), nc.tensor.snap(i * 2 + 1)
                tile(n, 0, G_X, [(0, v_read, i3), (1, free[1], b1)])
                modulation(nc.tensor.snap(i * 2 + 8))
                tile(n, 1, G_ALL, [(b, k_read, i3) for b in (2, 3, 4)])
                tile(n, 2, G_ALL, [(5, v_read, i3), (6, v_read, i3), (0, r_read, r0)])
                modulation(nc.tensor.snap(i * 2 + 9))
                wait(sem("sq"), i + 1)
                for g, (at, m) in enumerate(G_ALL):
                    wait(*((r_read, r0 + 1), (free[1], b1 + g))[g > 0])
                    nc.tensor.matmul(ps[1][:, 0:m], t["c_headones"], sq[:, at:at + m], start=True,
                                     stop=True).then_inc(full[1], 1)
                wait(sem("rkk"), i + 1)
                for g in range(2):
                    wait(free[1], b1 + (3 + g))
                    nc.tensor.matmul(ps[1][:], t["c_headones"], rkk[:, BANK * g:BANK * (g + 1)], start=True,
                                     stop=True).then_inc(full[1], 1)
            tile(8, 0, G_ALL, [(0, v_read, 12), (1, free[1], 24), (3, k_read, 12)])
            tile(8, 1, G_X, [(4, k_read, 12), (5, v_read, 12)])

        @block.scalar
        def _(act):
            def wait(s, value):
                hold(act, gate["act"], s, value)

            def hi(n, tl, bank, sums):
                if bank is not None:
                    wait(full[bank], sums)
                wait(sem("raw"), n * 16 + 16)
                nc.scalar.activation(w_hi[:, tl], raw[:, tl], ACT.Copy).then_inc(sem(f"hi{tl}"), 1)

            def read(out, b, m, sums):
                wait(full[b], sums)
                nc.scalar.activation(out, ps[b][:, 0:m], ACT.Copy).then_inc(free[b], 1)

            for tl in range(TILES):
                hi(0, tl, None, 0)
            with nc.scalar.Fori(0, 4) as i:
                n = nc.scalar.snap(i + 1)
                wait(free[3], i)
                wait(free[4], i)
                read(gcc[:, 0:BANK], 0, BANK, n)
                read(gcc[:, BANK:SEQ], 1, BANK, n)
                hi(n, 0, 1, n)
                hi(n, 1, 4, n)
                hi(n, 2, 6, n)
            with nc.scalar.Fori(0, 4) as i:
                n = nc.scalar.snap(i + 5)
                b0, b1 = nc.scalar.snap(i * 2 + 5), nc.scalar.snap(i * 6 + 5)
                wait(sem("stored_r"), i * 16)
                wait(sem("rkk"), i + 0)
                for g, b, w in ((0, 0, b0), (1, 1, b1)):
                    wait(full[b], w)
                    nc.scalar.activation(r[:, BANK * g:BANK * (g + 1)], ps[b][:], ACT.Copy).then_inc(sem("r_ready"), 1)
                hi(n, 0, None, 0)
                wait(sem("stored_k"), i * 32)
                for (at, m), b, w in zip(G_ALL, (2, 3, 4), (i + 1, n, n)):
                    wait(full[b], w)
                    nc.scalar.activation(k[:, at:at + m], ps[b][:, 0:m], ACT.Copy).then_inc(sem("k_ready"), 1)
                hi(n, 1, None, 0)
                wait(sem("stored_v"), i * 32)
                wait(free[1], nc.scalar.snap(i * 5 + 4))
                for (at, m), b, w in zip(G_ALL, (5, 6, 0), (n, n, b0 + 1)):
                    wait(full[b], w)
                    nc.scalar.activation(v[:, at:at + m], ps[b][:, 0:m], ACT.Copy).then_inc(sem("v_ready"), 1)
                hi(n, 2, None, 0)
                wait(free[1], nc.scalar.snap(i * 5 + 7))
                nc.scalar.activation(rn[:], rn[:], ACT.Sqrt).then_inc(sem("norm"), 1)
            for g, (b, sums, (at, m)) in enumerate(zip((0, 1, 3), (13, 29, 9), G_ALL)):
                act.wait_ge(full[b], sums)
                nc.scalar.activation(t["wa"][0:C, at:at + m], ps[b][0:C, 0:m], ACT.Tanh).then_inc(sem("wa"), 1)
                nc.scalar.activation(t["wa"][C:P, at:at + m], ps[b][C:P, 0:m], ACT.Copy).then_inc(sem("wa"), 1)
            act.wait_ge(sem("wa"), 2)
            nc.scalar.activation(t["wa"][:, TOK:TOK + CTX], t["wa"][:, 0:CTX], ACT.Copy).then_inc(sem("wa"), 1)
            for b, sums, at in ((4, 9, 0), (5, 9, BANK)):
                act.wait_ge(full[b], sums)
                nc.scalar.activation(t["sg"][:, at:at + BANK], ps[b][:], ACT.Sigmoid).then_inc(sem("sg"), 1)

        @block.gpsimd
        def _(pool):
            nc.gpsimd.memset(zero[:], 0.0).then_inc(sem("zero"), 1)

            def lo(n, tl):
                hold(pool, gate["pool"], sem(f"hi{tl}"), n + 1)
                nc.gpsimd.tensor_tensor(w_lo[:, tl], raw[:, tl], w_hi[:, tl].bitcast(F32),
                                        ALU.subtract).then_inc(sem(f"lo{tl}"), 1)

            for tl in range(TILES):
                lo(0, tl)
            with nc.gpsimd.Fori(0, 8) as i:
                n = nc.gpsimd.snap(i + 1)
                for tl in range(TILES):
                    lo(n, tl)

        @block.vector
        def _(dve):
            def wait(s, value):
                hold(dve, gate["dve"], s, value)

            def modulation(n):
                wait(sem("ada_used"), n + 1)
                at = nc.vector.snap(n * NADA + 16)
                nc.vector.tensor_tensor(t["mod"][:, 0, bass.ds(at, NADA)],
                                        ps[7][:, 0:2 * NADA].rearrange("p (n c) -> p n c", c=2)[:, :, 0],
                                        t["v_ada_b"][:, bass.ds(at, NADA)], ALU.add).then_inc(free[7], 1)

            nc.vector.memset(u, 0.0).then_inc(sem("u0"), 1)
            dve.wait_ge(sem("u0"), 1)
            with nc.vector.Fori(0, 4) as i:
                n = nc.vector.snap(i + 1)
                modulation(nc.vector.snap(i * 2))
                wait(sem("conv"), i * 3)
                for g, b in ((0, 3), (1, 4)):
                    wait(free[g], n)
                    wait(full[b], n)
                    nc.vector.tensor_tensor(u[:, 1 + BANK * g:1 + BANK * (g + 1)], ps[b][:],
                                            gcc[:, BANK * g:BANK * (g + 1)], ALU.mult).then_inc(free[b], 1)
                wait(free[3], n)
                wait(free[4], n)
                nc.vector.tensor_scalar(y[:], u[:, 0:SEQ], conv_w[:, bass.ds(i, 1)], None,
                                        ALU.mult).then_inc(sem("conv"), 1)
                for tap in (1, 2):
                    wait(sem("conv"), i * 3 + tap)
                    nc.vector.scalar_tensor_tensor(out=y[:], in0=u[:, tap:tap + SEQ],
                                                   scalar=conv_w[:, bass.ds(i + 4 * tap, 1)], in1=y[:],
                                                   op0=ALU.mult, op1=ALU.add).then_inc(sem("conv"), 1)
                wait(sem("conv"), i * 3 + 3)
                for g, b in ((0, 5), (1, 6)):
                    wait(full[b], n)
                    nc.vector.tensor_tensor(mix[:, bass.ds(i, 1), BANK * g:BANK * (g + 1)], ps[b][:].unsqueeze(1),
                                            y[:, BANK * g:BANK * (g + 1)].unsqueeze(1), ALU.mult).then_inc(free[b], 1)
                modulation(nc.vector.snap(i * 2 + 1))
            with nc.vector.Fori(0, 4) as i:
                n = nc.vector.snap(i + 1)
                b1 = nc.vector.snap(i * 6 + 4)
                modulation(nc.vector.snap(i * 2 + 8))
                wait(sem("k_ready"), n * 3)
                wait(sem("stored_kk"), i * 32)
                nc.vector.tensor_scalar(kk[:], k[:], k_k[:, bass.ds(i, 1)], None, ALU.mult).then_inc(sem("kk_raw"), 1)
                wait(sem("kk_raw"), n)
                nc.vector.tensor_tensor(sq[:], kk[:], kk[:], ALU.mult).then_inc(sem("sq"), 1)
                wait(sem("r_ready"), n * 2)
                nc.vector.scalar_tensor_tensor(out=rkk[:], in0=r[:], scalar=r_k[:, bass.ds(i, 1)], in1=k[:, CTX:TOK],
                                               op0=ALU.mult, op1=ALU.mult).then_inc(sem("rkk"), 1)
                modulation(nc.vector.snap(i * 2 + 9))
                wait(sem("r_ready"), n * 2)
                for g, (at, m) in enumerate(G_ALL):
                    wait(full[1], b1 + (2 + g))
                    nc.vector.tensor_scalar(rn[:, at:at + m], ps[1][:, 0:m], 1e-24, None, ALU.max).then_inc(free[1], 1)
                wait(sem("norm"), n)
                nc.vector.reciprocal(rn[:], rn[:]).then_inc(sem("rnorm"), 1)
                wait(sem("rnorm"), n)
                nc.vector.tensor_tensor(kk[:], kk[:], rn[:], ALU.mult).then_inc(sem("kk_ready"), 1)
                wait(sem("v_ready"), n * 3)
                for g in range(2):
                    wait(full[1], b1 + (5 + g))
                    nc.vector.tensor_tensor(mix[:, bass.ds(i + PAIRS, 1), BANK * g:BANK * (g + 1)], ps[1][:].unsqueeze(1),
                                            v[:, CTX + BANK * g:CTX + BANK * (g + 1)].unsqueeze(1),
                                            ALU.mult).then_inc(free[1], 1)
def scan(nc, d, t):
    EVENTS = {"lm": LEVELS, "p_y": LEVELS, "yl": LEVELS, "p_t": LEVELS - 1, "t": LEVELS, "p_u": LEVELS, "u": LEVELS + 1}
    DIRS = range(2)
    with ExitStack() as st:
        sem = Sems(nc, st, "c_")
        sb = lambda n, s, dt=F32: st.enter_context(nc.sbuf_tensor("c_" + n, s, dt))
        two = lambda n, s: [sb(f"{n}{x}", s) for x in DIRS]
        rk = two("rk", [P, 4, PAIRS, C])
        pre = two("pre", [P, 2, PAIRS, C])
        lw = two("lw", [P, PAIRS, C])
        cc = two("cc", [P, 2, PAIRS, C])
        pp = two("pp", [P, 2, PAIRS, C])
        pinv = two("pinv", [P, PAIRS, C])
        am1 = two("am1", [P, PAIRS, C])
        bb = two("bb", [P, PAIRS, C])
        kd = two("kd", [P, PAIRS, C])
        kr = two("kr", [P, PAIRS, 2, C])
        bet = two("bet", [P, PAIRS, C])
        khat = two("khat", [P, PAIRS, C])
        bnkt = two("bnkt", [P, 2, PAIRS, C])
        rd = two("rd", [P, 2, PAIRS, C])
        tm = two("tm", [P, 7, PAIRS, C])
        mm_ = two("mm", [P, PAIRS, 2, C])
        lm = two("lm", [P, LEVELS, PAIRS, C])
        tt = two("tt", [P, PAIRS, C])
        uu = two("uu", [P, PAIRS, C])
        yy = two("yy", [P, PAIRS, C])
        wu = two("wu", [P, PAIRS, 2, C])
        rp = two("rp", [P, 2, PAIRS, C])
        ss = two("ss", [P, PAIRS, C])
        yo = two("yo", [P, PAIRS, C])
        lora_w, lora_a = two("lora_w", [P, CH]), two("lora_a", [P, CH])
        bank = [[st.enter_context(nc.psum_tensor(f"c_ps{x}{n}", [P, BANK], F32)) for n in range(4)] for x in DIRS]
        gate = {n: sem("passed_" + n) for n in ("pe", "sp", "act", "dve", "pool")}
        S = lambda name, x: sem(f"{name}{x}")
        quad = lambda ap: ap.rearrange("p (q w c) -> p q w c", q=PAIRS, w=2)
        half = lambda ap: ap[:, 0:PAIRS * C].rearrange("p (q c) -> p q c", q=PAIRS)
        pack = lambda ap: ap.rearrange("p (w q c) -> p w q c", w=2, q=PAIRS)
        P_END = [C - 1, 0]
        block = st.enter_context(nc.Block())

        @block.sync
        def _(sp):
            def load(x, n, slot):
                sp.dma_start(rk[x][:], d["rkv"][slot]).then_inc(S("rk", x), 16)

            for x in DIRS:
                sp.dma_start(lora_w[x][0:C], d["w_up"][x]).then_inc(sem("lora"), 16)
                sp.dma_start(lora_a[x][C:P], d["a_up"][x]).then_inc(sem("lora"), 16)
                load(x, 0, (0, SLOTS - 1)[x])

            def store(x, i, slot):
                hold(sp, gate["sp"], S("yo", x), i + 1)
                sp.dma_start(d["ys"][x, slot], yo[x][:]).then_inc(S("stored", x), 16)

            with nc.sync.Fori(0, STEPS - 1) as i:
                for x in DIRS:
                    hold(sp, gate["sp"], S("p_tr2", x), nc.sync.snap(i + 1))
                    load(x, i + 1, nc.sync.snap((i + 1, SLOTS - 2 - i)[x]))
                for x in DIRS:
                    store(x, nc.sync.snap(i + 0), nc.sync.snap((i + 0, SLOTS - 1 - i)[x]))
            for x in DIRS:
                store(x, STEPS - 1, (STEPS - 1, SLOTS - STEPS)[x])
            for x in DIRS:
                sp.wait_ge(S("stored", x), 16 * STEPS)

        @block.tensor
        def _(pe):
            def heads(out, *pairs):
                for q in range(PAIRS):
                    for h in range(2):
                        rows = slice(HEAD * h, HEAD * h + HEAD)
                        for n, (left, right) in enumerate(pairs):
                            last = nc.tensor.matmul(out(rows, q), left(rows, q), right(rows, q), start=(n == 0),
                                                    stop=(n == len(pairs) - 1))
                return last

            at = lambda buf, *where: (lambda rows, q: buf[rows, q] if not where else buf[rows, where[0], q])
            sel = lambda buf, w: (lambda rows, q: buf[rows, q, w])
            wide = lambda ap: (lambda rows, q: ap[rows, 2 * C * q:2 * C * (q + 1)].rearrange("p (w c) -> p w c", w=2))
            thin = lambda ap: (lambda rows, q: ap[rows, C * q:C * (q + 1)])
            identc = lambda rows, q: t["c_identc"][rows, :]

            def wait(name, x, value):
                hold(pe, gate["pe"], S(name, x), value)

            def wait_level(name, x, i, lev):
                hold(pe, gate["pe"], S(name, x), i * EVENTS[name] + (lev + 1))

            def low_rank(x, v, col):
                for w, lora in enumerate((lora_w, lora_a)):
                    for q in range(PAIRS):
                        o = w * PAIRS + q
                        mm = nc.tensor.matmul(bank[x][1][:, C * o:C * (o + 1)], lora[x][:, P * q:P * (q + 1)],
                                              t["wa"][:, bass.ds(col, C)], start=True, stop=True)
                mm.then_inc(S("p_pre", x), 1)

            def step(i, v, last):
                for x in DIRS:
                    for name in ("kap", "rho", "bet"):
                        wait(name, x, v)
                    wait("yo", x, i)
                    heads(wide(bank[x][0]), (at(bet[x]), lambda rows, q: kr[x][rows, q])).then_inc(S("p_ll", x), 1)
                for x in DIRS:
                    wait("khat", x, v)
                    wait("wu", x, i)
                    heads(wide(bank[x][1]), (at(khat[x]), lambda rows, q: kr[x][rows, q])).then_inc(S("p_mm", x), 1)
                for x in DIRS:
                    wait("bn", x, v)
                    wait("rp", x, i)
                    b = pack(bank[x][2])
                    heads(at(b, 0), (at(bnkt[x], 0), identc))
                    heads(at(b, 1), (sel(kr[x], 0), identc)).then_inc(S("p_tr1", x), 1)
                for x in DIRS:
                    wait("kt", x, v)
                    wait("ss", x, v)
                    b = pack(bank[x][3])
                    heads(at(b, 0), (at(bnkt[x], 1), identc))
                    heads(at(b, 1), (at(rk[x], 2), identc)).then_inc(S("p_tr2", x), 1)
                for x in DIRS:
                    wait("ll", x, v)
                    heads(thin(bank[x][0]), (sel(kr[x], 0), at(bet[x]))).then_inc(S("p_l", x), 1)
                for x in DIRS:
                    wait("mm", x, v)
                    wait("tr2", x, v)
                    heads(thin(bank[x][1]), (sel(mm_[x], 0), at(tm[x], 6))).then_inc(S("p_mv", x), 1)
                for lev in range(LEVELS):
                    for x in DIRS:
                        wait_level("lm", x, i, lev)
                        if lev == 0:
                            wait("tr1", x, v)
                        else:
                            wait_level("yl", x, i, lev - 1)
                        wait_level("t", x, i, lev)
                        heads(thin(bank[x][2]), (at(lm[x], lev), at(tt[x]))).then_inc(S("p_y", x), 1)
                    if lev == 0 and not last:
                        for x in DIRS:
                            wait("mv", x, v)
                            low_rank(x, v, nc.tensor.snap(((i + 1) * C, (SLOTS - 2 - i) * C)[x]))
                    for x in DIRS:
                        wait_level("u", x, i, lev)
                        wait_level("yl", x, i, lev)
                        if lev < LEVELS - 1:
                            if lev == 0:
                                wait("tr2", x, v)
                            heads(thin(bank[x][3]), (at(uu[x]), at(yy[x]))).then_inc(S("p_t", x), 1)
                        heads(thin(bank[x][0]), (at(yy[x]), at(uu[x]))).then_inc(S("p_u", x), 1)
                for x in DIRS:
                    wait_level("u", x, i, LEVELS)
                    if last:
                        wait("mv", x, v)
                    else:
                        wait("pre", x, nc.tensor.snap(i + 2))
                    heads(wide(bank[x][1]), (at(uu[x]), lambda rows, q: tm[x][rows, 3:5, q])).then_inc(S("p_wu", x), 1)
                for x in DIRS:
                    wait("wu", x, v)
                    heads(wide(bank[x][2]), (sel(wu[x], 0), lambda rows, q: tm[x][rows, 1:3, q])).then_inc(S("p_rp", x), 1)
                for x in DIRS:
                    wait("rp", x, v)
                    heads(thin(bank[x][0]), (at(tm[x], 6), sel(mm_[x], 1)), (sel(wu[x], 1), at(tm[x], 1)),
                          (at(ss[x]), at(rp[x], 0))).then_inc(S("p_yo", x), 1)
                for x in DIRS:
                    heads(thin(bank[x][3]), (at(tm[x], 5), at(tm[x], 6)), (at(tm[x], 2), sel(wu[x], 1)),
                          (at(rp[x], 1), at(ss[x]))).then_inc(S("p_ss", x), 1)

            pe.wait_ge(sem("lora"), 64)
            pe.wait_ge(sem("lora0"), 4)
            for x in DIRS:
                low_rank(x, 0, (0, (SLOTS - 1) * C)[x])
                pe.wait_ge(S("pre", x), 1)
            with nc.tensor.Fori(0, STEPS - 1) as i:
                step(nc.tensor.snap(i + 0), nc.tensor.snap(i + 1), False)
            step(STEPS - 1, STEPS, True)

        @block.scalar
        def _(act):
            def wait(name, x, value):
                hold(act, gate["act"], S(name, x), value)

            def wait_level(name, x, i, lev):
                hold(act, gate["act"], S(name, x), i * EVENTS[name] + (lev + 1))

            def copy(x, name, out, src, after, v):
                wait(after, x, v)
                nc.scalar.activation(out, src, ACT.Copy).then_inc(S(name, x), 1)

            def sigmoids(x, v):
                wait("pre", x, v)
                nc.scalar.activation(pre[x][:], pre[x][:], ACT.Tanh, scale=0.5).then_inc(S("th", x), 1)

            def powers(x, v):
                wait("cex", x, v)
                nc.scalar.activation(pp[x][:], cc[x][:], ACT.Exp).then_inc(S("pp", x), 1)
                nc.scalar.activation(pinv[x][:], cc[x][:, 0], ACT.Exp, scale=-1.0).then_inc(S("pinv", x), 1)

            def step(i, v, last):
                nxt = None if last else nc.scalar.snap(i + 2)
                for x in DIRS:
                    copy(x, "tr1", tm[x][:, 2:4], pack(bank[x][2]), "p_tr1", v)
                for x in DIRS:
                    copy(x, "tr2", tm[x][:, 5:7], pack(bank[x][3]), "p_tr2", v)
                for x in DIRS:
                    copy(x, "mv", tm[x][:, 4], half(bank[x][1]), "p_mv", v)
                for lev in range(LEVELS):
                    for x in DIRS:
                        wait_level("p_y", x, i, lev)
                        nc.scalar.activation(yy[x][:], half(bank[x][2]), ACT.Copy).then_inc(S("yl", x), 1)
                    for x in DIRS:
                        if lev == 1 and not last:
                            sigmoids(x, nxt)
                        if lev == 2 and not last:
                            wait("rd", x, v)
                            powers(x, nxt)
                for x in DIRS:
                    copy(x, "wu", wu[x][:], quad(bank[x][1]), "p_wu", v)
                for x in DIRS:
                    hold(act, gate["act"], S("stored", x), i * 16)
                    copy(x, "yo", yo[x][:], half(bank[x][0]), "p_yo", v)
                for x in DIRS:
                    copy(x, "ss", ss[x][:], half(bank[x][3]), "p_ss", v)

            for x in DIRS:
                sigmoids(x, 1)
            for x in DIRS:
                powers(x, 1)
            with nc.scalar.Fori(0, STEPS - 1) as i:
                step(nc.scalar.snap(i + 0), nc.scalar.snap(i + 1), False)
            step(STEPS - 1, STEPS, True)

        @block.vector
        def _(dve):
            TT, TS, STT = nc.vector.tensor_tensor, nc.vector.tensor_scalar, nc.vector.scalar_tensor_tensor

            def wait(name, x, value):
                hold(dve, gate["dve"], S(name, x), value)

            def wait_level(name, x, i, lev):
                hold(dve, gate["dve"], S(name, x), i * EVENTS[name] + (lev + 1))

            def prep_pre(x, v):
                wait("p_pre", x, v)
                TT(pre[x][:], pack(bank[x][1]), bc(t["v_w0a0"].rearrange("p (x w q) -> p x w q", x=2, w=2)[:, x], 3, C),
                   ALU.add).then_inc(S("pre", x), 1)

            def prep_decay(x, v):
                wait("th", x, v)
                TS(lw[x][:], pre[x][:, 0], -0.5 * DECAY_SCALE, -0.5 * DECAY_SCALE, ALU.mult, ALU.add).then_inc(S("lw", x), 1)
                wait("lw", x, v)
                out, data = (a.rearrange("p q c -> p (q c)") for a in (cc[x][:, 0], lw[x][:]))
                flat = [out, t["c_reset"][:, x], data]
                out, reset, data = flat if x == 0 else [a[:, ::-1] for a in flat]
                nc.vector.tensor_tensor_scan(out, reset, data, 0.0, ALU.mult, ALU.add).then_inc(S("c", x), 1)

            def prep_kd(x, v):
                wait("am1", x, v)
                TT(kd[x][:], am1[x][:], bc(t["v_k_a"], 2, C), ALU.mult).then_inc(S("amk", x), 1)
                wait("amk", x, v)
                STT(out=kd[x][:], in0=kd[x][:], scalar=1.0, in1=rk[x][:, 1], op0=ALU.add,
                    op1=ALU.mult).then_inc(S("kd", x), 1)

            def prep_products(x, v):
                wait("pp", x, v)
                TT(kr[x][:, :, 0], rk[x][:, 3], pp[x][:, 1], ALU.mult).then_inc(S("kap", x), 1)
                TT(kr[x][:, :, 1], rk[x][:, 0], pp[x][:, 0], ALU.mult).then_inc(S("rho", x), 1)
                wait("pinv", x, v)
                wait("b", x, v)
                TT(bet[x][:], bb[x][:], pinv[x][:], ALU.mult).then_inc(S("bet", x), 1)
                wait("kd", x, v)
                TT(khat[x][:], kd[x][:], pinv[x][:], ALU.mult).then_inc(S("khat", x), 1)
                end = pp[x][:, 0, :, P_END[x]:P_END[x] + 1].broadcast_to([P, PAIRS, C])
                wait("bet", x, v)
                STT(out=bnkt[x][:, 0], in0=bet[x][:], scalar=-1.0, in1=end, op0=ALU.mult,
                    op1=ALU.mult).then_inc(S("bn", x), 1)
                wait("khat", x, v)
                TT(bnkt[x][:, 1], khat[x][:], end, ALU.mult).then_inc(S("kt", x), 1)

            def step(i, v, last):
                nxt = None if last else nc.vector.snap(i + 2)
                for x in DIRS:
                    wait("p_ll", x, v)
                    TT(tm[x][:, 0:2].rearrange("p w q c -> p q w c"), quad(bank[x][0]),
                       bc(t["c_mask_ll"][:, x], 1, PAIRS), ALU.mult).then_inc(S("ll", x), 1)
                for x in DIRS:
                    wait("p_mm", x, v)
                    TT(mm_[x][:], quad(bank[x][1]), bc(t["c_mask_mm"][:, x], 1, PAIRS), ALU.mult).then_inc(S("mm", x), 1)
                for x in DIRS:
                    wait("p_l", x, v)
                    TT(tt[x][:], half(bank[x][0]), bc(t["c_mask_l1"][:, x], 1, PAIRS), ALU.mult).then_inc(S("t_raw", x), 1)
                for x in DIRS:
                    wait("t_raw", x, v)
                    TT(tt[x][:], tt[x][:], bc(t["c_identc"], 1, PAIRS), ALU.add).then_inc(S("t", x), 1)
                for lev in range(LEVELS):
                    if lev == 1 and not last:
                        for x in DIRS:
                            prep_pre(x, nxt)
                    if lev == 2 and not last:
                        for x in DIRS:
                            prep_decay(x, nxt)
                    if lev == 3 and not last:
                        for x in DIRS:
                            prep_kd(x, nxt)
                    if lev == 4 and not last:
                        for x in DIRS:
                            wait("rd", x, v)
                            prep_products(x, nxt)
                    for x in DIRS:
                        if lev < LEVELS - 1:
                            wait_level("p_t", x, i, lev)
                            TT(tt[x][:], tt[x][:], half(bank[x][3]), ALU.subtract).then_inc(S("t", x), 1)
                        wait_level("p_u", x, i, lev)
                        TT(uu[x][:], uu[x][:], half(bank[x][0]), ALU.subtract).then_inc(S("u", x), 1)
                for x in DIRS:
                    wait("p_rp", x, v)
                    wait("rd", x, v)
                    TT(rp[x][:].rearrange("p w q c -> p q w c"), quad(bank[x][2]),
                       rd[x][:].rearrange("p w q c -> p q w c"), ALU.add).then_inc(S("rp", x), 1)

            for x in DIRS:
                nc.vector.memset(lora_w[x][C:P], 0.0).then_inc(sem("lora0"), 1)
                nc.vector.memset(lora_a[x][0:C], 0.0).then_inc(sem("lora0"), 1)
                nc.vector.memset(ss[x][:], 0.0).then_inc(S("ss", x), 1)
            for x in DIRS:
                prep_pre(x, 1)
            for x in DIRS:
                prep_decay(x, 1)
            for x in DIRS:
                prep_kd(x, 1)
            for x in DIRS:
                prep_products(x, 1)
            with nc.vector.Fori(0, STEPS - 1) as i:
                step(nc.vector.snap(i + 0), nc.vector.snap(i + 1), False)
            step(STEPS - 1, STEPS, True)

        @block.gpsimd
        def _(pool):
            TT, TS = nc.gpsimd.tensor_tensor, nc.gpsimd.tensor_scalar

            def wait(name, x, value):
                hold(pool, gate["pool"], S(name, x), value)

            def prep_a(x, v, v16):
                hold(pool, gate["pool"], S("rk", x), v16)
                wait("th", x, v)
                TS(am1[x][:], pre[x][:, 1], 0.5, -0.5, ALU.mult, ALU.add).then_inc(S("am1", x), 1)
                TS(bb[x][:], pre[x][:, 1], 0.5, 0.5, ALU.mult, ALU.add).then_inc(S("a", x), 1)
                wait("a", x, v)
                TT(bb[x][:], bb[x][:], rk[x][:, 3], ALU.mult).then_inc(S("b", x), 1)

            def prep_cex(x, v):
                wait("c", x, v)
                TT(cc[x][:, 1], cc[x][:, 0], lw[x][:], ALU.subtract).then_inc(S("cex", x), 1)

            def step(i, v, last):
                nxt = None if last else nc.gpsimd.snap(i + 2)
                for x in DIRS:
                    wait("ll", x, v)
                    TT(uu[x][:], tm[x][:, 0], bc(t["c_mask_u1"][:, x], 1, PAIRS), ALU.mult).then_inc(S("u_raw", x), 1)
                    TT(lm[x][:, 0], tm[x][:, 0], bc(t["c_mask_lev"][:, x, 0], 1, PAIRS), ALU.mult).then_inc(S("lm", x), 1)
                    wait("u_raw", x, v)
                    TT(uu[x][:], uu[x][:], bc(t["c_identc"], 1, PAIRS), ALU.add).then_inc(S("u", x), 1)
                for lev in range(1, LEVELS):
                    for x in DIRS:
                        TT(lm[x][:, lev], tm[x][:, 0], bc(t["c_mask_lev"][:, x, lev], 1, PAIRS),
                           ALU.mult).then_inc(S("lm", x), 1)
                    if lev == 1:
                        for x in DIRS:
                            wait("rho", x, v)
                            wait("rp", x, i)
                            nc.gpsimd.tensor_copy(rd[x][:, 0], kr[x][:, :, 1]).then_inc(S("rd_rho", x), 1)
                            TT(rd[x][:, 1], bc(t["c_identc"], 1, PAIRS),
                               pp[x][:, 0, :, P_END[x]:P_END[x] + 1].broadcast_to([P, PAIRS, C]),
                               ALU.mult).then_inc(S("rd_diag", x), 1)
                            wait("rd_rho", x, v)
                            wait("rd_diag", x, v)
                            pool.sem_inc(S("rd", x), 1)
                if not last:
                    for x in DIRS:
                        prep_a(x, nxt, nc.gpsimd.snap((i + 2) * 16))
                    for x in DIRS:
                        prep_cex(x, nxt)

            for x in DIRS:
                prep_a(x, 1, 16)
            for x in DIRS:
                prep_cex(x, 1)
            with nc.gpsimd.Fori(0, STEPS - 1) as i:
                step(nc.gpsimd.snap(i + 0), nc.gpsimd.snap(i + 1), False)
            step(STEPS - 1, STEPS, True)
def mixer_out(nc, d, t):
    G = range(2)
    cols = lambda g: slice(BANK * g, BANK * (g + 1))
    with ExitStack() as st:
        sem = Sems(nc, st, "d_")
        sb = lambda n, s, dt=F32: st.enter_context(nc.sbuf_tensor("d_" + n, s, dt))
        yf, yr = sb("yf", [P, 2, SEQ]), sb("yr", [P, 2, SEQ])
        yc, sq, rstd = sb("yc", [P, SEQ]), sb("sq", [P, SEQ]), sb("rstd", [P, SEQ])
        g_up = sb("g_up", [P, CH])
        raw = sb("raw", [P, 2, KD, P])
        w_hi, w_lo = sb("w_hi", [P, 2, KD, P], F32R), sb("w_lo", [P, 2, KD, P], F32R)
        ps = [st.enter_context(nc.psum_tensor(f"d_ps{n}", [P, BANK], F32)) for n in range(8)]
        mix, x1, hi, lo = t["mix"], t["x1"], t["h2_hi"], t["h2_lo"]
        full = [sem(f"psum_full{b}") for b in range(4)]
        free = [sem(f"psum_free{b}") for b in range(4)]
        gate = {n: sem("passed_" + n) for n in ("pe", "sp", "act", "dve", "pool")}
        block = st.enter_context(nc.Block())

        @block.sync
        def _(sp):
            for j in range(PAIRS):
                if j >= 2:
                    sp.wait_ge(sem("centred"), j - 1)
                for x, buf in ((0, yf), (1, yr)):
                    sp.dma_start(buf[:, j % 2].rearrange("p (s c) -> p s c", c=C),
                                 d["ys"][x, NCTX:STEPS, :, j].rearrange("s p c -> p s c")).then_inc(sem(f"y{j % 2}"), 16)
                if j == 0:
                    sp.dma_start(g_up[:], d["g_up"]).then_inc(sem("g_up"), 16)
                    sp.dma_start(raw[:], d["w_out"][0]).then_inc(sem("raw"), 16)
            sp.dma_start(x1[:], d["xT"]).then_inc(sem("x"), 16)
            with nc.sync.Fori(0, 3) as i:
                for s in range(2):
                    hold(sp, gate["sp"], sem(f"lo{s}"), nc.sync.snap(i + 1))
                sp.dma_start(raw[:], d["w_out"][i + 1]).then_inc(sem("raw"), 16)

        @block.tensor
        def _(pe):
            pe.wait_ge(sem("g_up"), 16)
            for j in range(PAIRS):
                pe.wait_ge(sem("summed"), j + 1)
                pe.wait_ge(sem("centred"), j)
                for g in G:
                    mm = nc.tensor.matmul(ps[g][:], t["c_headones"], yf[:, j % 2, cols(g)], start=True, stop=True)
                mm.then_inc(sem("p_mean"), 1)
                pe.wait_ge(sem("gated"), j)
                for g in G:
                    mm = nc.tensor.matmul(ps[4 + g][:], g_up[:, P * j:P * (j + 1)], t["sg"][:, cols(g)], start=True, stop=True)
                mm.then_inc(sem("p_gate"), 1)
                pe.wait_ge(sem("sq"), j + 1)
                pe.wait_ge(sem("std"), j)
                for g in G:
                    mm = nc.tensor.matmul(ps[2 + g][:], t["c_headones"], sq[:, cols(g)], start=True, stop=True)
                mm.then_inc(sem("p_var"), 1)
            pe.wait_ge(sem("mix_lo"), 2)
            pe.wait_ge(sem("centred"), PAIRS)
            pe.wait_ge(sem("std"), PAIRS)
            with nc.tensor.Fori(0, 4) as i:
                n = nc.tensor.snap(i + 1)
                for s in range(2):
                    hold(pe, gate["pe"], sem(f"hi{s}"), n)
                    hold(pe, gate["pe"], sem(f"lo{s}"), n)
                    for g in G:
                        b = 2 * s + g
                        hold(pe, gate["pe"], free[b], i)
                        product(nc, ps[b][:], w_hi[:, s], w_lo[:, s], hi, lo, KD, cols(g)).then_inc(full[b], 1)

        @block.scalar
        def _(act):
            nc.scalar.activation(hi[:, 0:PAIRS], mix[:, 0:PAIRS], ACT.Copy).then_inc(sem("mix_hi"), 1)
            for j in range(PAIRS):
                act.wait_ge(sem("centred"), j + 1)
                nc.scalar.activation(sq[:], yc[:], ACT.Square).then_inc(sem("sq"), 1)
                act.wait_ge(sem("p_var"), j + 1)
                act.wait_ge(sem("yn"), j)
                for g in G:
                    a = nc.scalar.activation(rstd[:, cols(g)], ps[2 + g][:], ACT.Sqrt, scale=1.0 / HEAD, bias=t["c_gneps"])
                a.then_inc(sem("std"), 1)
            act.wait_ge(sem("gated"), PAIRS)
            nc.scalar.activation(hi[:, PAIRS:KD], mix[:, PAIRS:KD], ACT.Copy).then_inc(sem("mix_hi"), 1)

            def split_hi(n, first):
                hold(act, gate["act"], sem("raw"), n * 16 + 16)
                for s in range(2):
                    if not first:
                        hold(act, gate["act"], full[2 * s + 1], n)
                    nc.scalar.activation(w_hi[:, s], raw[:, s], ACT.Copy).then_inc(sem(f"hi{s}"), 1)

            split_hi(0, True)
            with nc.scalar.Fori(0, 3) as i:
                split_hi(nc.scalar.snap(i + 1), False)

        @block.gpsimd
        def _(pool):
            def split_lo(n):
                for s in range(2):
                    hold(pool, gate["pool"], sem(f"hi{s}"), n + 1)
                    nc.gpsimd.tensor_tensor(w_lo[:, s], raw[:, s], w_hi[:, s].bitcast(F32),
                                            ALU.subtract).then_inc(sem(f"lo{s}"), 1)

            with nc.gpsimd.Fori(0, 4) as i:
                split_lo(i)

        @block.vector
        def _(dve):
            TT, TS, STT = nc.vector.tensor_tensor, nc.vector.tensor_scalar, nc.vector.scalar_tensor_tensor
            dve.wait_ge(sem("mix_hi"), 1)
            TT(lo[:, 0:PAIRS], mix[:, 0:PAIRS], hi[:, 0:PAIRS].bitcast(F32), ALU.subtract).then_inc(sem("mix_lo"), 1)
            for j in range(PAIRS):
                y = yf[:, j % 2]
                dve.wait_ge(sem(f"y{j % 2}"), 32 * (j // 2 + 1))
                TT(y, y, yr[:, j % 2], ALU.add).then_inc(sem("summed"), 1)
                dve.wait_ge(sem("p_mean"), j + 1)
                for g in G:
                    a = STT(out=yc[:, cols(g)], in0=ps[g][:], scalar=-1.0 / HEAD, in1=y[:, cols(g)], op0=ALU.mult, op1=ALU.add)
                a.then_inc(sem("centred"), 1)
                dve.wait_ge(sem("std"), j + 1)
                nc.vector.reciprocal(rstd[:], rstd[:]).then_inc(sem("rstd"), 1)
                dve.wait_ge(sem("rstd"), j + 1)
                TT(yc[:], yc[:], rstd[:], ALU.mult).then_inc(sem("yn"), 1)
                dve.wait_ge(sem("yn"), j + 1)
                TS(yc[:], yc[:], t["v_ln_g"][:, j:j + 1], t["v_ln_b"][:, j:j + 1], ALU.mult, ALU.add).then_inc(sem("scaled"), 1)
                dve.wait_ge(sem("scaled"), j + 1)
                TT(yc[:], yc[:], mix[:, PAIRS + j], ALU.add).then_inc(sem("bonus"), 1)
                dve.wait_ge(sem("bonus"), j + 1)
                dve.wait_ge(sem("p_gate"), j + 1)
                for g in G:
                    a = TT(mix[:, PAIRS + j, cols(g)], yc[:, cols(g)], ps[4 + g][:], ALU.mult)
                a.then_inc(sem("gated"), 1)
            dve.wait_ge(sem("mix_hi"), 2)
            TT(lo[:, PAIRS:KD], mix[:, PAIRS:KD], hi[:, PAIRS:KD].bitcast(F32), ALU.subtract).then_inc(sem("mix_lo"), 1)
            dve.wait_ge(sem("x"), 16)
            with nc.vector.Fori(0, 4) as i:
                n = nc.vector.snap(i + 1)
                for s in range(2):
                    tile = nc.vector.snap(i * 2 + s)
                    for g in G:
                        b = 2 * s + g
                        hold(dve, gate["dve"], full[b], n)
                        xs = x1[:, bass.ds(tile, 1), cols(g)]
                        STT(out=xs, in0=ps[b][:].unsqueeze(1), scalar=t["mod"][:, 0, bass.ds(tile + 16, 1)], in1=xs,
                            op0=ALU.mult, op1=ALU.add).then_inc(free[b], 1)


def rms(nc, t, name, x, out, parts, gain, shift, store=None):
    N = 256
    groups = [slice(N * g, N * (g + 1)) for g in range(SEQ // N)]
    with ExitStack() as st:
        sem = Sems(nc, st, name + "_")
        sq = st.enter_context(nc.sbuf_tensor(name + "_sq", [P, 2, KD, N], F32))
        rstd = st.enter_context(nc.sbuf_tensor(name + "_rstd", [P, 2, N], F32))
        g1 = st.enter_context(nc.sbuf_tensor(name + "_gain", [P, KD], F32))
        ps = [st.enter_context(nc.psum_tensor(f"{name}_ps{n}", [P, BANK], F32)) for n in range(2)]
        block = st.enter_context(nc.Block())

        @block.scalar
        def _(act):
            def squares(g):
                if g >= 2:
                    act.wait_ge(sem("sums"), g - 1)
                nc.scalar.activation(sq[:, g % 2], x[:, :, groups[g]], ACT.Square).then_inc(sem("squares"), 1)

            squares(0)
            for g, cols in enumerate(groups):
                if g + 1 < len(groups):
                    squares(g + 1)
                act.wait_ge(sem("sums"), g + 1)
                if g >= 2:
                    act.wait_ge(sem("normed"), g - 1)
                nc.scalar.activation(rstd[:, g % 2], ps[g % 2][:, 0:N], ACT.Sqrt, scale=1.0 / D,
                                     bias=t["c_eps"]).then_inc(sem("std"), 1)
                if parts:
                    act.wait_ge(sem("full"), KD * (g + 1))
                    nc.scalar.activation(parts[0][:, :, cols], out[:, :, cols], ACT.Copy).then_inc(sem("hi"), 1)

        @block.tensor
        def _(pe):
            for g in range(len(groups)):
                pe.wait_ge(sem("squares"), g + 1)
                if g >= 2:
                    pe.wait_ge(sem("std"), g - 1)
                for k in range(KD):
                    mm = nc.tensor.matmul(ps[g % 2][:, 0:N], t["c_ones"], sq[:, g % 2, k], start=(k == 0), stop=(k == KD - 1))
                mm.then_inc(sem("sums"), 1)

        @block.vector
        def _(dve):
            gain(g1[:]).then_inc(sem("gain"), 1)
            dve.wait_ge(sem("gain"), 1)
            for g, cols in enumerate(groups):
                dve.wait_ge(sem("std"), g + 1)
                nc.vector.reciprocal(rstd[:, g % 2], rstd[:, g % 2]).then_inc(sem("rstd"), 1)
                dve.wait_ge(sem("rstd"), g + 1)
                nc.vector.tensor_tensor(out[:, :, cols], x[:, :, cols], bc(rstd[:, g % 2], 1, KD), ALU.mult).then_inc(sem("normed"), 1)
                dve.wait_ge(sem("normed"), g + 1)
                for k in range(KD):
                    if shift is None:
                        a = nc.vector.tensor_scalar(out[:, k, cols], out[:, k, cols], g1[:, k:k + 1], None, ALU.mult)
                    else:
                        a = nc.vector.tensor_scalar(out[:, k, cols], out[:, k, cols], g1[:, k:k + 1], shift[:, k:k + 1], ALU.mult, ALU.add)
                    a.then_inc(sem("full"), 1)

        if parts:
            @block.gpsimd
            def _(pool):
                for g, cols in enumerate(groups):
                    pool.wait_ge(sem("hi"), g + 1)
                    nc.gpsimd.tensor_tensor(parts[1][:, :, cols], out[:, :, cols], parts[0][:, :, cols].bitcast(F32),
                                            ALU.subtract).then_inc(sem("lo"), 1)

        if store is not None:
            @block.sync
            def _(sp):
                for g, cols in enumerate(groups):
                    sp.wait_ge(sem("full"), KD * (g + 1))
                    sp.dma_start(store[:, :, cols], out[:, :, cols]).then_inc(sem("stored"), 16)
                sp.wait_ge(sem("stored"), 16 * len(groups))


def ffn_up(nc, d, t):
    with ExitStack() as st:
        sem = Sems(nc, st, "e_")
        sb = lambda n, s, dt=F32: st.enter_context(nc.sbuf_tensor("e_" + n, s, dt))
        raw = sb("raw", [P, 2, KD, P])
        w_hi, w_lo = sb("w_hi", [P, 2, KD, P], F32R), sb("w_lo", [P, 2, KD, P], F32R)
        grid = sb("grid", [P, GRID_H + 2, GRID_W + 2])
        acc = sb("acc", [P, GRID_H, GRID_W])
        act_g = sb("act_g", [P, SEQ])
        z = sb("z", [P, SEQ])
        ps = [st.enter_context(nc.psum_tensor(f"e_ps{n}", [P, BANK], F32)) for n in range(4)]
        full = [sem(f"psum_full{b}") for b in range(4)]
        free = [sem(f"psum_free{b}") for b in range(4)]
        gate = {n: sem("passed_" + n) for n in ("pe", "sp", "act", "dve", "pool")}
        hi, lo = t["h2_hi"], t["h2_lo"]
        ROWS = GRID_H // 2
        cols = lambda g: slice(BANK * g, BANK * (g + 1))
        block = st.enter_context(nc.Block())

        @block.sync
        def _(sp):
            sp.dma_start(raw[:], d["w_ffn"][0]).then_inc(sem("raw"), 16)

            def store(i):
                hold(sp, gate["sp"], sem("z"), i * 2 + 2)
                sp.dma_start(d["zs"][i], z[:]).then_inc(sem("stored"), 16)

            with nc.sync.Fori(0, NFF - 1) as i:
                n = nc.sync.snap(i + 1)
                for s in range(2):
                    hold(sp, gate["sp"], sem(f"lo{s}"), n)
                sp.dma_start(raw[:], d["w_ffn"][n]).then_inc(sem("raw"), 16)
                store(nc.sync.snap(i + 0))
            store(NFF - 1)
            sp.wait_ge(sem("stored"), 16 * NFF)

        @block.tensor
        def _(pe):
            with nc.tensor.Fori(0, NFF) as i:
                n = nc.tensor.snap(i + 1)
                for s in range(2):
                    hold(pe, gate["pe"], sem(f"hi{s}"), n)
                    hold(pe, gate["pe"], sem(f"lo{s}"), n)
                    for g in range(2):
                        b = 2 * s + g
                        hold(pe, gate["pe"], free[b], i)
                        product(nc, ps[b][:], w_hi[:, s], w_lo[:, s], hi, lo, KD, cols(g)).then_inc(full[b], 1)

        @block.scalar
        def _(act):
            def split_hi(n, s):
                hold(act, gate["act"], sem("raw"), n * 16 + 16)
                if not isinstance(n, int):
                    hold(act, gate["act"], full[2 * s + 1], n)
                nc.scalar.activation(w_hi[:, s], raw[:, s], ACT.Copy).then_inc(sem(f"hi{s}"), 1)

            def step(i, n, last):
                hold(act, gate["act"], sem("conv"), i * 9)
                for g in range(2):
                    hold(act, gate["act"], full[g], n)
                    nc.scalar.activation(grid[:, 1 + ROWS * g:1 + ROWS * (g + 1), 1:1 + GRID_W],
                                         ps[g][:].rearrange("p (h w) -> p h w", w=GRID_W), ACT.Copy).then_inc(free[g], 1)
                if not last:
                    split_hi(n, 0)
                hold(act, gate["act"], sem("conv"), i * 9 + 9)
                hold(act, gate["act"], sem("z"), i * 2)
                nc.scalar.activation(act_g[:], acc[:].rearrange("p h w -> p (h w)"), ACT.Silu).then_inc(sem("silu"), 1)
                if not last:
                    split_hi(n, 1)

            act.wait_ge(sem("rim"), 1)
            for s in range(2):
                split_hi(0, s)
            with nc.scalar.Fori(0, NFF - 1) as i:
                step(nc.scalar.snap(i + 0), nc.scalar.snap(i + 1), False)
            step(NFF - 1, NFF, True)

        @block.gpsimd
        def _(pool):
            with nc.gpsimd.Fori(0, NFF) as i:
                n = nc.gpsimd.snap(i + 1)
                for s in range(2):
                    hold(pool, gate["pool"], sem(f"hi{s}"), n)
                    nc.gpsimd.tensor_tensor(w_lo[:, s], raw[:, s], w_hi[:, s].bitcast(F32), ALU.subtract).then_inc(sem(f"lo{s}"), 1)

        @block.vector
        def _(dve):
            nc.vector.memset(grid[:], 0.0).then_inc(sem("rim"), 1)
            w = t["v_ffn_conv_w"]
            with nc.vector.Fori(0, NFF) as i:
                n = nc.vector.snap(i + 1)
                for g in range(2):
                    hold(dve, gate["dve"], free[g], n)
                hold(dve, gate["dve"], sem("silu"), i)
                for tap in range(9):
                    dy, dx = tap // 3, tap % 3
                    view = grid[:, dy:dy + GRID_H, dx:dx + GRID_W]
                    wt = w[:, bass.ds(i + tap * NFF, 1)]
                    if tap:
                        hold(dve, gate["dve"], sem("conv"), nc.vector.snap(i * 9 + tap))
                        a = nc.vector.scalar_tensor_tensor(out=acc[:], in0=view, scalar=wt, in1=acc[:], op0=ALU.mult, op1=ALU.add)
                    else:
                        a = nc.vector.tensor_scalar(acc[:], view, wt, t["v_ffn_conv_b"][:, bass.ds(i, 1)], ALU.mult, ALU.add)
                    a.then_inc(sem("conv"), 1)
                hold(dve, gate["dve"], sem("silu"), n)
                hold(dve, gate["dve"], sem("stored"), i * 16)
                for g in range(2):
                    hold(dve, gate["dve"], full[2 + g], n)
                    hold(dve, gate["dve"], free[2 + g], i)
                    nc.vector.tensor_tensor(z[:, cols(g)], act_g[:, cols(g)], ps[2 + g][:], ALU.mult).then_inc(free[2 + g], 1)
                for g in range(2):
                    hold(dve, gate["dve"], free[2 + g], n)
                dve.sem_inc(sem("z"), 2)


def ffn_down(nc, d, t):
    with ExitStack() as st:
        sem = Sems(nc, st, "f_")
        sb = lambda n, s, dt=F32: st.enter_context(nc.sbuf_tensor("f_" + n, s, dt))
        z_hi, z_lo = sb("z_hi", [P, NFF, BANK], F32R), sb("z_lo", [P, NFF, BANK], F32R)
        z_raw = sb("z_raw", [P, 2, BANK])
        raw = sb("raw", [P, 2, NFF, P])
        w_hi, w_lo = sb("w_hi", [P, 2, NFF, P], F32R), sb("w_lo", [P, 2, NFF, P], F32R)
        x1, x2 = sb("x1", [P, 2, BANK]), sb("x2", [P, 2, BANK])
        ps = [st.enter_context(nc.psum_tensor(f"f_ps{n}", [P, BANK], F32)) for n in range(2)]
        gate = {n: sem("passed_" + n) for n in ("pe", "sp", "act", "dve", "pool")}
        HALVES, TURNS = 2, KD // 2
        ZT = NFF // 2
        cols = lambda g: slice(BANK * g, BANK * (g + 1))
        ended = lambda turn, s: turn * (2 * NFF) + (s + 1) * NFF
        block = st.enter_context(nc.Block())

        @block.sync
        def _(sp):
            def wait(s, value):
                hold(sp, gate["sp"], s, value)

            def load_z(g):
                with nc.sync.Fori(0, ZT) as j:
                    for s in range(2):
                        wait(sem(f"z_lo{s}"), nc.sync.snap(j + g * ZT))
                        sp.dma_start(z_raw[:, s], d["zs"][2 * j + s, :, cols(g)]).then_inc(sem(f"z_raw{s}"), 16)

            def load_w(g, i, s):
                turn = held(nc.sync, i + g * TURNS)
                wait(sem(f"lo{s}"), turn)
                sp.dma_start(raw[:, s], d["w_down"][2 * i + s]).then_inc(sem(f"raw{s}"), 16)
                wait(sem(f"x2_{s}"), turn)
                sp.dma_start(x1[:, s], d["x1s"][:, 2 * i + s, cols(g)]).then_inc(sem(f"x1_{s}"), 16)

            def store(g, i, s):
                wait(sem(f"x2_{s}"), held(nc.sync, i + (g * TURNS + 1)))
                sp.dma_start(d["x2s"][:, 2 * i + s, cols(g)], x2[:, s]).then_inc(sem(f"stored{s}"), 16)

            for g in range(HALVES):
                for s in range(2):
                    load_w(g, 0, s)
                load_z(g)
                with nc.sync.Fori(1, TURNS) as i:
                    for s in range(2):
                        load_w(g, i, s)
                    for s in range(2):
                        store(g, nc.sync.snap(i - 1), s)
                for s in range(2):
                    store(g, TURNS - 1, s)
            for s in range(2):
                sp.wait_ge(sem(f"stored{s}"), 16 * HALVES * TURNS)

        @block.gpsimd
        def _(pool):
            def split_w(turn, s):
                hold(pool, gate["pool"], sem(f"hi{s}"), turn + 1)
                nc.gpsimd.tensor_tensor(w_lo[:, s], raw[:, s], w_hi[:, s].bitcast(F32), ALU.subtract).then_inc(sem(f"lo{s}"), 1)

            with nc.gpsimd.Fori(0, HALVES * TURNS) as turn:
                for s in range(2):
                    split_w(turn, s)

        @block.scalar
        def _(act):
            def wait(s, value):
                hold(act, gate["act"], s, value)

            def split_z(g):
                with nc.scalar.Fori(0, ZT) as j:
                    for s in range(2):
                        wait(sem(f"z_raw{s}"), nc.scalar.snap((j + (g * ZT + 1)) * 16))
                        if g:
                            wait(sem("z_used"), nc.scalar.snap(2 * j + (s + 1 + ended(TURNS - 1, 0))))
                        nc.scalar.activation(z_hi[:, bass.ds(2 * j + s, 1)], z_raw[:, s:s + 1], ACT.Copy).then_inc(sem(f"z_hi{s}"), 1)

            def split_w(turn, s, first=False):
                wait(sem(f"raw{s}"), held(nc.scalar, turn * 16 + 16))
                if not first:
                    wait(sem("z_used"), held(nc.scalar, ended(turn - 1, s)))
                nc.scalar.activation(w_hi[:, s], raw[:, s], ACT.Copy).then_inc(sem(f"hi{s}"), 1)

            for g in range(HALVES):
                split_w(g * TURNS, 0, g == 0)
                split_z(g)
                split_w(g * TURNS, 1, g == 0)
                with nc.scalar.Fori(1, TURNS) as i:
                    for s in range(2):
                        split_w(nc.scalar.snap(i + g * TURNS), s)

        @block.tensor
        def _(pe):
            def tile(turn, g, s):
                hold(pe, gate["pe"], sem(f"hi{s}"), turn + 1)
                hold(pe, gate["pe"], sem(f"lo{s}"), turn + 1)
                hold(pe, gate["pe"], sem(f"x2_{s}"), turn)
                for k in range(NFF):
                    pe.wait_ge(sem(f"z_lo{k % 2}"), g * ZT + k // 2 + 1)
                    for n, (w, x) in enumerate(((w_hi, z_hi), (w_hi, z_lo), (w_lo, z_hi))):
                        mm = nc.tensor.matmul(ps[s][:], w[:, s, k], x[:, k], start=(k == 0 and n == 0), stop=(k == NFF - 1 and n == 2))
                    mm.then_inc(sem("z_used"), 1)

            for g in range(HALVES):
                with nc.tensor.Fori(0, TURNS) as i:
                    turn = nc.tensor.snap(i + g * TURNS)
                    for s in range(2):
                        tile(turn, g, s)

        @block.vector
        def _(dve):
            def wait(s, value):
                hold(dve, gate["dve"], s, value)

            for g in range(HALVES):
                with nc.vector.Fori(0, ZT) as j:
                    for s in range(2):
                        wait(sem(f"z_hi{s}"), nc.vector.snap(j + (g * ZT + 1)))
                        k = bass.ds(2 * j + s, 1)
                        nc.vector.tensor_tensor(z_lo[:, k], z_raw[:, s:s + 1], z_hi[:, k].bitcast(F32), ALU.subtract).then_inc(sem(f"z_lo{s}"), 1)
                with nc.vector.Fori(0, TURNS) as i:
                    turn = nc.vector.snap(i + g * TURNS)
                    for s in range(2):
                        wait(sem("z_used"), nc.vector.snap(ended(turn, s)))
                        wait(sem(f"x1_{s}"), nc.vector.snap(turn * 16 + 16))
                        wait(sem(f"stored{s}"), nc.vector.snap(turn * 16))
                        nc.vector.scalar_tensor_tensor(out=x2[:, s], in0=ps[s][:], scalar=t["mod"][:, 0, bass.ds(2 * i + (s + 40), 1)],
                                                       in1=x1[:, s], op0=ALU.mult, op1=ALU.add).then_inc(sem(f"x2_{s}"), 1)
def attention(nc, d, t):
    NT = 4
    QT = SEQ // P
    FOX, SB = 4, 2
    W_POOL = ((2, 4), (8, 16))
    RIM = 16
    cols = lambda g: slice(BANK * g, BANK * (g + 1))
    with ExitStack() as st:
        sem = Sems(nc, st, "g_")
        sb = lambda n, s, dt=F32: st.enter_context(nc.sbuf_tensor("g_" + n, s, dt))
        raw = sb("raw", [P, NT, KD, P])
        w_hi, w_lo = sb("w_hi", [P, NT, KD, P], F32R), sb("w_lo", [P, NT, KD, P], F32R)
        q, k, v = sb("q", [P, SEQ]), sb("k", [P, SEQ]), sb("v", [P, SEQ])
        sq, rstd = sb("sq", [P, 2, SEQ]), sb("rstd", [P, 2, SEQ])
        vt = sb("vt", [P, QT, P])
        gs = sb("gs", [P, SEQ])
        out = sb("out", [P, SEQ])
        cum = sb("cum", [8, SEQ])
        csel = sb("csel", [8, 2, SEQ])
        negc = sq
        sc = sb("sc", [P, 2, SEQ])
        s2 = sb("s2", [P, 2, SEQ])
        pt = sb("pt", [P, 2, QT, P])
        mx, den, rden = sb("mx", [P, 2]), sb("den", [P, 4]), sb("rden", [P, 4])
        ot = sb("ot", [P, 2, P])
        qg8 = sb("qg8", [P, 1])
        wpool = sb("wpool", [P, 2, P])
        ps = [st.enter_context(nc.psum_tensor(f"g_ps{n}", [P, BANK], F32)) for n in range(2)]
        pb = [st.enter_context(nc.psum_tensor(f"g_pb{n}", [P, 2 * BANK], F32)) for n in range(3)]
        gate = {n: sem("passed_" + n) for n in ("pe", "sp", "act", "dve", "pool")}
        h_hi, h_lo, ident = t["h3_hi"], t["h3_lo"], t["c_ident"]
        TURNS = 2 + FOX + SB
        block = st.enter_context(nc.Block())
        full = {n: sem("full_" + n) for n in ("pb0", "pb1", "pb2", "ps0", "ps1")}
        free = {n: sem("free_" + n) for n in ("pb0", "pb1", "pb2", "ps0", "ps1")}
        buf = {"pb0": pb[0], "pb1": pb[1], "pb2": pb[2], "ps0": ps[0], "ps1": ps[1]}
        UNITS = 2 * QT
        USES_POOL = {"pb0": 2, "pb1": 2, "pb2": 2, "ps0": 1, "ps1": 1}
        USES_FOX = {"pb0": 3 + QT, "pb1": 3 + QT, "pb2": 2 + UNITS, "ps0": 1 + UNITS, "ps1": 1 + QT}
        USES_SB = {"pb0": 1 + QT, "pb1": 1 + QT, "pb2": 2 + UNITS, "ps0": 1 + UNITS, "ps1": 1 + QT}
        unit = lambda u: (u // 2, u % 2, P * (u // 2 + 1))

        def bases(eng, i, sbr):
            if not sbr:
                return {n: eng.snap(i * USES_FOX[n] + USES_POOL[n]) for n in full}
            return {n: eng.snap(i * USES_SB[n] + (USES_POOL[n] + FOX * USES_FOX[n])) for n in full}

        @block.sync
        def _(sp):
            def wait(s, value):
                hold(sp, gate["sp"], s, value)

            def load(n):
                for tl in range(NT):
                    wait(sem(f"lo{tl}"), n)
                sp.dma_start(raw[:], d["w2"][n]).then_inc(sem("raw"), 16)

            def store(n, tile):
                wait(sem("out"), held(nc.sync, n + 1))
                sp.dma_start(d["mix2"][:, tile], out[:]).then_inc(sem("stored"), 16)

            sp.dma_start(raw[:], d["w2"][0]).then_inc(sem("raw"), 16)
            sp.wait_ge(sem("wpool0"), 1)
            for g in range(4):
                half = slice(HEAD * (g % 2), HEAD * (g % 2) + HEAD)
                sp.dma_start(wpool[half, g // 2, half], d["w_pool"][g]).then_inc(sem("wpool"), 16)
            for j in range(2):
                load(j + 1)
                store(j, FOX + j)
            with nc.sync.Fori(0, FOX) as i:
                load(nc.sync.snap(i + 3))
                store(nc.sync.snap(i + 2), i)
            load(7)
            store(2 + FOX, FOX + 2)
            store(3 + FOX, FOX + 3)
            sp.wait_ge(sem("stored"), 16 * TURNS)

        @block.tensor
        def _(pe):
            def wait(s, value):
                hold(pe, gate["pe"], s, value)

            def tile(n, tl, outs):
                wait(sem(f"hi{tl}"), n + 1)
                wait(sem(f"lo{tl}"), n + 1)
                for g, (o, name, reads) in enumerate(outs):
                    wait(free[name], reads)
                    mm = product(nc, o, w_hi[:, tl], w_lo[:, tl], h_hi, h_lo, KD, cols(g))
                    if g or outs[1][1] != name:
                        mm.then_inc(full[name], 1)

            def both(name, reads):
                return [(buf[name][:, cols(g)], name, reads) for g in range(2)]

            def pooled_turn(j):
                if j == 0:
                    tile(0, 0, [(ps[0][:], "ps0", 0), (ps[1][:], "ps1", 0)])
                    pe.wait_ge(sem("wpool"), 64)
                tile(j, 1 - j, both("pb0", j))
                tile(j, 2 - j, both("pb1", j))
                pe.wait_ge(sem("pooled"), j + 1)
                wait(free["pb2"], j)
                for g in range(2):
                    mm = nc.tensor.matmul(pb[2][:, cols(g)], wpool[:, j], q[:, cols(g)], start=True, stop=True)
                mm.then_inc(full["pb2"], 1)

            def scores(u, first, base, mask):
                qt, h, keys = unit(u)
                name, rows = f"pb{u % 2}", slice(HEAD * h, HEAD * h + HEAD)
                wait(free[name], base[name] + (first + u // 2))
                for at in range(0, keys, BANK):
                    to = min(keys, at + BANK)
                    mm = nc.tensor.matmul(buf[name][:, at:to], q[rows, P * qt:P * (qt + 1)], k[rows, at:to], start=True,
                                          stop=(to < keys))
                mm = nc.tensor.matmul(buf[name][:, keys - P:keys], ident, mask, start=False, stop=True)
                mm.then_inc(full[name], 1)

            def turn_weights(u, base):
                qt, h, keys = unit(u)
                wait(sem(f"weights{u % 2}"), base[f"w{u % 2}"] + (u // 2 + 1))
                wait(free["pb2"], base["pb2"] + (2 + u))
                for b in range(qt + 1):
                    mm = nc.tensor.transpose(pb[2][:, P * b:P * (b + 1)], s2[:, u % 2, P * b:P * (b + 1)], ident)
                mm.then_inc(full["pb2"], 1)

            def values(u, base):
                qt, h, keys = unit(u)
                wait(free["pb2"], base["pb2"] + (3 + u))
                wait(free["ps0"], base["ps0"] + (1 + u))
                for b in range(qt + 1):
                    mm = nc.tensor.matmul(ps[0][:, 0:HEAD], pt[:, u % 2, b], vt[:, b, HEAD * h:HEAD * (h + 1)],
                                          start=(b == 0), stop=(b == qt))
                mm.then_inc(full["ps0"], 1)

            def turn_output(qt, base):
                wait(free["ps0"], base["ps0"] + (1 + 2 * (qt + 1)))
                wait(free["ps1"], base["ps1"] + (1 + qt))
                nc.tensor.transpose(ps[1][:, 0:P], ot[:, qt % 2], ident).then_inc(full["ps1"], 1)

            def heads(n, i, sbr):
                base = bases(nc.tensor, i, sbr)
                w = nc.tensor.snap(i * QT + (FOX * QT if sbr else 0))
                base.update(w0=w, w1=w)
                tile(n, 0, both("pb0", base["pb0"]))
                tile(n, 1, both("pb1", base["pb1"]))
                tile(n, 2, both("pb2", base["pb2"]))
                tile(n, 3, [(ps[0][:], "ps0", base["ps0"]), (ps[1][:], "ps1", base["ps1"])])
                wait(free["pb2"], base["pb2"] + 1)
                for b in range(QT):
                    mm = nc.tensor.transpose(pb[2][:, P * b:P * (b + 1)], v[:, P * b:P * (b + 1)], ident)
                mm.then_inc(full["pb2"], 1)
                if not sbr:
                    for x, name in ((0, "pb0"), (1, "pb1")):
                        wait(sem("sq"), i * 2 + (x + 1))
                        wait(free[name], base[name] + 1)
                        for g in range(2):
                            mm = nc.tensor.matmul(buf[name][:, cols(g)], t["c_headones"], sq[:, x, cols(g)], start=True, stop=True)
                        mm.then_inc(full[name], 1)
                    for x, name in ((0, "pb0"), (1, "pb1")):
                        wait(sem("csel"), i * 2 + (x + 1))
                        wait(free[name], base[name] + 2)
                        for g in range(2):
                            mm = nc.tensor.matmul(buf[name][:, cols(g)], t["c_ones"][0:8], csel[:, x, cols(g)], start=True, stop=True)
                        mm.then_inc(full[name], 1)
                    wait(sem("qk"), i * 2 + 2)
                else:
                    for name in ("pb0", "pb1"):
                        wait(free[name], base[name] + 1)
                wait(free["pb2"], base["pb2"] + 2)
                first = 1 if sbr else 3
                mask = t["c_negstrict"] if sbr else t["c_negcausal"]
                scores(0, first, base, mask)
                scores(1, first, base, mask)
                for u in range(UNITS + 3):
                    if u < UNITS:
                        turn_weights(u, base)
                    if u + 2 < UNITS:
                        scores(u + 2, first, base, mask)
                    if 1 <= u <= UNITS:
                        values(u - 1, base)
                    if u >= 3 and u % 2:
                        turn_output((u - 3) // 2, base)

            for j in range(2):
                pooled_turn(j)
            with nc.tensor.Fori(0, FOX) as i:
                heads(nc.tensor.snap(i + 2), i, False)
            with nc.tensor.Fori(0, SB) as i:
                heads(nc.tensor.snap(i + (2 + FOX)), i, True)

        @block.scalar
        def _(act):
            def wait(s, value):
                hold(act, gate["act"], s, value)

            def split_hi(n, tl):
                wait(sem("raw"), n * 16 + 16)
                nc.scalar.activation(w_hi[:, tl], raw[:, tl], ACT.Copy).then_inc(sem(f"hi{tl}"), 1)

            def pooled_turn(j):
                if j == 0:
                    for g in range(2):
                        act.wait_ge(full[f"ps{g}"], 1)
                        nc.scalar.activation(csel[:, 0, cols(g)], ps[g][0:8, :], ACT.Abs, bias=t["v_b_f"][0:8]).then_inc(sem("ff"), 1)
                    act.wait_ge(sem("ff"), 2)
                    nc.scalar.activation(csel[:, 0], csel[:, 0], ACT.Exp, scale=-1.0).then_inc(sem("ff"), 1)
                    act.wait_ge(sem("ff"), 3)
                    nc.scalar.activation(csel[:, 0], csel[:, 0], ACT.Ln, bias=1.0).then_inc(sem("ff"), 1)
                act.wait_ge(full["pb0"], j + 1)
                act.wait_ge(sem("pooled"), j)
                nc.scalar.activation(v[:], pb[0][:], ACT.Copy).then_inc(free["pb0"], 1)
                act.wait_ge(full["pb1"], j + 1)
                act.wait_ge(sem("out"), j)
                nc.scalar.activation(gs[:], pb[1][:], ACT.Silu).then_inc(free["pb1"], 1)
                for tl in range(NT):
                    split_hi(j + 1, tl)

            def heads(n, i, sbr, last):
                base = bases(nc.scalar, i, sbr)
                for tl, name, dst in ((0, "pb0", q), (1, "pb1", k), (2, "pb2", v)):
                    wait(full[name], base[name] + 1)
                    nc.scalar.activation(dst[:], buf[name][:], ACT.Copy, scale=0.125 if sbr and tl == 0 else 1.0).then_inc(free[name], 1)
                    if not last:
                        split_hi(n + 1, tl)
                wait(full["pb2"], base["pb2"] + 2)
                nc.scalar.activation(vt[:].rearrange("p b c -> p (b c)"), pb[2][:], ACT.Copy).then_inc(free["pb2"], 1)
                wait(sem("out"), n)
                for g in range(2):
                    wait(full[f"ps{g}"], base[f"ps{g}"] + 1)
                    nc.scalar.activation(gs[:, cols(g)], ps[g][:], ACT.Silu).then_inc(free[f"ps{g}"], 1)
                if not last:
                    split_hi(n + 1, 3)
                if not sbr:
                    for x, name in ((0, "pb0"), (1, "pb1")):
                        wait(full[name], base[name] + 2)
                        nc.scalar.activation(rstd[:, x], buf[name][:], ACT.Sqrt, scale=1.0 / HEAD, bias=t["c_eps"]).then_inc(free[name], 1)
                    for x, name in ((0, "pb0"), (1, "pb1")):
                        wait(full[name], base[name] + 3)
                        nc.scalar.activation(negc[:, x], buf[name][:], ACT.Copy, scale=-1.0).then_inc(free[name], 1)
                    for u in range(UNITS):
                        qt, h, keys = unit(u)
                        wait(sem("mx"), i * UNITS + (u + 1))
                        if u >= 2:
                            wait(full["pb2"], base["pb2"] + (2 + u - 1))
                        nc.scalar.activation(s2[:, u % 2, 0:keys], sc[:, u % 2, 0:keys], ACT.Exp, bias=mx[:, u % 2:u % 2 + 1],
                                             accum_out=den[:, u % 4:u % 4 + 1]).then_inc(sem(f"weights{u % 2}"), 1)
                else:
                    def front(u):
                        qt, h, keys = unit(u)
                        name, x = f"pb{u % 2}", s2[:, u % 2, 0:keys]
                        wait(full[name], base[name] + (2 + u // 2))
                        if u >= 2:
                            wait(full["pb2"], base["pb2"] + (2 + u - 1))
                        nc.scalar.activation(x, buf[name][:, 0:keys], ACT.Abs).then_inc(sem("abs"), 1)
                        wait(sem("abs"), i * UNITS + (u + 1))
                        nc.scalar.activation(x, x, ACT.Exp, scale=-1.0).then_inc(sem("exp"), 1)
                        wait(sem("exp"), i * UNITS + (u + 1))
                        nc.scalar.activation(x, x, ACT.Ln, bias=1.0).then_inc(sem("ln"), 1)

                    front(0)
                    front(1)
                    for u in range(UNITS):
                        qt, h, keys = unit(u)
                        wait(sem("logits"), i * UNITS + (u + 1))
                        nc.scalar.activation(s2[:, u % 2, 0:keys], sc[:, u % 2, 0:keys], ACT.Exp).then_inc(sem(f"weights{u % 2}"), 1)
                        if u + 2 < UNITS:
                            front(u + 2)

            for tl in range(NT):
                split_hi(0, tl)
            for j in range(2):
                pooled_turn(j)
            with nc.scalar.Fori(0, FOX) as i:
                heads(nc.scalar.snap(i + 2), i, False, False)
            with nc.scalar.Fori(0, 1) as i:
                heads(nc.scalar.snap(i + (2 + FOX)), i, True, False)
            with nc.scalar.Fori(1, 2) as i:
                heads(nc.scalar.snap(i + (2 + FOX)), i, True, True)

        @block.gpsimd
        def _(pool):
            nc.gpsimd.memset(wpool[:], 0.0).then_inc(sem("wpool0"), 1)
            with nc.gpsimd.Fori(0, TURNS) as n:
                for tl in range(NT):
                    hold(pool, gate["pool"], sem(f"hi{tl}"), n + 1)
                    nc.gpsimd.tensor_tensor(w_lo[:, tl], raw[:, tl], w_hi[:, tl].bitcast(F32), ALU.subtract).then_inc(sem(f"lo{tl}"), 1)

        @block.vector
        def _(dve):
            TT, TS, STT = nc.vector.tensor_tensor, nc.vector.tensor_scalar, nc.vector.scalar_tensor_tensor

            def wait(s, value):
                hold(dve, gate["dve"], s, value)

            def ones(n):
                return t["c_ones"][:, 0:1].broadcast_to([P, n])

            def forget_sums():
                for g in range(2):
                    dve.wait_ge(sem("ff"), 4)
                    TS(csel[:, 1, cols(g)], ps[g][0:8, :], t["v_b_f"][0:8], 0.0, ALU.add, ALU.min).then_inc(free[f"ps{g}"], 1)
                for g in range(2):
                    dve.wait_ge(free[f"ps{g}"], 1)
                TT(csel[:, 1], csel[:, 1], csel[:, 0], ALU.subtract).then_inc(sem("logf"), 1)
                dve.wait_ge(sem("logf"), 1)
                nc.vector.tensor_tensor_scan(cum[:], ones(SEQ)[0:8], csel[:, 1], 0.0, ALU.mult, ALU.add).then_inc(sem("cum"), 1)

            def pooled_turn(j):
                run = sq[:].rearrange("p x s -> p (x s)")
                dve.wait_ge(free["pb0"], j + 1)
                dve.wait_ge(sem("rim"), 1)
                nc.vector.tensor_tensor_scan(run[:, RIM:RIM + SEQ], ones(SEQ), v[:], 0.0, ALU.mult, ALU.add).then_inc(sem("run"), 1)
                dve.wait_ge(sem("run"), j + 1)
                mean = rstd[:, 0]
                for h, win in enumerate(W_POOL[j]):
                    rows = slice(HEAD * h, HEAD * h + HEAD)
                    TT(mean[rows], run[rows, RIM:RIM + SEQ], run[rows, RIM - win:RIM + SEQ - win], ALU.subtract).then_inc(sem("diff"), 1)
                dve.wait_ge(sem("diff"), 2 * j + 2)
                TT(mean[:, 0:RIM], mean[:, 0:RIM], t["c_invcount"][:, j], ALU.mult).then_inc(sem("mean"), 1)
                STT(out=q[:, RIM:SEQ], in0=mean[:, RIM:SEQ], scalar=t["c_invwin"][:, j:j + 1], in1=v[:, RIM:SEQ],
                    op0=ALU.mult, op1=ALU.subtract).then_inc(sem("rest"), 1)
                dve.wait_ge(sem("mean"), j + 1)
                dve.wait_ge(sem("rest"), j + 1)
                TT(q[:, 0:RIM], mean[:, 0:RIM], v[:, 0:RIM], ALU.subtract).then_inc(sem("pooled"), 1)
                dve.wait_ge(full["pb2"], j + 1)
                dve.wait_ge(free["pb1"], j + 1)
                dve.wait_ge(sem("stored"), 16 * j)
                STT(out=out[:], in0=pb[2][:], scalar=t["v_pool_scale"][:, j:j + 1], in1=gs[:], op0=ALU.mult,
                    op1=ALU.mult).then_inc(free["pb2"], 1)
                dve.wait_ge(free["pb2"], j + 1)
                dve.sem_inc(sem("out"), 1)

            def heads(n, i, sbr):
                base = bases(nc.vector, i, sbr)

                def mid_fox(u):
                    qt, h, keys = unit(u)
                    name = f"pb{u % 2}"
                    wait(full[name], base[name] + (4 + u // 2))
                    if u >= 2:
                        wait(sem(f"weights{u % 2}"), i * QT + u // 2)
                    nc.vector.tensor_tensor_reduce(out=sc[:, u % 2, 0:keys], in0=buf[name][:, 0:keys], in1=negc[:, h, 0:keys],
                                                   scale=1.0, scalar=-3.0e38, op0=ALU.add, op1=ALU.max,
                                                   accum_out=mx[:, u % 2:u % 2 + 1]).then_inc(free[name], 1)
                    wait(free[name], base[name] + (4 + u // 2))
                    TS(mx[:, u % 2:u % 2 + 1], mx[:, u % 2:u % 2 + 1], -1.0, None, ALU.mult).then_inc(sem("mx"), 1)

                def mid_sb(u):
                    qt, h, keys = unit(u)
                    name = f"pb{u % 2}"
                    z, x, y = buf[name][:, 0:keys], sc[:, u % 2, 0:keys], s2[:, u % 2, 0:keys]
                    wait(sem("ln"), i * UNITS + (u + 1))
                    STT(out=x, in0=z, scalar=0.0, in1=y, op0=ALU.max, op1=ALU.add).then_inc(sem("softplus"), 1)
                    wait(sem("softplus"), i * UNITS + (u + 1))
                    nc.vector.tensor_tensor_scan(y[:, ::-1], ones(keys), x[:, ::-1], 0.0, ALU.mult, ALU.add).then_inc(sem("suffix"), 1)
                    wait(sem("suffix"), i * UNITS + (u + 1))
                    TT(x, z, y, ALU.subtract).then_inc(free[name], 1)
                    wait(free[name], base[name] + (2 + u // 2))
                    dve.sem_inc(sem("logits"), 1)

                def weights_out(u):
                    qt, h, keys = unit(u)
                    wait(full["pb2"], base["pb2"] + (3 + u))
                    if u >= 2:
                        wait(full["ps0"], base["ps0"] + (1 + u - 1))
                    nc.vector.tensor_copy(pt[:, u % 2, 0:qt + 1].rearrange("p b c -> p (b c)"), pb[2][:, 0:keys]).then_inc(free["pb2"], 1)

                def values_out(u):
                    qt, h, keys = unit(u)
                    dst = ot[:, qt % 2, HEAD * h:HEAD * (h + 1)]
                    if not sbr:
                        wait(sem(f"weights{u % 2}"), i * QT + (u // 2 + 1))
                        nc.vector.reciprocal(rden[:, u % 4:u % 4 + 1], den[:, u % 4:u % 4 + 1]).then_inc(sem("rden"), 1)
                        wait(sem("rden"), i * UNITS + (u + 1))
                    wait(full["ps0"], base["ps0"] + (2 + u))
                    if qt >= 2:
                        wait(full["ps1"], base["ps1"] + (1 + qt - 1))
                    if sbr:
                        nc.vector.tensor_copy(dst, ps[0][:, 0:HEAD]).then_inc(free["ps0"], 1)
                    else:
                        TS(dst, ps[0][:, 0:HEAD], rden[:, u % 4:u % 4 + 1], None, ALU.mult).then_inc(free["ps0"], 1)

                def gated(qt):
                    wait(full["ps1"], base["ps1"] + (2 + qt))
                    TT(out[:, P * qt:P * (qt + 1)], ps[1][:, 0:P], gs[:, P * qt:P * (qt + 1)], ALU.mult).then_inc(free["ps1"], 1)

                if not sbr:
                    for x, name, src in ((0, "pb0", q), (1, "pb1", k)):
                        wait(free[name], base[name] + 1)
                        TT(sq[:, x], src[:], src[:], ALU.mult).then_inc(sem("sq"), 1)
                    for x in range(2):
                        TS(csel[:, x], cum[:], t["c_headsel"][0:8, bass.ds(2 * i + x, 1)], None, ALU.mult).then_inc(sem("csel"), 1)
                    for x, name, src, g in ((0, "pb0", q, qg8[:]), (1, "pb1", k, t["v_kg"])):
                        wait(free[name], base[name] + 2)
                        nc.vector.reciprocal(rstd[:, x], rstd[:, x]).then_inc(sem("rstd"), 1)
                        wait(sem("rstd"), i * 2 + (x + 1))
                        STT(out=src[:], in0=src[:], scalar=g, in1=rstd[:, x], op0=ALU.mult, op1=ALU.mult).then_inc(sem("qk"), 1)
                    for x, name in ((0, "pb0"), (1, "pb1")):
                        wait(free[name], base[name] + 3)
                wait(sem("stored"), n * 16)
                mid = mid_sb if sbr else mid_fox
                mid(0)
                mid(1)
                for u in range(UNITS + 3):
                    if u < UNITS:
                        weights_out(u)
                    if u + 2 < UNITS:
                        mid(u + 2)
                    if 1 <= u <= UNITS:
                        values_out(u - 1)
                    if u >= 3 and u % 2:
                        gated((u - 3) // 2)
                wait(free["ps1"], base["ps1"] + (1 + QT))
                dve.sem_inc(sem("out"), 1)

            nc.vector.memset(sq[:, 0, 0:RIM], 0.0).then_inc(sem("rim"), 1)
            TS(qg8[:], t["v_qg"], 0.125, None, ALU.mult).then_inc(sem("qg8"), 1)
            forget_sums()
            for j in range(2):
                pooled_turn(j)
            dve.wait_ge(sem("cum"), 1)
            dve.wait_ge(sem("qg8"), 1)
            with nc.vector.Fori(0, FOX) as i:
                heads(nc.vector.snap(i + 2), i, False)
            with nc.vector.Fori(0, SB) as i:
                heads(nc.vector.snap(i + (2 + FOX)), i, True)


def output(nc, d, t):
    G = range(2)
    cols = lambda g: slice(BANK * g, BANK * (g + 1))
    with ExitStack() as st:
        sem = Sems(nc, st, "h_")
        sb = lambda n, s, dt=F32: st.enter_context(nc.sbuf_tensor("h_" + n, s, dt))
        mix, x3 = sb("mix", [P, KD, SEQ]), sb("x3", [P, KD, SEQ])
        m_hi, m_lo = sb("m_hi", [P, KD, SEQ], F32R), sb("m_lo", [P, KD, SEQ], F32R)
        raw = sb("raw", [P, 2, KD, P])
        w_hi, w_lo = sb("w_hi", [P, 2, KD, P], F32R), sb("w_lo", [P, 2, KD, P], F32R)
        ps = [st.enter_context(nc.psum_tensor(f"h_ps{n}", [P, BANK], F32)) for n in range(4)]
        full = [sem(f"psum_full{b}") for b in range(4)]
        free = [sem(f"psum_free{b}") for b in range(4)]
        gate = {n: sem("passed_" + n) for n in ("pe", "sp", "act", "dve", "pool")}
        block = st.enter_context(nc.Block())

        @block.sync
        def _(sp):
            sp.dma_start(raw[:], d["w_out_2"][0]).then_inc(sem("raw"), 16)
            for k in range(KD):
                sp.dma_start(mix[:, k], d["mix2"][:, k]).then_inc(sem("mix"), 16)
            sp.dma_start(x3[:], d["x3s"]).then_inc(sem("x3"), 16)

            def store(i):
                for s in range(2):
                    for g in G:
                        hold(sp, gate["sp"], free[2 * s + g], held(nc.sync, i + 1))
                    sp.dma_start(d["out"][2 * i + s], x3[:, 2 * i + s]).then_inc(sem("stored"), 16)

            with nc.sync.Fori(0, 3) as i:
                n = nc.sync.snap(i + 1)
                for s in range(2):
                    hold(sp, gate["sp"], sem(f"lo{s}"), n)
                sp.dma_start(raw[:], d["w_out_2"][n]).then_inc(sem("raw"), 16)
                store(nc.sync.snap(i + 0))
            store(3)
            sp.wait_ge(sem("stored"), 16 * KD)

        @block.tensor
        def _(pe):
            pe.wait_ge(sem("mix_lo"), KD)
            with nc.tensor.Fori(0, 4) as i:
                n = nc.tensor.snap(i + 1)
                for s in range(2):
                    hold(pe, gate["pe"], sem(f"hi{s}"), n)
                    hold(pe, gate["pe"], sem(f"lo{s}"), n)
                    for g in G:
                        b = 2 * s + g
                        hold(pe, gate["pe"], free[b], i)
                        product(nc, ps[b][:], w_hi[:, s], w_lo[:, s], m_hi, m_lo, KD, cols(g)).then_inc(full[b], 1)

        @block.scalar
        def _(act):
            def split_hi(n, s):
                hold(act, gate["act"], sem("raw"), n * 16 + 16)
                if not isinstance(n, int):
                    hold(act, gate["act"], full[2 * s + 1], n)
                nc.scalar.activation(w_hi[:, s], raw[:, s], ACT.Copy).then_inc(sem(f"hi{s}"), 1)

            for s in range(2):
                split_hi(0, s)
            for k in range(KD):
                act.wait_ge(sem("mix"), 16 * KD)
                nc.scalar.activation(m_hi[:, k], mix[:, k], ACT.Copy).then_inc(sem("mix_hi"), 1)
            with nc.scalar.Fori(1, 4) as n:
                for s in range(2):
                    split_hi(n, s)

        @block.gpsimd
        def _(pool):
            with nc.gpsimd.Fori(0, 4) as n:
                for s in range(2):
                    hold(pool, gate["pool"], sem(f"hi{s}"), n + 1)
                    nc.gpsimd.tensor_tensor(w_lo[:, s], raw[:, s], w_hi[:, s].bitcast(F32), ALU.subtract).then_inc(sem(f"lo{s}"), 1)

        @block.vector
        def _(dve):
            for k in range(KD):
                dve.wait_ge(sem("mix_hi"), k + 1)
                nc.vector.tensor_tensor(m_lo[:, k], mix[:, k], m_hi[:, k].bitcast(F32), ALU.subtract).then_inc(sem("mix_lo"), 1)
            dve.wait_ge(sem("x3"), 16)
            with nc.vector.Fori(0, 4) as i:
                n = nc.vector.snap(i + 1)
                for s in range(2):
                    for g in G:
                        b = 2 * s + g
                        hold(dve, gate["dve"], full[b], n)
                        xs = x3[:, bass.ds(2 * i + s, 1), cols(g)]
                        nc.vector.tensor_tensor(xs, ps[b][:].unsqueeze(1), xs, ALU.add).then_inc(free[b], 1)


DRAM_IN = {"vecs": [P, NVEC], "consts": [P, NCON], "xT": [P, KD, SEQ], "ctxT": [P, KD, CTX], "ada": [24, P, 2, KD, P],
           "w1": [9, P, 3, KD, P], "w_up": [2, C, CH], "a_up": [2, C, CH], "g_up": [P, CH], "w_out": [4, P, 2, KD, P],
           "w_ffn": [NFF, P, 2, KD, P], "w_down": [KD, P, NFF, P], "w2": [8, P, 4, KD, P], "w_pool": [4, HEAD, HEAD],
           "w_out_2": [4, P, 2, KD, P]}
SCRATCH = {"rkv": [SLOTS, P, 4, PAIRS, C], "ys": [2, SLOTS, P, PAIRS, C], "x1s": [P, KD, SEQ], "zs": [NFF, P, SEQ],
           "x2s": [P, KD, SEQ], "x3s": [P, KD, SEQ], "mix2": [P, KD, SEQ]}


def program(nc):
    d = {n: nc.dram_tensor(n, s, F32, kind="ExternalInput").ap() for n, s in DRAM_IN.items()}
    d.update({n: nc.dram_tensor(n, s, F32, kind="Internal").ap() for n, s in SCRATCH.items()})
    d["out"] = nc.dram_tensor("out", [KD, P, SEQ], F32, kind="ExternalOutput").ap()
    with ExitStack() as whole:
        keep = lambda st, n, s, dt=F32, **k: st.enter_context(nc.sbuf_tensor(n, s, dt, **k))[:]
        t = {"vec": keep(whole, "vec", [P, NVEC]), "con": keep(whole, "con", [P, NCON]),
             "mod": keep(whole, "mod", [P, 2, 48]), "silu_c": keep(whole, "silu_c", [P, KD, 2]),
             "c_eps": keep(whole, "eps", [P, 1]), "c_gneps": keep(whole, "gneps", [P, 1])}
        for n, (at, m) in VECS.items():
            t["v_" + n] = t["vec"][:, at:at + m]
        for n, (at, m) in CONS.items():
            t["c_" + n] = t["con"][:, at:at + m]
        for n, inner in (("mask_ll", "p (x w c) -> p x w c"), ("mask_mm", "p (x w c) -> p x w c")):
            t["c_" + n] = t["c_" + n].rearrange(inner, x=2, w=2)
        for n in ("mask_l1", "mask_u1", "reset", "invcount"):
            t["c_" + n] = t["c_" + n].rearrange("p (x c) -> p x c", x=2)
        t["c_mask_lev"] = t["c_mask_lev"].rearrange("p (x l c) -> p x l c", x=2, l=LEVELS)
        with ExitStack() as mixer:
            with ExitStack() as st:
                t["h_hi"], t["h_lo"] = keep(st, "h_hi", [P, KD, TOK], F32R), keep(st, "h_lo", [P, KD, TOK], F32R)
                prologue(nc, d, t)
                t["mix"] = keep(mixer, "mix", [P, KD, SEQ], side="right")
                t["wa"] = keep(mixer, "wa", [P, TOK + CTX], side="right")
                t["sg"] = keep(mixer, "sg", [P, SEQ], side="right")
                projections(nc, d, t)
            scan(nc, d, t)
            ffn = whole.enter_context(ExitStack())
            t["h2_hi"], t["h2_lo"] = keep(ffn, "h2_hi", [P, KD, SEQ], F32R), keep(ffn, "h2_lo", [P, KD, SEQ], F32R)
            with ExitStack() as st:
                t["x1"] = keep(st, "x1", [P, KD, SEQ])
                mixer_out(nc, d, t)
                norm_x1(nc, d, t)
        ffn_up(nc, d, t)
        ffn.close()
        ffn_down(nc, d, t)
        with ExitStack() as st:
            t["h3_hi"], t["h3_lo"] = keep(st, "h3_hi", [P, KD, SEQ], F32R), keep(st, "h3_lo", [P, KD, SEQ], F32R)
            with ExitStack() as inner:
                t["x3"] = keep(inner, "x3", [P, KD, SEQ])
                norm_x3(nc, d, t)
            attention(nc, d, t)
        output(nc, d, t)


def norm_x1(nc, d, t):
    with ExitStack() as st:
        stored = Sems(nc, st, "n1_")("stored")
        with nc.Block() as block:
            @block.sync
            def _(sp):
                sp.dma_start(d["x1s"], t["x1"]).then_inc(stored, 16)
                sp.wait_ge(stored, 16)
        gain = lambda g: nc.vector.scalar_tensor_tensor(out=g, in0=t["mod"][:, 0, 32:40], scalar=1.0, in1=t["v_norm2_g"],
                                                        op0=ALU.add, op1=ALU.mult)
        rms(nc, t, "n1", t["x1"], t["x1"], (t["h2_hi"], t["h2_lo"]), gain, t["mod"][:, 0, 24:32])


def norm_x3(nc, d, t):
    with ExitStack() as st:
        loaded = Sems(nc, st, "n2_")("loaded")
        with nc.Block() as block:
            @block.sync
            def _(sp):
                sp.dma_start(t["x3"], d["x2s"]).then_inc(loaded, 16)
                sp.wait_ge(loaded, 16)
        rms(nc, t, "n2", t["x3"], t["x3"], None, lambda g: nc.vector.tensor_copy(g, t["v_final_g"]), None, d["x3s"])
        rms(nc, t, "n3", t["x3"], t["x3"], (t["h3_hi"], t["h3_lo"]), lambda g: nc.vector.tensor_copy(g, t["v_norm_g_2"]), None)


def constants():
    row, col = np.arange(P)[:, None], np.arange(P)[None, :]
    s, u = (np.arange(P) % C)[:, None], np.arange(C)[None, :]
    tri = lambda keep: keep.astype(np.float32)
    parts = {"ident": np.eye(P), "ones": np.ones((P, P)), "headones": tri(row // HEAD == col // HEAD), "identc": tri(s == u),
             "negcausal": -1e30 * tri(col > row), "negstrict": -1e30 * tri(col >= row)}
    before = [s < u, s > u]
    after = [s > u, s < u]
    parts["mask_ll"] = np.concatenate([np.concatenate([tri(b), -tri(b | (s == u))], 1) for b in before], 1)
    parts["mask_mm"] = np.concatenate([np.concatenate([tri(b), tri(b | (s == u))], 1) for b in before], 1)
    block = lambda m: s // m == u // m
    parts["mask_l1"] = np.concatenate([-tri(a & block(2)) for a in after], 1)
    parts["mask_u1"] = np.concatenate([-tri(b & block(2)) for b in before], 1)
    parts["mask_lev"] = np.concatenate([tri(b & block(2 ** (l + 2)) & ~block(2 ** (l + 1))) for b in before for l in range(LEVELS)], 1)
    first = np.tile(np.arange(C), PAIRS)[None, :]
    parts["reset"] = np.concatenate([np.repeat(tri(first != e), P, 0) for e in (0, C - 1)], 1)
    parts["headsel"] = np.eye(P)[:, 0:8]
    win = np.array([[2] * HEAD + [4] * HEAD, [8] * HEAD + [16] * HEAD]).T[:, :, None]
    parts["invcount"] = (1.0 / np.minimum(np.arange(16)[None, None, :] + 1, win)).reshape(P, 32)
    parts["invwin"] = (1.0 / win).reshape(P, 2)
    return np.concatenate([parts[n].astype(np.float32) for n in CONS], 1)


def kernel(**a):
    import concourse.bacc as bacc
    from concourse.bass_utils import run_bass_kernel_spmd

    a = {n: np.asarray(x) for n, x in a.items()}

    def tiles(w):
        return w.reshape(w.shape[0] // P, P, w.shape[1] // P, P).transpose(2, 1, 0, 3)

    def turns(w, order):
        w = tiles(w)
        return np.ascontiguousarray(w[np.array(order)].transpose(0, 2, 1, 3, 4))

    def column(v):
        return v.reshape(-1, P).T

    def featmajor(x):
        return np.ascontiguousarray(x.T.reshape(KD, P, x.shape[0]).transpose(1, 0, 2))

    w0a0 = np.stack([a["rw_w0"][0], a["rw_a0"][0]], 1)
    vec = {"norm1_g": column(a["norm1_g"][0]), "norm2_g": column(a["norm2_g"][0]), "final_g": column(a["final_g"]),
           "norm_g_2": column(a["norm_g_2"][0]), "ada_b": column(a["ada_b"][0]), "conv_a_w": column(a["conv_a_w"][0]),
           "w0a0": column(w0a0), "k_k": column(a["rw_k_k"][0]), "k_a": column(a["rw_k_a"][0]), "r_k": column(a["rw_r_k"][0]),
           "ln_g": column(a["rw_ln_g"][0]), "ln_b": column(a["rw_ln_b"][0]), "ffn_conv_w": column(a["ffn_conv_w"][0]),
           "ffn_conv_b": column(a["ffn_conv_b"][0]), "pool_scale": column(a["pool_scale_2"][0]),
           "cc": np.stack([column(a["c"][0]), column(a["c_ctx"])], 2).reshape(P, 16),
           "qg": np.tile(a["q_norm_g_2"][0], 2)[:, None], "kg": np.tile(a["k_norm_g_2"][0], 2)[:, None],
           "b_f": np.pad(a["b_f_2"][0], (0, P - 8))[:, None]}
    w_in = a["w_in"][0]
    w2 = a["w_in_2"][0]
    at = 4 * CH
    ff = np.pad(w2[:, at:at + 8], ((0, 0), (0, P - 8)))
    w2 = np.concatenate([w2[:, 0:at], w2[:, at + 8:], ff], 1)
    FF, Z = 28, 28
    given = {
        "vecs": np.concatenate([vec[n] for n in VECS], 1), "consts": constants(),
        "xT": featmajor(a["x"][0]), "ctxT": featmajor(a["ctx"][0]),
        "ada": turns(a["ada_w"][0], np.arange(48).reshape(24, 2)),
        "w1": turns(w_in, [[4 + j, 8 + j, j] for j in range(4)] + [[12 + j, 16 + j, 20 + j] for j in range(4)] + [[24, 25, 25]]),
        "w_up": a["rw_w_up"][0], "a_up": a["rw_a_up"][0], "g_up": a["rw_g_up"][0],
        "w_out": turns(a["w_out"][0], np.arange(8).reshape(4, 2)),
        "w_ffn": turns(a["ffn_w_up"][0], [[i, NFF + i] for i in range(NFF)]),
        "w_down": tiles(a["ffn_w_down"][0]),
        "w2": turns(w2, [[FF, 16, 18, Z], [17, 19, Z, Z]] + [[p, 4 + p, 8 + p, 12 + p] for p in range(4)]
                    + [[20 + p, 22 + p, 24 + p, 26 + p] for p in range(2)]),
        "w_pool": a["w_pool_2"][0], "w_out_2": turns(a["w_out_2"][0], np.arange(8).reshape(4, 2)),
    }
    nc = bacc.Bacc("TRN2", target_bir_lowering=False, num_devices=1)
    program(nc)
    got = run_bass_kernel_spmd(nc, [{n: np.ascontiguousarray(x) for n, x in given.items()}], core_ids=[0])
    out = got.results[0]["out"]
    return np.ascontiguousarray(out.reshape(D, SEQ).T)[None]
```

```python
import numpy as np
import concourse.bass as bass
import concourse.mybir as mybir
from contextlib import ExitStack

F32 = mybir.dt.float32
F32R = mybir.dt.float32r
ALU = mybir.AluOpType
ACT = mybir.ActivationFunctionType

P = 128
D = 1024
KD = D // P
SEQ, CTX = 1024, 256
TOK = CTX + SEQ
HEAD = 64
CH = 512
PAIRS = CH // P
NFF = 22
GRID_W = 64
GRID_H = SEQ // GRID_W
C = 64
NCTX, NSEQ = CTX // C, SEQ // C
STEPS = NCTX + NSEQ
SLOTS = STEPS + NCTX
LEVELS = 5
DECAY_SCALE = float(np.exp(-0.5))
RMS_EPS, GN_EPS = 1e-6, 64e-5
BANK = 512

VECS = {}
_at = 0
for _name, _n in (("norm1_g", 8), ("norm2_g", 8), ("final_g", 8), ("norm_g_2", 8), ("ada_b", 48),
                  ("conv_a_w", 12), ("w0a0", 16), ("k_k", 4), ("k_a", 4), ("r_k", 4), ("ln_g", 4),
                  ("ln_b", 4), ("ffn_conv_w", 9 * NFF), ("ffn_conv_b", NFF), ("pool_scale", 2),
                  ("cc", 16), ("qg", 1), ("kg", 1), ("b_f", 1)):
    VECS[_name] = (_at, _n)
    _at += _n
NVEC = _at

CONS = {}
_at = 0
for _name, _n in (("ident", P), ("ones", P), ("headones", P), ("identc", C), ("negcausal", P),
                  ("negstrict", P), ("strict", 2 * 2 * C), ("incl", 2 * C),
                  ("mask_u1", 2 * C), ("mask_lev", 2 * LEVELS * C), ("reset", 2 * BANK),
                  ("invcount", 2 * 16), ("invwin", 2)):
    CONS[_name] = (_at, _n)
    _at += _n
NCON = _at


def bc(ap, axis, n):
    shape = list(ap.shape)
    return ap.unsqueeze(axis).broadcast_to(shape[:axis] + [n] + shape[axis:])


class Sems:

    def __init__(self, nc, stack, prefix):
        self.nc, self.prefix, self.known = nc, prefix, {}
        stack.callback(self.close)

    def __call__(self, name):
        if name not in self.known:
            self.known[name] = self.nc.alloc_semaphore(name=self.prefix + name)
        return self.known[name]

    def close(self):
        self.nc.clear_and_free_semaphores(list(self.known.values()))
        self.nc.all_engine_barrier()


def hold(eng, gate, sem, value):
    if isinstance(value, int) and value <= 0:
        return
    eng.wait_ge(sem, value)
    if not isinstance(value, int):
        eng.sem_inc(gate, 1)


def held(eng, value):
    return value if isinstance(value, int) else eng.snap(value)


def product(nc, out, w_hi, w_lo, x_hi, x_lo, nk, cols):
    for k in range(nk):
        for n, (w, x) in enumerate(((w_hi, x_hi), (w_hi, x_lo), (w_lo, x_hi))):
            last = nc.tensor.matmul(out, w[:, k, :], x[:, k, cols], start=(k == 0 and n == 0),
                                    stop=(k == nk - 1 and n == 2))
    return last


def prologue(nc, d, t):
    groups = [(0, CTX, 1), (CTX, BANK, 0), (CTX + BANK, BANK, 0)]
    NADA = 2
    GADA = 16 // NADA
    with ExitStack() as st:
        sem = Sems(nc, st, "a_")
        sb = lambda n, s, dt=F32: st.enter_context(nc.sbuf_tensor("a_" + n, s, dt))
        xin = sb("xin", [P, KD, TOK])
        tmp = sb("tmp", [P, KD, TOK])
        rstd = sb("rstd", [P, TOK])
        adaw = sb("adaw", [P, 2, NADA, KD, P])
        silu_c = t["silu_c"]
        gain = sb("gain", [P, 2, KD])
        ps = [st.enter_context(nc.psum_tensor(f"a_ps{n}", [P, BANK], F32)) for n in range(4)]
        modps = ps[3][:, 0:32].rearrange("p (n c) -> p n c", c=2)
        vec, con = t["vec"], t["con"]
        block = st.enter_context(nc.Block())

        @block.sync
        def _(sp):
            sp.dma_start(vec, d["vecs"]).then_inc(sem("vecs"), 16)
            sp.dma_start(con, d["consts"]).then_inc(sem("consts"), 16)
            sp.dma_start(xin[:, :, 0:CTX], d["ctxT"]).then_inc(sem("x0"), 16)
            for n in range(2):
                sp.dma_start(adaw[:, n], d["ada"][n]).then_inc(sem(f"ada{n}"), 16)
            for g in (1, 2):
                sp.dma_start(xin[:, :, CTX + BANK * (g - 1):CTX + BANK * g],
                             d["xT"][:, :, BANK * (g - 1):BANK * g]).then_inc(sem(f"x{g}"), 16)
            for i in range(1, GADA // 2):
                for n in range(2):
                    sp.wait_ge(sem(f"ada_used{n}"), i)
                    sp.dma_start(adaw[:, n], d["ada"][2 * i + n]).then_inc(sem(f"ada{n}"), 16)

        @block.tensor
        def _(pe):
            pe.wait_ge(sem("consts"), 16)
            for g, (at, n, _) in enumerate(groups):
                pe.wait_ge(sem("squares"), g + 1)
                for k in range(KD):
                    mm = nc.tensor.matmul(ps[g][:, 0:n], t["c_ones"], tmp[:, k, at:at + n],
                                          start=(k == 0), stop=(k == KD - 1))
                mm.then_inc(sem("sumsq"), 1)
            pe.wait_ge(sem("silu_c"), 1)
            for i in range(GADA // 2):
                for s in range(2):
                    pe.wait_ge(sem(f"ada{s}"), 16 * (i + 1))
                    for m in range(NADA):
                        for k in range(KD):
                            mm = nc.tensor.matmul(modps[:, (2 * i + s) * NADA + m, :], adaw[:, s, m, k, :],
                                                  silu_c[:, k, :], start=(k == 0), stop=(k == KD - 1))
                    mm.then_inc(sem(f"ada_used{s}"), 1)

        @block.scalar
        def _(act):
            act.wait_ge(sem("vecs"), 16)
            nc.scalar.activation(silu_c, t["v_cc"].rearrange("p (k c) -> p k c", c=2),
                                 ACT.Silu).then_inc(sem("silu_c"), 1)
            for g, (at, n, _) in enumerate(groups):
                act.wait_ge(sem(f"x{g}"), 16)
                nc.scalar.activation(tmp[:, :, at:at + n], xin[:, :, at:at + n],
                                     ACT.Square).then_inc(sem("squares"), 1)
            act.wait_ge(sem("eps"), 2)
            for g, (at, n, _) in enumerate(groups):
                act.wait_ge(sem("sumsq"), g + 1)
                nc.scalar.activation(rstd[:, at:at + n], ps[g][:, 0:n], ACT.Sqrt, scale=1.0 / D,
                                     bias=t["c_eps"]).then_inc(sem("std"), 1)
            act.wait_ge(sem("gain"), 1)
            for g, (at, n, c) in enumerate(groups):
                act.wait_ge(sem("normed"), g + 1)
                for k in range(KD):
                    a = nc.scalar.activation(tmp[:, k, at:at + n], tmp[:, k, at:at + n], ACT.Identity,
                                             scale=gain[:, c, k:k + 1], bias=t["mod"][:, c, k:k + 1])
                a.then_inc(sem("full"), 1)
                act.wait_ge(sem("full"), g + 1)
                nc.scalar.activation(t["h_hi"][:, :, at:at + n], tmp[:, :, at:at + n],
                                     ACT.Copy).then_inc(sem("hi"), 1)

        @block.vector
        def _(dve):
            nc.vector.memset(t["c_eps"], RMS_EPS).then_inc(sem("eps"), 1)
            nc.vector.memset(t["c_gneps"], GN_EPS).then_inc(sem("eps"), 1)
            for g, (at, n, _) in enumerate(groups):
                dve.wait_ge(sem("std"), g + 1)
                nc.vector.reciprocal(rstd[:, at:at + n], rstd[:, at:at + n]).then_inc(sem("rstd"), 1)
                dve.wait_ge(sem("rstd"), g + 1)
                nc.vector.tensor_tensor(tmp[:, :, at:at + n], xin[:, :, at:at + n], bc(rstd[:, at:at + n], 1, KD),
                                        ALU.mult).then_inc(sem("normed"), 1)
            dve.wait_ge(sem("ada_used1"), GADA // 2)
            for c in range(2):
                nc.vector.tensor_tensor(t["mod"][:, c, 0:16], modps[:, :, c], t["v_ada_b"][:, 0:16],
                                        ALU.add).then_inc(sem("mod"), 1)
            dve.wait_ge(sem("mod"), 2)
            for c in range(2):
                g = nc.vector.scalar_tensor_tensor(out=gain[:, c], in0=t["mod"][:, c, 8:16], scalar=1.0,
                                                   in1=t["v_norm1_g"], op0=ALU.add, op1=ALU.mult)
            g.then_inc(sem("gain"), 1)
            for g, (at, n, _) in enumerate(groups):
                dve.wait_ge(sem("hi"), g + 1)
                nc.vector.tensor_tensor(t["h_lo"][:, :, at:at + n], tmp[:, :, at:at + n],
                                        t["h_hi"][:, :, at:at + n].bitcast(F32), ALU.subtract).then_inc(sem("lo"), 1)


def projections(nc, d, t):
    NADA = 2
    GROUPS = [(0, CTX), (CTX, BANK), (CTX + BANK, BANK)]
    JOBS = [(g, x) for g in range(3) for x in range(2)]
    NJ = len(JOBS)
    FIRST, PER_TURN = 5, 8
    CC, CX, CB = 0, 1, 2
    V, K, R = 0, 1, 2
    ADA_TURN = 2
    with ExitStack() as st:
        sem = Sems(nc, st, "b_")
        sb = lambda n, s, dt=F32: st.enter_context(nc.sbuf_tensor("b_" + n, s, dt))
        raw = sb("raw", [P, KD, P])
        w_hi, w_lo = sb("w_hi", [P, 3, KD, P], F32R), sb("w_lo", [P, 3, KD, P], F32R)
        adaw = sb("adaw", [P, NADA, KD, P])
        wa = sb("wa", [P, TOK])
        lora = sb("lora", [P, 2, P])
        bias = sb("bias", [P, 4])
        ka1 = sb("ka1", [P, PAIRS])
        r, k, v, kk, sq = (sb(n, [P, TOK]) for n in ("r", "k", "v", "kk", "sq"))
        rn = sq
        rkk = sb("rkk", [P, SEQ])
        vt = sb("vt", [P, TOK // P, P])
        th = sb("th", [P, 2, 2, BANK])
        cum = sb("cum", [P, 2, BANK])
        pinv = sb("pinv", [P, 2, BANK])
        kd = sb("kd", [P, 2, BANK])
        ops = sb("ops", [P, 2, 4, BANK])
        gcc, u, y = v[:, 0:SEQ], sq[:, 0:SEQ + 2], r[:, 0:SEQ]
        ps = [st.enter_context(nc.psum_tensor(f"b_ps{n}", [P, BANK], F32)) for n in range(8)]
        PS_HEADS, PS_W, PS_A, PS_ADA = 4, 5, 6, 7
        gate = {n: sem("passed_" + n) for n in ("pe", "sp", "act", "dve", "pool")}
        h_hi, h_lo = t["h_hi"], t["h_lo"]
        conv_w, k_k, r_k, k_a = t["v_conv_a_w"], t["v_k_k"], t["v_r_k"], t["v_k_a"]
        cols = lambda g: slice(GROUPS[g][0], GROUPS[g][0] + GROUPS[g][1])
        seq = lambda g: slice(BANK * (g - 1), BANK * g)
        dense_at = lambda n, j: n * PER_TURN + (FIRST + j)
        bank_of = lambda j: (FIRST + j) % 4
        DENSE = [(V, 0), (V, 1), (V, 2), (K, 0), (K, 1), (K, 2), (R, 1), (R, 2)]
        ALL = FIRST + PAIRS * PER_TURN
        block = st.enter_context(nc.Block())

        tanh_before = lambda m, j: m * NJ + (j + 1)
        made_at = lambda m, j: m * NJ + (j + 3)
        job = lambda m, j: m * NJ + (j + 1)

        @block.sync
        def _(sp):
            def wait(s, value):
                hold(sp, gate["sp"], s, value)

            def load_w(tile):
                wait(sem("lo"), tile)
                sp.dma_start(raw[:], d["w1"][tile]).then_inc(sem("raw"), 16)

            def store_job(m, j):
                g, x = JOBS[j]
                at, n = GROUPS[g]
                s0 = at // C if g or x == 0 else STEPS
                wait(sem("made"), made_at(m, j))
                sp.dma_start(d["ops"][x, :, m, :, s0 * C:s0 * C + n].rearrange("a p c -> p a c"),
                             ops[:, j % 2, :, 0:n]).then_inc(sem(f"ops_stored{j % 2}"), 16)

            def store_bonus(m):
                wait(sem("bonus"), m * 2 + 2)
                sp.dma_start(d["mixd"][:, m + PAIRS], rkk[:]).then_inc(sem("bonus_stored"), 16)

            def store_vt(m):
                wait(sem("vt"), m * 3 + 3)
                for c in range(2):
                    for h in range(2):
                        rows, heads = slice(C * c, C * c + C), slice(HEAD * h, HEAD * h + HEAD)
                        for s0, n in ((0, STEPS), (STEPS, NCTX)):
                            dst = d["vts"][s0:s0 + n, heads, m, :].rearrange("(j c) s v -> c s j v", c=2)[c]
                            sp.dma_start(dst, vt[rows, 0:n // 2, heads]).then_inc(sem("vt_stored"), 16)

            def store_conv(c):
                wait(sem("conv_out"), c * 2 + 2)
                sp.dma_start(d["mixd"][:, c], y).then_inc(sem("conv_stored"), 16)

            def pair_turn(n, jobs):
                m = held(nc.sync, n - 1)
                load_w(n * 3 + 5)
                if jobs:
                    store_bonus(m)
                if jobs:
                    for j in range(4):
                        store_job(m, j)
                load_w(n * 3 + 6)
                if jobs:
                    for j in range(4, NJ):
                        store_job(m, j)
                store_vt(n)
                wait(sem("p_lora"), n * NJ)
                sp.dma_start(lora[:], d["lora"][n]).then_inc(sem("lora"), 16)
                load_w(n * 3 + 7)

            for tile in range(5):
                load_w(tile)
                if tile == 3:
                    sp.wait_ge(sem("sg"), 2)
                    sp.dma_start(d["sgs"], sq[:, 0:SEQ]).then_inc(sem("sg_stored"), 16)
            pair_turn(0, False)
            with nc.sync.Fori(1, PAIRS) as n:
                pair_turn(n, True)
            tile = 2 + 3 * (PAIRS + 1)
            load_w(tile)
            store_bonus(PAIRS - 1)
            for j in range(3):
                store_job(PAIRS - 1, j)
            load_w(tile + 1)
            for j in range(3, NJ):
                store_job(PAIRS - 1, j)
            load_w(tile + 2)
            store_conv(0)
            with nc.sync.Fori(1, 3) as c:
                for i in range(3):
                    load_w(held(nc.sync, c * 3 + (tile + i)))
                store_conv(c)
            store_conv(3)
            sp.wait_ge(sem("sg_stored"), 16)
            for j in range(2):
                sp.wait_ge(sem(f"ops_stored{j}"), 16 + 16 * NJ // 2 * PAIRS)
            sp.wait_ge(sem("vt_stored"), 128 * PAIRS)
            sp.wait_ge(sem("bonus_stored"), 16 * PAIRS)
            sp.wait_ge(sem("conv_stored"), 16 * 4)

        @block.tensor
        def _(pe):
            def wait(s, value):
                hold(pe, gate["pe"], s, value)

            def weights(slot, tile):
                wait(sem("hi"), tile + 1)
                wait(sem("lo"), tile + 1)

            def dense(bank, slot, g, done):
                at, n = GROUPS[g]
                return product(nc, ps[bank][:, 0:n], w_hi[:, slot], w_lo[:, slot], h_hi, h_lo, KD,
                               cols(g)).then_inc(done, 1)

            def modulation(n):
                wait(sem("ada"), n * 16 + 16)
                wait(sem("ada_read"), n)
                for m in range(NADA):
                    for q in range(KD):
                        mm = nc.tensor.matmul(ps[PS_ADA][:, 2 * m:2 * m + 2], adaw[:, m, q, :], t["silu_c"][:, q, :],
                                              start=(q == 0), stop=(q == KD - 1))
                mm.then_inc(sem("ada_used"), 1)

            def low_rank(m, j):
                g, x = JOBS[j]
                n = GROUPS[g][1]
                wait(sem("lora"), m * 16 + 16)
                wait(sem("tanh"), tanh_before(m, j))
                if j == 0:
                    wait(sem("norms_read"), m * 3 + 3)
                    wait(sem("bonus"), m * 2 + 2)
                nc.tensor.matmul(ps[PS_W][:, 0:n], lora[0:C, x], wa[0:C, cols(g)], start=True, stop=True)
                nc.tensor.matmul(ps[PS_A][:, 0:n], lora[C:P, x], wa[C:P, cols(g)], start=True,
                                 stop=True).then_inc(sem("p_lora"), 1)

            def bonus_sums(n):
                wait(sem("rkk"), n + 1)
                for g in range(2):
                    wait(sem("norms_read"), n * 3 + (g + 1))
                    nc.tensor.matmul(ps[PS_HEADS + g][:], t["c_headones"], rkk[:, BANK * g:BANK * (g + 1)], start=True,
                                     stop=True).then_inc(sem("p_bonus"), 1)

            def turn_v(n, g):
                wait(sem("dense_read"), dense_at(n, g + 1))
                wait(sem("bonus"), n * 2)
                wait(sem("vt"), n * 3 + g)
                at, m = GROUPS[g]
                for b in range(m // P):
                    mm = nc.tensor.transpose(ps[PS_HEADS][:, P * b:P * (b + 1)], v[:, at + P * b:at + P * (b + 1)],
                                             t["c_ident"])
                mm.then_inc(sem("p_vt"), 1)

            def norm_sums(n):
                wait(sem("sq"), n + 1)
                wait(sem("vt"), n * 3 + 3)
                wait(sem("tanh"), tanh_before(n, 0))
                for g, (at, m) in enumerate(GROUPS):
                    nc.tensor.matmul(ps[PS_HEADS + g][:, 0:m], t["c_headones"], sq[:, cols(g)], start=True,
                                     stop=True).then_inc(sem("p_norms"), 1)

            def pair_turn(n, jobs):
                m = held(nc.tensor, n - 1)
                for j, (slot, g) in enumerate(DENSE):
                    weights(slot, n * 3 + (2 + slot))
                    wait(sem("dense_read"), dense_at(n, j - 3))
                    dense(bank_of(j), slot, g, sem("dense"))
                    if jobs and j < NJ:
                        low_rank(m, j)
                    if j in (3, 7):
                        modulation(n * ADA_TURN + j // 4)
                    if 3 <= j < 6:
                        turn_v(n, j - 3)
                norm_sums(n)
                bonus_sums(n)

            def conv_turn(c, jobs):
                for slot, g, banks, read in ((CC, 1, 0, "cc_read"), (CC, 2, 1, "cc_read"), (CX, 1, 2, "cx_read"),
                                             (CX, 2, 3, "cx_read"), (CB, 1, PS_HEADS, "conv_out"), (CB, 2, PS_HEADS, "conv_out")):
                    if jobs:
                        low_rank(PAIRS - 1, 2 * slot + g - 1)
                    weights(slot, c * 3 + (2 + 3 * PAIRS + slot))
                    wait(sem(read), c * 2 - (1 - g if slot == CB else 2 - g))
                    dense(banks, slot, g, sem(("p_cc", "p_cx", "p_cb")[slot]))
                    if jobs and (slot, g) == (CX, 2):
                        wait(sem("bonus"), PAIRS * 2)
                    if g == 2 and slot != CX:
                        modulation((c + PAIRS) * ADA_TURN + slot // 2)

            for j, (slot, g) in enumerate(((0, 0), (0, 1), (0, 2), (1, 1), (1, 2))):
                weights(slot, slot)
                wait(sem("dense_read"), j - 3)
                dense(j % 4, slot, g, sem("dense"))
            pe.wait_ge(sem("wa"), 4)
            pair_turn(0, False)
            with nc.tensor.Fori(1, PAIRS) as n:
                pair_turn(n, True)
            pe.wait_ge(sem("dense_read"), ALL)
            conv_turn(0, True)
            with nc.tensor.Fori(1, 4) as c:
                conv_turn(c, False)

        @block.scalar
        def _(act):
            def wait(s, value):
                hold(act, gate["act"], s, value)

            def hi(slot, tile):
                wait(sem("raw"), tile * 16 + 16)
                nc.scalar.activation(w_hi[:, slot], raw[:], ACT.Copy).then_inc(sem("hi"), 1)

            def read(n, j):
                slot, g = DENSE[j]
                wait(sem("dense"), dense_at(n, j + 1))
                nc.scalar.activation((v, k, r)[slot][:, cols(g)], ps[bank_of(j)][:, 0:GROUPS[g][1]],
                                     ACT.Copy).then_inc(sem("dense_read"), 1)

            def read_vt(n, g):
                at, m = GROUPS[g]
                wait(sem("p_vt"), n * 3 + (g + 1))
                nc.scalar.activation(vt[:, at // P:(at + m) // P].rearrange("p j c -> p (j c)"), ps[PS_HEADS][:, 0:m],
                                     ACT.Copy).then_inc(sem("vt"), 1)

            def tanhs(m, j):
                g, x = JOBS[j]
                n = GROUPS[g][1]
                wait(sem("p_lora"), job(m, j))
                wait(sem("bias"), m + 1)
                wait(sem("made"), made_at(m, j - 2))
                for w, bank in ((0, PS_W), (1, PS_A)):
                    a = nc.scalar.activation(th[:, j % 2, w, 0:n], ps[bank][:, 0:n], ACT.Tanh, scale=0.5,
                                             bias=bias[:, 2 * x + w:2 * x + w + 1])
                a.then_inc(sem("tanh"), 1)

            def powers(m, j):
                g, x = JOBS[j]
                s, n = j % 2, GROUPS[g][1]
                wait(sem("cum"), job(m, j))
                nc.scalar.activation(pinv[:, s, 0:n], cum[:, s, 0:n], ACT.Exp, scale=DECAY_SCALE)
                wait(sem("cex"), job(m, j))
                nc.scalar.activation(cum[:, s, 0:n], cum[:, s, 0:n], ACT.Exp, scale=-DECAY_SCALE)
                nc.scalar.activation(th[:, s, 0, 0:n], th[:, s, 0, 0:n], ACT.Exp, scale=-DECAY_SCALE).then_inc(sem("powers"), 1)

            def load_ada(n):
                wait(sem("ada_used"), n)
                nc.scalar.dma_start(adaw[:], d["ada"][held(nc.scalar, n + 8)]).then_inc(sem("ada"), 16)

            def pair_turn(n, jobs):
                m = held(nc.scalar, n - 1)
                if jobs:
                    tanhs(m, 0)
                for j in range(6):
                    if j == 0 and jobs:
                        wait(sem("bonus"), n * 2)
                    if j == 0:
                        wait(sem("vt_stored"), n * 128)
                    if j == NJ - 1 and jobs:
                        powers(m, j)
                    if j >= 3 and jobs:
                        wait(sem("made"), made_at(m, 2 * j - 5))
                    read(n, j)
                    if j in (4, 5):
                        read_vt(n, j - 4)
                    if jobs and j + 1 < NJ:
                        tanhs(m, j + 1)
                        powers(m, j)
                    if j == 2:
                        hi(V, n * 3 + 5)
                    if j == 4:
                        load_ada(n * ADA_TURN + 1)
                hi(K, n * 3 + 6)
                read_vt(n, 2)
                for j in (6, 7):
                    read(n, j)
                hi(R, n * 3 + 7)
                wait(sem("norms_read"), n * 3 + 3)
                nc.scalar.activation(rn[:], rn[:], ACT.Sqrt).then_inc(sem("norm"), 1)
                load_ada(n * ADA_TURN + 2)

            def conv_turn(c, last):
                wait(sem("cx_read"), c * 2)
                for g in (1, 2):
                    wait(sem("p_cc"), c * 2 + g)
                    nc.scalar.activation(gcc[:, seq(g)], ps[g - 1][:], ACT.Copy).then_inc(sem("cc_read"), 1)
                for slot, done in () if last == "alone" else ((CC, "p_cc"), (CX, "p_cx"), (CB, "p_cb")):
                    wait(sem(done), c * 2 + 2)
                    if slot == CX:
                        load_ada((c + PAIRS) * ADA_TURN + 1)
                    if not last:
                        hi(slot, c * 3 + (5 + 3 * PAIRS + slot))
                if not last:
                    load_ada((c + PAIRS) * ADA_TURN + 2)

            act.sem_inc(sem("tanh"), 1)
            load_ada(0)
            for tile in range(2):
                hi(tile, tile)
            for g, (at, n) in enumerate(GROUPS):
                act.wait_ge(sem("dense"), g + 1)
                nc.scalar.activation(wa[0:C, cols(g)], ps[g][0:C, 0:n], ACT.Tanh)
                nc.scalar.activation(wa[C:P, cols(g)], ps[g][C:P, 0:n], ACT.Copy).then_inc(sem("dense_read"), 1)
            act.sem_inc(sem("wa"), 1)
            hi(V, 2)
            for g, bank in ((1, 3), (2, 0)):
                act.wait_ge(sem("dense"), 3 + g)
                nc.scalar.activation(sq[:, seq(g)], ps[bank][:], ACT.Sigmoid).then_inc(sem("dense_read"), 1)
            act.wait_ge(sem("dense_read"), FIRST)
            act.sem_inc(sem("sg"), 2)
            act.sem_inc(sem("wa"), 3)
            hi(K, 3)
            hi(R, 4)
            pair_turn(0, False)
            with nc.scalar.Fori(1, PAIRS) as n:
                pair_turn(n, True)
            m = PAIRS - 1
            tanhs(m, 0)
            tanhs(m, 1)
            powers(m, 0)
            tanhs(m, 2)
            powers(m, 1)
            act.wait_ge(sem("bonus"), 2 * PAIRS)
            act.wait_ge(sem("vt_stored"), 128 * PAIRS)
            for j in range(2, NJ):
                if j + 1 < NJ:
                    tanhs(m, j + 1)
                powers(m, j)
                if j == 3:
                    conv_turn(0, "alone")
            for slot, done in ((CC, "p_cc"), (CX, "p_cx"), (CB, "p_cb")):
                act.wait_ge(sem(done), 2)
                if slot == CX:
                    load_ada(PAIRS * ADA_TURN + 1)
                hi(slot, 5 + 3 * PAIRS + slot)
            load_ada(PAIRS * ADA_TURN + 2)
            with nc.scalar.Fori(1, 3) as c:
                conv_turn(c, False)
            conv_turn(3, True)

        @block.gpsimd
        def _(pool):
            TT, TS = nc.gpsimd.tensor_tensor, nc.gpsimd.tensor_scalar

            def wait(s, value):
                hold(pool, gate["pool"], s, value)

            def lo(slot, tile):
                wait(sem("hi"), tile + 1)
                TT(w_lo[:, slot], raw[:], w_hi[:, slot].bitcast(F32), ALU.subtract).then_inc(sem("lo"), 1)

            def sigmoids(m, j):
                s, n = j % 2, GROUPS[JOBS[j][0]][1]
                wait(sem("tanh"), tanh_before(m, j + 1))
                TS(th[:, s, :, 0:n], th[:, s, :, 0:n], 0.5, 0.5, ALU.mult, ALU.add).then_inc(sem("sig"), 1)

            def parts(m, j):
                g, x = JOBS[j]
                s, (at, n) = j % 2, GROUPS[g]
                wait(sem("kk"), m + 1)
                wait(sem("km"), job(m, j))
                TT(th[:, s, 1, 0:n], th[:, s, 1, 0:n], kk[:, cols(g)], ALU.mult).then_inc(sem("b"), 1)
                wait(sem("cum"), job(m, j))
                TT(th[:, s, 0, 0:n], cum[:, s, 0:n], th[:, s, 0, 0:n], ALU.subtract).then_inc(sem("cex"), 1)

            def jobs_of(m, splits):
                sigmoids(m, 0)
                for j in range(NJ):
                    if j + 1 < NJ:
                        sigmoids(m, j + 1)
                    parts(m, j)
                    if j in splits:
                        lo(*splits[j])

            for slot, tile in ((0, 0), (1, 1), (V, 2), (K, 3), (R, 4), (V, 5), (K, 6), (R, 7)):
                lo(slot, tile)
            with nc.gpsimd.Fori(1, PAIRS) as n:
                jobs_of(nc.gpsimd.snap(n - 1), {3: (V, n * 3 + 5)})
                lo(K, n * 3 + 6)
                lo(R, n * 3 + 7)
            jobs_of(PAIRS - 1, {})
            with nc.gpsimd.Fori(0, 3) as c:
                for slot in range(3):
                    lo(slot, c * 3 + (5 + 3 * PAIRS + slot))

        @block.vector
        def _(dve):
            TT, TS, STT = nc.vector.tensor_tensor, nc.vector.tensor_scalar, nc.vector.scalar_tensor_tensor

            def wait(s, value):
                hold(dve, gate["dve"], s, value)

            def modulation(n):
                wait(sem("ada_used"), n + 1)
                at = held(nc.vector, n * NADA + 16)
                TT(t["mod"][:, 0, bass.ds(at, NADA)], ps[PS_ADA][:, 0:2 * NADA].rearrange("p (n c) -> p n c", c=2)[:, :, 0],
                   t["v_ada_b"][:, bass.ds(at, NADA)], ALU.add).then_inc(sem("ada_read"), 1)

            def biases(m):
                wait(sem("tanh"), tanh_before(m, 0))
                TS(bias[:].unsqueeze(2), t["v_w0a0"].rearrange("p (w q) -> p w q", q=PAIRS)[:, :, bass.ds(m, 1)], 0.5, None,
                   ALU.mult).then_inc(sem("bias"), 1)

            def bonus(m):
                for g in (1, 2):
                    wait(sem("p_bonus"), m * 2 + g)
                    TT(rkk[:, seq(g)], ps[PS_HEADS + g - 1][:], v[:, cols(g)], ALU.mult).then_inc(sem("bonus"), 1)

            def sums(m, j):
                g, x = JOBS[j]
                s, n = j % 2, GROUPS[g][1]
                wait(sem("sig"), job(m, j))
                TS(kd[:, s, 0:n], th[:, s, 1, 0:n], k_a[:, bass.ds(m, 1)], ka1[:, bass.ds(m, 1)], ALU.mult,
                   ALU.add).then_inc(sem("km"), 1)
                flat = [cum[:, s, 0:n], t["c_reset"][:, x, 0:n], th[:, s, 0, 0:n]]
                out, reset, data = flat if x == 0 else [a[:, ::-1] for a in flat]
                nc.vector.tensor_tensor_scan(out, reset, data, 0.0, ALU.mult, ALU.add).then_inc(sem("cum"), 1)

            def products(m, j):
                g, x = JOBS[j]
                s, (at, n) = j % 2, GROUPS[g]
                wait(sem("km"), job(m, j))
                TT(kd[:, s, 0:n], kd[:, s, 0:n], k[:, cols(g)], ALU.mult).then_inc(sem("kd"), 1)
                wait(sem(f"ops_stored{j % 2}"), (m * (NJ // 2) + (j // 2 + 1)) * 16)
                wait(sem("powers"), job(m, j))
                s0 = at // C if g or x == 0 else STEPS
                TS(t["pend"][:, x, s0:s0 + n // C, bass.ds(m, 1)], cum[:, s, (C - 1, 0)[x]:n:C].unsqueeze(2), 1.0, None, ALU.mult)
                TT(ops[:, s, 0, 0:n], r[:, cols(g)], cum[:, s, 0:n], ALU.mult)
                TT(ops[:, s, 1, 0:n], kk[:, cols(g)], th[:, s, 0, 0:n], ALU.mult)
                wait(sem("b"), job(m, j))
                TT(ops[:, s, 2, 0:n], th[:, s, 1, 0:n], pinv[:, s, 0:n], ALU.mult)
                wait(sem("kd"), job(m, j))
                TT(ops[:, s, 3, 0:n], kd[:, s, 0:n], pinv[:, s, 0:n], ALU.mult).then_inc(sem("made"), 1)

            def norms(n):
                wait(sem("dense_read"), dense_at(n, 6))
                wait(sem("b"), n * NJ)
                TS(kk[:], k[:], k_k[:, bass.ds(n, 1)], None, ALU.mult).then_inc(sem("kk_raw"), 1)
                wait(sem("kk_raw"), n + 1)
                TT(sq[:], kk[:], kk[:], ALU.mult).then_inc(sem("sq"), 1)
                wait(sem("dense_read"), dense_at(n, 8))
                wait(sem("bonus_stored"), n * 16)
                STT(out=rkk[:], in0=r[:, CTX:TOK], scalar=r_k[:, bass.ds(n, 1)], in1=k[:, CTX:TOK], op0=ALU.mult,
                    op1=ALU.mult).then_inc(sem("rkk"), 1)
                for g, (at, m) in enumerate(GROUPS):
                    wait(sem("p_norms"), n * 3 + (g + 1))
                    TS(rn[:, cols(g)], ps[PS_HEADS + g][:, 0:m], 1e-24, None, ALU.max).then_inc(sem("norms_read"), 1)
                bonus(n)
                wait(sem("norm"), n + 1)
                nc.vector.reciprocal(rn[:], rn[:]).then_inc(sem("rnorm"), 1)
                wait(sem("rnorm"), n + 1)
                TT(kk[:], kk[:], rn[:], ALU.mult).then_inc(sem("kk"), 1)

            def jobs_of(m, n):
                biases(m)
                wait(sem("kk"), m + 1)
                sums(m, 0)
                for j in range(NJ):
                    if j + 1 < NJ:
                        sums(m, j + 1)
                    products(m, j)
                    if n is not None and j == 3:
                        modulation(n * ADA_TURN)

            def conv_turn(c):
                wait(sem("conv"), c * 3)
                for g in (1, 2):
                    wait(sem("cc_read"), c * 2 + g)
                    wait(sem("p_cx"), c * 2 + g)
                    TT(u[:, 1 + BANK * (g - 1):1 + BANK * g], ps[1 + g][:], gcc[:, seq(g)], ALU.mult).then_inc(sem("cx_read"), 1)
                wait(sem("cx_read"), c * 2 + 2)
                wait(sem("conv_stored"), c * 16)
                for tap in range(3):
                    wait(sem("conv"), c * 3 + tap)
                    w = conv_w[:, bass.ds(c + 4 * tap, 1)]
                    if tap == 0:
                        a = TS(y, u[:, 0:SEQ], w, None, ALU.mult)
                    else:
                        a = STT(out=y, in0=u[:, tap:tap + SEQ], scalar=w, in1=y, op0=ALU.mult, op1=ALU.add)
                    a.then_inc(sem("conv"), 1)
                wait(sem("conv"), c * 3 + 3)
                modulation((c + PAIRS) * ADA_TURN)
                for g in (1, 2):
                    wait(sem("p_cb"), c * 2 + g)
                    TT(y[:, seq(g)], ps[PS_HEADS][:], y[:, seq(g)], ALU.mult).then_inc(sem("conv_out"), 1)
                modulation((c + PAIRS) * ADA_TURN + 1)

            dve.sem_inc(sem("made"), 2)
            for j in range(2):
                dve.sem_inc(sem(f"ops_stored{j}"), 16)
            TS(ka1[:], k_a, -1.0, 1.0, ALU.mult, ALU.add).then_inc(sem("ka1"), 1)
            nc.vector.memset(r[:, 0:CTX], 0.0).then_inc(sem("ka1"), 1)
            dve.wait_ge(sem("ka1"), 2)
            modulation(0)
            dve.wait_ge(sem("sg_stored"), 16)
            norms(0)
            modulation(1)
            with nc.vector.Fori(1, PAIRS) as n:
                jobs_of(nc.vector.snap(n - 1), n)
                norms(n)
                modulation(n * ADA_TURN + 1)
            jobs_of(PAIRS - 1, None)
            nc.vector.memset(u[:, 0:1], 0.0)
            nc.vector.memset(u[:, SEQ + 1:SEQ + 2], 0.0).then_inc(sem("u0"), 1)
            dve.wait_ge(sem("u0"), 1)
            conv_turn(0)
            with nc.vector.Fori(1, 4) as c:
                conv_turn(c)


def scan(nc, d, t):
    DIRS, HEADS = range(2), range(2)
    ROWS = [slice(HEAD * h, HEAD * h + HEAD) for h in HEADS]
    LOADS = 6 * 16
    with ExitStack() as st:
        sem = Sems(nc, st, "c_")
        sb = lambda n, s, dt=F32: st.enter_context(nc.sbuf_tensor("c_" + n, s, dt))
        two = lambda n, s: [sb(f"{n}{x}", s) for x in DIRS]
        four = lambda n, s: [[sb(f"{n}{x}{par}", s) for par in range(2)] for x in DIRS]
        rk = four("rk", [P, 2, PAIRS, C])
        kbk = four("kbk", [P, 3, PAIRS, 2, C])
        vc = four("vc", [P, PAIRS, C])
        vd = four("vd", [P, PAIRS, 2, C])
        bk = four("bk", [P, 2, PAIRS, 2, C])
        lr = four("lr", [P, PAIRS, C])
        mr = four("mr", [P, PAIRS, C])
        md = four("md", [P, PAIRS, 2, C])
        uend = four("uend", [P, PAIRS, 2, C])
        ld = two("ld", [P, PAIRS, 2, C])
        tt = two("tt", [P, PAIRS, C])
        uu = two("uu", [P, PAIRS, C])
        ud = two("ud", [P, PAIRS, 2, C])
        yl = two("yl", [P, PAIRS, C])
        yd = two("yd", [P, PAIRS, 2, C])
        gg = two("gg", [P, PAIRS, C])
        zc = two("zc", [P, PAIRS, C])
        zd = two("zd", [P, PAIRS, 2, C])
        s1 = two("s1", [P, PAIRS, C])
        sc = two("sc", [P, PAIRS, C])
        sd = two("sd", [P, PAIRS, 2, C])
        yo = four("yo", [P, PAIRS, C])
        bank = [[st.enter_context(nc.psum_tensor(f"c_ps{x}{n}", [P, BANK], F32)) for n in range(4)] for x in DIRS]
        gate = {n: sem("passed_" + n) for n in ("pe", "sp", "act", "dve", "pool")}
        S = lambda name, x: sem(f"{name}{x}")
        half = lambda ap, w=0: ap[:, PAIRS * C * w:PAIRS * C * (w + 1)].rearrange("p (q c) -> p q c", q=PAIRS)
        quad = lambda ap: ap.rearrange("p (q w c) -> p q w c", q=PAIRS, w=2)
        whole = lambda ap: ap.rearrange("p (q c) -> p q c", q=PAIRS)
        flat = lambda ap: ap.rearrange("p q h c -> p q (h c)")
        slot_of = lambda x, s: (s + 0, SLOTS - 1 - s)[x]
        LEVEL = lambda u, lev: u * LEVELS + (lev + 1)
        block = st.enter_context(nc.Block())

        def steps(eng, inverse, both, chain):
            inverse(0, 0, 0)
            both(0, 0, 0, 0)
            both(1, 1, 0, 1)
            with eng.Fori(1, STEPS // 2 - 1) as j:
                both(eng.snap(j * 2), 0, j, j)
                both(eng.snap(j * 2 + 1), 1, j, eng.snap(j + 1))
            both(STEPS - 2, 0, STEPS // 2 - 1, STEPS // 2 - 1)
            chain(STEPS - 1, 1, STEPS // 2 - 1)

        @block.sync
        def _(sp):
            def load(x, slot, par):
                ld_ = S(f"loaded{par}_", x)
                at = bass.ds(slot * C, C)
                part = lambda a0, a1, rows: d["ops"][x, a0:a1, :, rows, at].rearrange("a q p c -> p (a q) c")
                sp.dma_start(rk[x][par][:].rearrange("p a q c -> p (a q) c"), part(0, 2, slice(0, P))).then_inc(ld_, 16)
                sp.dma_start(vc[x][par][:], d["vts"][slot]).then_inc(ld_, 16)
                for h, rows in enumerate(ROWS):
                    sp.dma_start(kbk[x][par][rows, :, :, h].rearrange("p a q c -> p (a q) c"),
                                 part(1, 4, rows)).then_inc(ld_, 16)
                    sp.dma_start(vd[x][par][rows, :, h], d["vts"][slot, rows]).then_inc(ld_, 16)

            def step(s, par, more):
                for x in DIRS:
                    if more:
                        hold(sp, gate["sp"], S("p_y", x), s + 1)
                        load(x, held(nc.sync, slot_of(x, s + 2)), par)
                for x in DIRS:
                    hold(sp, gate["sp"], S("yo", x), s + 1)
                    sp.dma_start(d["ys"][x, held(nc.sync, slot_of(x, s))], yo[x][par][:]).then_inc(S(f"stored{par}_", x), 16)

            sp.wait_ge(sem("zeros"), 4)
            for par in range(2):
                for x in DIRS:
                    load(x, slot_of(x, par), par)
            step(0, 0, True)
            step(1, 1, True)
            with nc.sync.Fori(1, STEPS // 2 - 1) as j:
                step(nc.sync.snap(j * 2), 0, True)
                step(nc.sync.snap(j * 2 + 1), 1, True)
            step(STEPS - 2, 0, False)
            step(STEPS - 1, 1, False)
            for x in DIRS:
                for par in range(2):
                    sp.wait_ge(S(f"stored{par}_", x), 16 * STEPS // 2)

        @block.tensor
        def _(pe):
            def heads(out, *pairs):
                for q in range(PAIRS):
                    for n, (still, moving) in enumerate(pairs):
                        last = nc.tensor.matmul(out[:, q], still[:, q].rearrange("p h c -> p (h c)"), moving(q),
                                                start=(n == 0), stop=(n == len(pairs) - 1))
                return last

            at = lambda buf: (lambda q: buf[:, q])
            identc = lambda q: t["c_identc"]

            def wait(name, x, value):
                hold(pe, gate["pe"], S(name, x), value)

            def token_major(x, u, par, u2, a):
                wait(f"loaded{par}_", x, u2 * LOADS + LOADS)
                wait(("yl", "t")[a], x, u * (LEVELS, LEVELS - 1)[a])
                for q in range(PAIRS):
                    mm = nc.tensor.transpose(bank[x][a][:, P * q:P * (q + 1)],
                                             kbk[x][par][:, 1 + a, q].rearrange("p h c -> p (h c)"), t["c_ident"])
                mm.then_inc(S(("p_bet", "p_khat")[a], x), 1)

            def triangles(x, u, par, a):
                wait(("bet", "khat")[a], x, u + 1)
                heads(quad(bank[x][a]), (kbk[x][par][:, 1 + a], lambda q: rk[x][par][:, :, q])).then_inc(S(("p_l", "p_m")[a], x), 1)

            def first_t(x, u):
                wait("ud", x, u * (LEVELS - 1) + 1)
                wait("lr", x, u + 1)
                heads(half(bank[x][0]), (ud[x], identc)).then_inc(S("p_t0", x), 1)

            def level_y(x, u, lev):
                if lev == 0:
                    wait("t0", x, u + 1)
                else:
                    wait("t", x, u * (LEVELS - 1) + lev)
                heads(half(bank[x][0]), (ld[x], at(tt[x]))).then_inc(S("p_yl", x), 1)

            def level_t(x, u, lev):
                wait("yl", x, LEVEL(u, lev))
                if lev == 0:
                    wait("mr", x, u + 1)
                wait("ud", x, u * (LEVELS - 1) + (lev + 1))
                heads(half(bank[x][1]), (ud[x], at(yl[x]))).then_inc(S("p_t", x), 1)

            def level_u(x, u, lev):
                wait("yd", x, LEVEL(u, lev))
                if lev == 0:
                    wait("uend", x, u)
                heads(half(bank[x][3]), (yd[x], at(uu[x]))).then_inc(S("p_u", x), 1)

            def chain_g(x, s, par):
                wait("mr", x, s + 1)
                wait("sc", x, s + 1)
                wait("yo", x, s)
                heads(half(bank[x][2]), (md[x][par], at(vc[x][par])), (kbk[x][par][:, 0], at(sc[x]))).then_inc(S("p_g", x), 1)

            def chain_z(x, s, par):
                wait("uend", x, s + 1)
                wait("gg", x, s + 1)
                heads(half(bank[x][2], 1), (uend[x][par], at(gg[x]))).then_inc(S("p_z", x), 1)

            def chain_s(x, s, par):
                wait("zc", x, s + 1)
                heads(half(bank[x][2]), (bk[x][par][:, 1], at(vc[x][par])), (bk[x][par][:, 0], at(zc[x]))).then_inc(S("p_s", x), 1)

            def chain_y(x, s, par):
                wait("s1", x, s + 1)
                wait("zd", x, s + 1)
                wait("sd", x, s + 1)
                heads(half(bank[x][2], 1), (sd[x], lambda q: rk[x][par][:, 0, q]), (vd[x][par], at(mr[x][par])),
                      (zd[x], at(lr[x][par]))).then_inc(S("p_y", x), 1)

            def levels(u, y):
                for lev in range(LEVELS):
                    for x in DIRS:
                        level_y(x, u, lev)
                    for x in DIRS:
                        if lev < LEVELS - 1:
                            level_t(x, u, lev)
                        if lev == 0:
                            y(x)
                    for x in DIRS:
                        level_u(x, u, lev)

            def inverse(u, par, u2):
                for part in (token_major, triangles):
                    for a in range(2):
                        for x in DIRS:
                            part(x, u, par, *((u2,) if part is token_major else ()), a)
                for x in DIRS:
                    first_t(x, u)
                levels(u, lambda x: None)

            def both(s, par, s2, u2):
                u, other = held(nc.tensor, s + 1), 1 - par
                for a in range(2):
                    for x in DIRS:
                        token_major(x, u, other, u2, a)
                for x in DIRS:
                    chain_g(x, s, par)
                for x in DIRS:
                    triangles(x, u, other, 0)
                for x in DIRS:
                    chain_z(x, s, par)
                for x in DIRS:
                    triangles(x, u, other, 1)
                for x in DIRS:
                    first_t(x, u)
                for x in DIRS:
                    chain_s(x, s, par)
                levels(u, lambda x: chain_y(x, s, par))

            def chain(s, par, s2):
                for part in (chain_g, chain_z, chain_s, chain_y):
                    for x in DIRS:
                        part(x, s, par)

            steps(nc.tensor, inverse, both, chain)

        @block.scalar
        def _(act):
            def wait(name, x, value):
                hold(act, gate["act"], S(name, x), value)

            def copy(out, src, scale=1.0):
                return nc.scalar.activation(out, src, ACT.Copy, scale=scale)

            def token_major(u, par):
                for a, name in ((0, "bet"), (1, "khat")):
                    for x in DIRS:
                        wait("p_" + name, x, u + 1)
                        copy(flat(bk[x][par][:, a]), whole(bank[x][a])).then_inc(S(name, x), 1)

            def first_t(x, u):
                wait("p_t0", x, u + 1)
                copy(tt[x][:], half(bank[x][0])).then_inc(S("t0", x), 1)

            def diag(out, src, name, x):
                for h, rows in enumerate(ROWS):
                    a = copy(out[rows, :, h], src[rows])
                a.then_inc(S(name, x), 1)

            def first_u(x, u):
                wait("u0", x, u + 1)
                diag(ud[x], uu[x], "ud", x)

            def level(u, lev):
                for x in DIRS:
                    wait("yl", x, LEVEL(u, lev))
                    diag(yd[x], yl[x], "yd", x)
                if lev < LEVELS - 2:
                    for x in DIRS:
                        wait("u", x, u * (LEVELS - 1) + (lev + 1))
                        diag(ud[x], uu[x], "ud", x)

            def chain_g(x, s):
                wait("p_g", x, s + 1)
                copy(gg[x][:], half(bank[x][2])).then_inc(S("gg", x), 1)

            def chain_z(x, s):
                wait("p_z", x, s + 1)
                copy(zc[x][:], half(bank[x][2], 1), -1.0).then_inc(S("zc", x), 1)

            def chain_zd(x, s):
                wait("zc", x, s + 1)
                diag(zd[x], zc[x], "zd", x)

            def chain_y(x, s, par, s2):
                wait("p_y", x, s + 1)
                wait(f"stored{par}_", x, s2 * 16)
                copy(yo[x][par][:], half(bank[x][2], 1)).then_inc(S("yo", x), 1)

            def inverse(u, par, u2):
                token_major(u, par)
                for x in DIRS:
                    first_u(x, u)
                for x in DIRS:
                    first_t(x, u)
                for lev in range(LEVELS):
                    level(u, lev)

            def both(s, par, s2, u2):
                u = held(nc.scalar, s + 1)
                token_major(u, 1 - par)
                for x in DIRS:
                    chain_g(x, s)
                for x in DIRS:
                    first_u(x, u)
                for x in DIRS:
                    chain_z(x, s)
                for x in DIRS:
                    first_t(x, u)
                for x in DIRS:
                    chain_zd(x, s)
                for lev in range(LEVELS):
                    level(u, lev)
                    if lev == 0:
                        for x in DIRS:
                            chain_y(x, s, par, s2)

            def chain(s, par, s2):
                for x in DIRS:
                    chain_g(x, s)
                for x in DIRS:
                    chain_z(x, s)
                for x in DIRS:
                    chain_zd(x, s)
                for x in DIRS:
                    chain_y(x, s, par, s2)

            for x in DIRS:
                wait("sd", x, 1)
            steps(nc.scalar, inverse, both, chain)

        @block.vector
        def _(dve):
            TT = nc.vector.tensor_tensor

            def wait(name, x, value):
                hold(dve, gate["dve"], S(name, x), value)

            strict, incl = t["c_strict"], t["c_incl"]

            def triangles_l(x, u, par):
                wait("p_l", x, u + 1)
                wait("uend", x, u)
                b = quad(bank[x][0])
                TT(uu[x][:], b[:, :, 1], bc(t["c_mask_u1"][:, x], 1, PAIRS), ALU.mult).then_inc(S("u_raw", x), 1)
                wait("u_raw", x, u + 1)
                TT(uu[x][:], uu[x][:], bc(t["c_identc"], 1, PAIRS), ALU.add).then_inc(S("u0", x), 1)
                TT(ld[x][:], bc(b[:, :, 1], 2, 2), bc(strict[:, x], 1, PAIRS), ALU.mult)
                TT(lr[x][par][:], b[:, :, 0], bc(incl[:, x], 1, PAIRS), ALU.mult).then_inc(S("lr", x), 1)

            def triangles_m(x, u, par):
                wait("p_m", x, u + 1)
                b = quad(bank[x][1])
                TT(md[x][par][:], bc(b[:, :, 1], 2, 2), bc(strict[:, x], 1, PAIRS), ALU.mult)
                TT(mr[x][par][:], b[:, :, 0], bc(incl[:, x], 1, PAIRS), ALU.mult).then_inc(S("mr", x), 1)

            def level_yl(x, u, lev):
                wait("p_yl", x, LEVEL(u, lev))
                TT(yl[x][:], half(bank[x][0]), bc(t["c_mask_lev"][:, x, lev], 1, PAIRS), ALU.mult).then_inc(S("yl", x), 1)

            def level_t(x, u, lev):
                wait("p_t", x, u * (LEVELS - 1) + (lev + 1))
                TT(tt[x][:], tt[x][:], half(bank[x][1]), ALU.subtract).then_inc(S("t", x), 1)

            def level_u(x, u, par, lev):
                wait("p_u", x, LEVEL(u, lev))
                if lev < LEVELS - 1:
                    TT(uu[x][:], uu[x][:], half(bank[x][3]), ALU.subtract).then_inc(S("u", x), 1)
                else:
                    for h, rows in enumerate(ROWS):
                        a = TT(uend[x][par][rows, :, h], uu[x][rows], half(bank[x][3])[rows], ALU.subtract)
                    a.then_inc(S("uend", x), 1)

            def levels(u, par):
                for lev in range(LEVELS):
                    for x in DIRS:
                        level_yl(x, u, lev)
                    if lev < LEVELS - 1:
                        for x in DIRS:
                            level_t(x, u, lev)
                    for x in DIRS:
                        level_u(x, u, par, lev)

            def chain_s(x, s):
                wait("p_s", x, s + 1)
                wait("sd", x, s + 1)
                TT(s1[x][:], sc[x][:], half(bank[x][2]), ALU.add).then_inc(S("s1", x), 1)
                wait("s1", x, s + 1)
                end = t["pend"][:, x, bass.ds(held(nc.vector, slot_of(x, s)), 1)].rearrange("p o q -> p (o q)")
                TT(sc[x][:], s1[x][:], bc(end, 2, C), ALU.mult).then_inc(S("sc", x), 1)

            def inverse(u, par, u2):
                for part in (triangles_l, triangles_m):
                    for x in DIRS:
                        part(x, u, par)
                levels(u, par)

            def both(s, par, s2, u2):
                u, other = held(nc.vector, s + 1), 1 - par
                for part in (triangles_l, triangles_m):
                    for x in DIRS:
                        part(x, u, other)
                for x in DIRS:
                    chain_s(x, s)
                levels(u, other)

            def chain(s, par, s2):
                for x in DIRS:
                    chain_s(x, s)

            for x in DIRS:
                for par in range(2):
                    nc.vector.memset(kbk[x][par][:], 0.0)
                    nc.vector.memset(vd[x][par][:], 0.0).then_inc(sem("zeros"), 1)
            for x in DIRS:
                for par in range(2):
                    nc.vector.memset(uend[x][par][:], 0.0)
                nc.vector.memset(sc[x][:], 0.0).then_inc(S("sc", x), 1)
            steps(nc.vector, inverse, both, chain)

        @block.gpsimd
        def _(pool):
            TS = nc.gpsimd.tensor_scalar

            def wait(name, x, value):
                hold(pool, gate["pool"], S(name, x), value)

            def state(s, par, s2, u2):
                for x in DIRS:
                    wait("sc", x, s + 2)
                    wait("p_y", x, s + 1)
                    for h in HEADS:
                        a = TS(sd[x][:, :, h], sc[x][:], t["c_headones"][:, HEAD * h:HEAD * h + 1], None, ALU.mult)
                    a.then_inc(S("sd", x), 1)

            for x in DIRS:
                nc.gpsimd.memset(ud[x][:], 0.0)
                nc.gpsimd.memset(yd[x][:], 0.0)
                nc.gpsimd.memset(zd[x][:], 0.0)
                nc.gpsimd.memset(sd[x][:], 0.0).then_inc(S("sd", x), 1)
            steps(nc.gpsimd, lambda u, par, u2: None, state, lambda s, par, s2: None)


def mixer_out(nc, d, t):
    G = range(2)
    cols = lambda g: slice(BANK * g, BANK * (g + 1))
    with ExitStack() as st:
        sem = Sems(nc, st, "d_")
        sb = lambda n, s, dt=F32: st.enter_context(nc.sbuf_tensor("d_" + n, s, dt))
        yf, yr = sb("yf", [P, 2, SEQ]), sb("yr", [P, 2, SEQ])
        yc, sq, rstd = sb("yc", [P, SEQ]), sb("sq", [P, SEQ]), sb("rstd", [P, SEQ])
        g_up = sb("g_up", [P, CH])
        raw = sb("raw", [P, 2, KD, P])
        w_hi, w_lo = sb("w_hi", [P, 2, KD, P], F32R), sb("w_lo", [P, 2, KD, P], F32R)
        ps = [st.enter_context(nc.psum_tensor(f"d_ps{n}", [P, BANK], F32)) for n in range(8)]
        mix, sg = sb("mix", [P, KD, SEQ]), sb("sg", [P, SEQ])
        x1, hi, lo = t["x1"], t["h2_hi"], t["h2_lo"]
        full = [sem(f"psum_full{b}") for b in range(4)]
        free = [sem(f"psum_free{b}") for b in range(4)]
        gate = {n: sem("passed_" + n) for n in ("pe", "sp", "act", "dve", "pool")}
        block = st.enter_context(nc.Block())

        @block.sync
        def _(sp):
            sp.dma_start(sg[:], d["sgs"]).then_inc(sem("g_up"), 16)
            sp.dma_start(mix[:, PAIRS:KD], d["mixd"][:, PAIRS:KD]).then_inc(sem("mix_r"), 16)
            for j in range(PAIRS):
                if j >= 2:
                    sp.wait_ge(sem("centred"), j - 1)
                for x, buf in ((0, yf), (1, yr)):
                    sp.dma_start(buf[:, j % 2].rearrange("p (s c) -> p s c", c=C),
                                 d["ys"][x, NCTX:STEPS, :, j].rearrange("s p c -> p s c")).then_inc(sem(f"y{j % 2}"), 16)
                if j == 0:
                    sp.dma_start(mix[:, 0:PAIRS], d["mixd"][:, 0:PAIRS]).then_inc(sem("mix_c"), 16)
                    sp.dma_start(g_up[:], d["g_up"]).then_inc(sem("g_up"), 16)
                    sp.dma_start(raw[:], d["w_out"][0]).then_inc(sem("raw"), 16)
            sp.dma_start(x1[:], d["xT"]).then_inc(sem("x"), 16)
            with nc.sync.Fori(0, 3) as i:
                for s in range(2):
                    hold(sp, gate["sp"], sem(f"lo{s}"), nc.sync.snap(i + 1))
                sp.dma_start(raw[:], d["w_out"][i + 1]).then_inc(sem("raw"), 16)

        @block.tensor
        def _(pe):
            pe.wait_ge(sem("g_up"), 32)
            for j in range(PAIRS):
                pe.wait_ge(sem("summed"), j + 1)
                pe.wait_ge(sem("centred"), j)
                for g in G:
                    mm = nc.tensor.matmul(ps[g][:], t["c_headones"], yf[:, j % 2, cols(g)], start=True, stop=True)
                mm.then_inc(sem("p_mean"), 1)
                pe.wait_ge(sem("gated"), j)
                for g in G:
                    mm = nc.tensor.matmul(ps[4 + g][:], g_up[:, P * j:P * (j + 1)], sg[:, cols(g)], start=True, stop=True)
                mm.then_inc(sem("p_gate"), 1)
                pe.wait_ge(sem("sq"), j + 1)
                pe.wait_ge(sem("std"), j)
                for g in G:
                    mm = nc.tensor.matmul(ps[2 + g][:], t["c_headones"], sq[:, cols(g)], start=True, stop=True)
                mm.then_inc(sem("p_var"), 1)
            pe.wait_ge(sem("mix_lo"), 2)
            pe.wait_ge(sem("centred"), PAIRS)
            pe.wait_ge(sem("std"), PAIRS)
            with nc.tensor.Fori(0, 4) as i:
                n = nc.tensor.snap(i + 1)
                for s in range(2):
                    hold(pe, gate["pe"], sem(f"hi{s}"), n)
                    hold(pe, gate["pe"], sem(f"lo{s}"), n)
                    for g in G:
                        b = 2 * s + g
                        hold(pe, gate["pe"], free[b], i)
                        product(nc, ps[b][:], w_hi[:, s], w_lo[:, s], hi, lo, KD, cols(g)).then_inc(full[b], 1)

        @block.scalar
        def _(act):
            act.wait_ge(sem("mix_c"), 16)
            nc.scalar.activation(hi[:, 0:PAIRS], mix[:, 0:PAIRS], ACT.Copy).then_inc(sem("mix_hi"), 1)
            for j in range(PAIRS):
                act.wait_ge(sem("centred"), j + 1)
                nc.scalar.activation(sq[:], yc[:], ACT.Square).then_inc(sem("sq"), 1)
                act.wait_ge(sem("p_var"), j + 1)
                act.wait_ge(sem("yn"), j)
                for g in G:
                    a = nc.scalar.activation(rstd[:, cols(g)], ps[2 + g][:], ACT.Sqrt, scale=1.0 / HEAD, bias=t["c_gneps"])
                a.then_inc(sem("std"), 1)
            act.wait_ge(sem("gated"), PAIRS)
            nc.scalar.activation(hi[:, PAIRS:KD], mix[:, PAIRS:KD], ACT.Copy).then_inc(sem("mix_hi"), 1)

            def split_hi(n, first):
                hold(act, gate["act"], sem("raw"), n * 16 + 16)
                for s in range(2):
                    if not first:
                        hold(act, gate["act"], full[2 * s + 1], n)
                    nc.scalar.activation(w_hi[:, s], raw[:, s], ACT.Copy).then_inc(sem(f"hi{s}"), 1)

            split_hi(0, True)
            with nc.scalar.Fori(0, 3) as i:
                split_hi(nc.scalar.snap(i + 1), False)

        @block.gpsimd
        def _(pool):
            def split_lo(n):
                for s in range(2):
                    hold(pool, gate["pool"], sem(f"hi{s}"), n + 1)
                    nc.gpsimd.tensor_tensor(w_lo[:, s], raw[:, s], w_hi[:, s].bitcast(F32),
                                            ALU.subtract).then_inc(sem(f"lo{s}"), 1)

            with nc.gpsimd.Fori(0, 4) as i:
                split_lo(i)

        @block.vector
        def _(dve):
            TT, TS, STT = nc.vector.tensor_tensor, nc.vector.tensor_scalar, nc.vector.scalar_tensor_tensor
            dve.wait_ge(sem("mix_r"), 16)
            dve.wait_ge(sem("mix_hi"), 1)
            TT(lo[:, 0:PAIRS], mix[:, 0:PAIRS], hi[:, 0:PAIRS].bitcast(F32), ALU.subtract).then_inc(sem("mix_lo"), 1)
            for j in range(PAIRS):
                y = yf[:, j % 2]
                dve.wait_ge(sem(f"y{j % 2}"), 32 * (j // 2 + 1))
                TT(y, y, yr[:, j % 2], ALU.add).then_inc(sem("summed"), 1)
                dve.wait_ge(sem("p_mean"), j + 1)
                for g in G:
                    a = STT(out=yc[:, cols(g)], in0=ps[g][:], scalar=-1.0 / HEAD, in1=y[:, cols(g)], op0=ALU.mult, op1=ALU.add)
                a.then_inc(sem("centred"), 1)
                dve.wait_ge(sem("std"), j + 1)
                nc.vector.reciprocal(rstd[:], rstd[:]).then_inc(sem("rstd"), 1)
                dve.wait_ge(sem("rstd"), j + 1)
                TT(yc[:], yc[:], rstd[:], ALU.mult).then_inc(sem("yn"), 1)
                dve.wait_ge(sem("yn"), j + 1)
                TS(yc[:], yc[:], t["v_ln_g"][:, j:j + 1], t["v_ln_b"][:, j:j + 1], ALU.mult, ALU.add).then_inc(sem("scaled"), 1)
                dve.wait_ge(sem("scaled"), j + 1)
                TT(yc[:], yc[:], mix[:, PAIRS + j], ALU.add).then_inc(sem("bonus"), 1)
                dve.wait_ge(sem("bonus"), j + 1)
                dve.wait_ge(sem("p_gate"), j + 1)
                for g in G:
                    a = TT(mix[:, PAIRS + j, cols(g)], yc[:, cols(g)], ps[4 + g][:], ALU.mult)
                a.then_inc(sem("gated"), 1)
            dve.wait_ge(sem("mix_hi"), 2)
            TT(lo[:, PAIRS:KD], mix[:, PAIRS:KD], hi[:, PAIRS:KD].bitcast(F32), ALU.subtract).then_inc(sem("mix_lo"), 1)
            dve.wait_ge(sem("x"), 16)
            with nc.vector.Fori(0, 4) as i:
                n = nc.vector.snap(i + 1)
                for s in range(2):
                    tile = nc.vector.snap(i * 2 + s)
                    for g in G:
                        b = 2 * s + g
                        hold(dve, gate["dve"], full[b], n)
                        xs = x1[:, bass.ds(tile, 1), cols(g)]
                        STT(out=xs, in0=ps[b][:].unsqueeze(1), scalar=t["mod"][:, 0, bass.ds(tile + 16, 1)], in1=xs,
                            op0=ALU.mult, op1=ALU.add).then_inc(free[b], 1)


def rms(nc, t, name, x, out, parts, gain, shift, store=None):
    N = 256
    groups = [slice(N * g, N * (g + 1)) for g in range(SEQ // N)]
    with ExitStack() as st:
        sem = Sems(nc, st, name + "_")
        sq = st.enter_context(nc.sbuf_tensor(name + "_sq", [P, 2, KD, N], F32))
        rstd = st.enter_context(nc.sbuf_tensor(name + "_rstd", [P, 2, N], F32))
        g1 = st.enter_context(nc.sbuf_tensor(name + "_gain", [P, KD], F32))
        ps = [st.enter_context(nc.psum_tensor(f"{name}_ps{n}", [P, BANK], F32)) for n in range(2)]
        block = st.enter_context(nc.Block())

        @block.scalar
        def _(act):
            def squares(g):
                if g >= 2:
                    act.wait_ge(sem("sums"), g - 1)
                nc.scalar.activation(sq[:, g % 2], x[:, :, groups[g]], ACT.Square).then_inc(sem("squares"), 1)

            squares(0)
            for g, cols in enumerate(groups):
                if g + 1 < len(groups):
                    squares(g + 1)
                act.wait_ge(sem("sums"), g + 1)
                if g >= 2:
                    act.wait_ge(sem("normed"), g - 1)
                nc.scalar.activation(rstd[:, g % 2], ps[g % 2][:, 0:N], ACT.Sqrt, scale=1.0 / D,
                                     bias=t["c_eps"]).then_inc(sem("std"), 1)
                if parts:
                    act.wait_ge(sem("full"), KD * (g + 1))
                    nc.scalar.activation(parts[0][:, :, cols], out[:, :, cols], ACT.Copy).then_inc(sem("hi"), 1)

        @block.tensor
        def _(pe):
            for g in range(len(groups)):
                pe.wait_ge(sem("squares"), g + 1)
                if g >= 2:
                    pe.wait_ge(sem("std"), g - 1)
                for k in range(KD):
                    mm = nc.tensor.matmul(ps[g % 2][:, 0:N], t["c_ones"], sq[:, g % 2, k], start=(k == 0), stop=(k == KD - 1))
                mm.then_inc(sem("sums"), 1)

        @block.vector
        def _(dve):
            gain(g1[:]).then_inc(sem("gain"), 1)
            dve.wait_ge(sem("gain"), 1)
            for g, cols in enumerate(groups):
                dve.wait_ge(sem("std"), g + 1)
                nc.vector.reciprocal(rstd[:, g % 2], rstd[:, g % 2]).then_inc(sem("rstd"), 1)
                dve.wait_ge(sem("rstd"), g + 1)
                nc.vector.tensor_tensor(out[:, :, cols], x[:, :, cols], bc(rstd[:, g % 2], 1, KD), ALU.mult).then_inc(sem("normed"), 1)
                dve.wait_ge(sem("normed"), g + 1)
                for k in range(KD):
                    if shift is None:
                        a = nc.vector.tensor_scalar(out[:, k, cols], out[:, k, cols], g1[:, k:k + 1], None, ALU.mult)
                    else:
                        a = nc.vector.tensor_scalar(out[:, k, cols], out[:, k, cols], g1[:, k:k + 1], shift[:, k:k + 1], ALU.mult, ALU.add)
                    a.then_inc(sem("full"), 1)

        if parts:
            @block.gpsimd
            def _(pool):
                for g, cols in enumerate(groups):
                    pool.wait_ge(sem("hi"), g + 1)
                    nc.gpsimd.tensor_tensor(parts[1][:, :, cols], out[:, :, cols], parts[0][:, :, cols].bitcast(F32),
                                            ALU.subtract).then_inc(sem("lo"), 1)

        if store is not None:
            @block.sync
            def _(sp):
                for g, cols in enumerate(groups):
                    sp.wait_ge(sem("full"), KD * (g + 1))
                    sp.dma_start(store[:, :, cols], out[:, :, cols]).then_inc(sem("stored"), 16)
                sp.wait_ge(sem("stored"), 16 * len(groups))


def ffn_up(nc, d, t):
    with ExitStack() as st:
        sem = Sems(nc, st, "e_")
        sb = lambda n, s, dt=F32: st.enter_context(nc.sbuf_tensor("e_" + n, s, dt))
        raw = sb("raw", [P, 2, KD, P])
        w_hi, w_lo = sb("w_hi", [P, 2, KD, P], F32R), sb("w_lo", [P, 2, KD, P], F32R)
        grid = sb("grid", [P, GRID_H + 2, GRID_W + 2])
        acc = sb("acc", [P, GRID_H, GRID_W])
        act_g = sb("act_g", [P, SEQ])
        z = sb("z", [P, SEQ])
        ps = [st.enter_context(nc.psum_tensor(f"e_ps{n}", [P, BANK], F32)) for n in range(4)]
        full = [sem(f"psum_full{b}") for b in range(4)]
        free = [sem(f"psum_free{b}") for b in range(4)]
        gate = {n: sem("passed_" + n) for n in ("pe", "sp", "act", "dve", "pool")}
        hi, lo = t["h2_hi"], t["h2_lo"]
        ROWS = GRID_H // 2
        cols = lambda g: slice(BANK * g, BANK * (g + 1))
        block = st.enter_context(nc.Block())

        @block.sync
        def _(sp):
            sp.dma_start(raw[:], d["w_ffn"][0]).then_inc(sem("raw"), 16)

            def store(i):
                hold(sp, gate["sp"], sem("z"), i * 2 + 2)
                sp.dma_start(d["zs"][i], z[:]).then_inc(sem("stored"), 16)

            with nc.sync.Fori(0, NFF - 1) as i:
                n = nc.sync.snap(i + 1)
                for s in range(2):
                    hold(sp, gate["sp"], sem(f"lo{s}"), n)
                sp.dma_start(raw[:], d["w_ffn"][n]).then_inc(sem("raw"), 16)
                store(nc.sync.snap(i + 0))
            store(NFF - 1)
            sp.wait_ge(sem("stored"), 16 * NFF)

        @block.tensor
        def _(pe):
            with nc.tensor.Fori(0, NFF) as i:
                n = nc.tensor.snap(i + 1)
                for s in range(2):
                    hold(pe, gate["pe"], sem(f"hi{s}"), n)
                    hold(pe, gate["pe"], sem(f"lo{s}"), n)
                    for g in range(2):
                        b = 2 * s + g
                        hold(pe, gate["pe"], free[b], i)
                        product(nc, ps[b][:], w_hi[:, s], w_lo[:, s], hi, lo, KD, cols(g)).then_inc(full[b], 1)

        @block.scalar
        def _(act):
            def split_hi(n, s):
                hold(act, gate["act"], sem("raw"), n * 16 + 16)
                if not isinstance(n, int):
                    hold(act, gate["act"], full[2 * s + 1], n)
                nc.scalar.activation(w_hi[:, s], raw[:, s], ACT.Copy).then_inc(sem(f"hi{s}"), 1)

            def step(i, n, last):
                hold(act, gate["act"], sem("conv"), i * 9)
                for g in range(2):
                    hold(act, gate["act"], full[g], n)
                    nc.scalar.activation(grid[:, 1 + ROWS * g:1 + ROWS * (g + 1), 1:1 + GRID_W],
                                         ps[g][:].rearrange("p (h w) -> p h w", w=GRID_W), ACT.Copy).then_inc(free[g], 1)
                if not last:
                    split_hi(n, 0)
                hold(act, gate["act"], sem("conv"), i * 9 + 9)
                hold(act, gate["act"], sem("z"), i * 2)
                nc.scalar.activation(act_g[:], acc[:].rearrange("p h w -> p (h w)"), ACT.Silu).then_inc(sem("silu"), 1)
                if not last:
                    split_hi(n, 1)

            act.wait_ge(sem("rim"), 1)
            for s in range(2):
                split_hi(0, s)
            with nc.scalar.Fori(0, NFF - 1) as i:
                step(nc.scalar.snap(i + 0), nc.scalar.snap(i + 1), False)
            step(NFF - 1, NFF, True)

        @block.gpsimd
        def _(pool):
            with nc.gpsimd.Fori(0, NFF) as i:
                n = nc.gpsimd.snap(i + 1)
                for s in range(2):
                    hold(pool, gate["pool"], sem(f"hi{s}"), n)
                    nc.gpsimd.tensor_tensor(w_lo[:, s], raw[:, s], w_hi[:, s].bitcast(F32), ALU.subtract).then_inc(sem(f"lo{s}"), 1)

        @block.vector
        def _(dve):
            nc.vector.memset(grid[:], 0.0).then_inc(sem("rim"), 1)
            w = t["v_ffn_conv_w"]
            with nc.vector.Fori(0, NFF) as i:
                n = nc.vector.snap(i + 1)
                for g in range(2):
                    hold(dve, gate["dve"], free[g], n)
                hold(dve, gate["dve"], sem("silu"), i)
                for tap in range(9):
                    dy, dx = tap // 3, tap % 3
                    view = grid[:, dy:dy + GRID_H, dx:dx + GRID_W]
                    wt = w[:, bass.ds(i + tap * NFF, 1)]
                    if tap:
                        hold(dve, gate["dve"], sem("conv"), nc.vector.snap(i * 9 + tap))
                        a = nc.vector.scalar_tensor_tensor(out=acc[:], in0=view, scalar=wt, in1=acc[:], op0=ALU.mult, op1=ALU.add)
                    else:
                        a = nc.vector.tensor_scalar(acc[:], view, wt, t["v_ffn_conv_b"][:, bass.ds(i, 1)], ALU.mult, ALU.add)
                    a.then_inc(sem("conv"), 1)
                hold(dve, gate["dve"], sem("silu"), n)
                hold(dve, gate["dve"], sem("stored"), i * 16)
                for g in range(2):
                    hold(dve, gate["dve"], full[2 + g], n)
                    hold(dve, gate["dve"], free[2 + g], i)
                    nc.vector.tensor_tensor(z[:, cols(g)], act_g[:, cols(g)], ps[2 + g][:], ALU.mult).then_inc(free[2 + g], 1)
                for g in range(2):
                    hold(dve, gate["dve"], free[2 + g], n)
                dve.sem_inc(sem("z"), 2)


def ffn_down(nc, d, t):
    with ExitStack() as st:
        sem = Sems(nc, st, "f_")
        sb = lambda n, s, dt=F32: st.enter_context(nc.sbuf_tensor("f_" + n, s, dt))
        z_hi, z_lo = sb("z_hi", [P, NFF, BANK], F32R), sb("z_lo", [P, NFF, BANK], F32R)
        z_raw = sb("z_raw", [P, 2, BANK])
        raw = sb("raw", [P, 2, NFF, P])
        w_hi, w_lo = sb("w_hi", [P, 2, NFF, P], F32R), sb("w_lo", [P, 2, NFF, P], F32R)
        x1, x2 = sb("x1", [P, 2, BANK]), sb("x2", [P, 2, BANK])
        ps = [st.enter_context(nc.psum_tensor(f"f_ps{n}", [P, BANK], F32)) for n in range(2)]
        gate = {n: sem("passed_" + n) for n in ("pe", "sp", "act", "dve", "pool")}
        HALVES, TURNS = 2, KD // 2
        ZT = NFF // 2
        cols = lambda g: slice(BANK * g, BANK * (g + 1))
        ended = lambda turn, s: turn * (2 * NFF) + (s + 1) * NFF
        block = st.enter_context(nc.Block())

        @block.sync
        def _(sp):
            def wait(s, value):
                hold(sp, gate["sp"], s, value)

            def load_z(g):
                with nc.sync.Fori(0, ZT) as j:
                    for s in range(2):
                        wait(sem(f"z_lo{s}"), nc.sync.snap(j + g * ZT))
                        sp.dma_start(z_raw[:, s], d["zs"][2 * j + s, :, cols(g)]).then_inc(sem(f"z_raw{s}"), 16)

            def load_w(g, i, s):
                turn = held(nc.sync, i + g * TURNS)
                wait(sem(f"lo{s}"), turn)
                sp.dma_start(raw[:, s], d["w_down"][2 * i + s]).then_inc(sem(f"raw{s}"), 16)
                wait(sem(f"x2_{s}"), turn)
                sp.dma_start(x1[:, s], d["x1s"][:, 2 * i + s, cols(g)]).then_inc(sem(f"x1_{s}"), 16)

            def store(g, i, s):
                wait(sem(f"x2_{s}"), held(nc.sync, i + (g * TURNS + 1)))
                sp.dma_start(d["x2s"][:, 2 * i + s, cols(g)], x2[:, s]).then_inc(sem(f"stored{s}"), 16)

            for g in range(HALVES):
                for s in range(2):
                    load_w(g, 0, s)
                load_z(g)
                with nc.sync.Fori(1, TURNS) as i:
                    for s in range(2):
                        load_w(g, i, s)
                    for s in range(2):
                        store(g, nc.sync.snap(i - 1), s)
                for s in range(2):
                    store(g, TURNS - 1, s)
            for s in range(2):
                sp.wait_ge(sem(f"stored{s}"), 16 * HALVES * TURNS)

        @block.gpsimd
        def _(pool):
            def split_w(turn, s):
                hold(pool, gate["pool"], sem(f"hi{s}"), turn + 1)
                nc.gpsimd.tensor_tensor(w_lo[:, s], raw[:, s], w_hi[:, s].bitcast(F32), ALU.subtract).then_inc(sem(f"lo{s}"), 1)

            with nc.gpsimd.Fori(0, HALVES * TURNS) as turn:
                for s in range(2):
                    split_w(turn, s)

        @block.scalar
        def _(act):
            def wait(s, value):
                hold(act, gate["act"], s, value)

            def split_z(g):
                with nc.scalar.Fori(0, ZT) as j:
                    for s in range(2):
                        wait(sem(f"z_raw{s}"), nc.scalar.snap((j + (g * ZT + 1)) * 16))
                        if g:
                            wait(sem("z_used"), nc.scalar.snap(2 * j + (s + 1 + ended(TURNS - 1, 0))))
                        nc.scalar.activation(z_hi[:, bass.ds(2 * j + s, 1)], z_raw[:, s:s + 1], ACT.Copy).then_inc(sem(f"z_hi{s}"), 1)

            def split_w(turn, s, first=False):
                wait(sem(f"raw{s}"), held(nc.scalar, turn * 16 + 16))
                if not first:
                    wait(sem("z_used"), held(nc.scalar, ended(turn - 1, s)))
                nc.scalar.activation(w_hi[:, s], raw[:, s], ACT.Copy).then_inc(sem(f"hi{s}"), 1)

            for g in range(HALVES):
                split_w(g * TURNS, 0, g == 0)
                split_z(g)
                split_w(g * TURNS, 1, g == 0)
                with nc.scalar.Fori(1, TURNS) as i:
                    for s in range(2):
                        split_w(nc.scalar.snap(i + g * TURNS), s)

        @block.tensor
        def _(pe):
            def tile(turn, g, s):
                hold(pe, gate["pe"], sem(f"hi{s}"), turn + 1)
                hold(pe, gate["pe"], sem(f"lo{s}"), turn + 1)
                hold(pe, gate["pe"], sem(f"x2_{s}"), turn)
                for k in range(NFF):
                    pe.wait_ge(sem(f"z_lo{k % 2}"), g * ZT + k // 2 + 1)
                    for n, (w, x) in enumerate(((w_hi, z_hi), (w_hi, z_lo), (w_lo, z_hi))):
                        mm = nc.tensor.matmul(ps[s][:], w[:, s, k], x[:, k], start=(k == 0 and n == 0), stop=(k == NFF - 1 and n == 2))
                    mm.then_inc(sem("z_used"), 1)

            for g in range(HALVES):
                with nc.tensor.Fori(0, TURNS) as i:
                    turn = nc.tensor.snap(i + g * TURNS)
                    for s in range(2):
                        tile(turn, g, s)

        @block.vector
        def _(dve):
            def wait(s, value):
                hold(dve, gate["dve"], s, value)

            for g in range(HALVES):
                with nc.vector.Fori(0, ZT) as j:
                    for s in range(2):
                        wait(sem(f"z_hi{s}"), nc.vector.snap(j + (g * ZT + 1)))
                        k = bass.ds(2 * j + s, 1)
                        nc.vector.tensor_tensor(z_lo[:, k], z_raw[:, s:s + 1], z_hi[:, k].bitcast(F32), ALU.subtract).then_inc(sem(f"z_lo{s}"), 1)
                with nc.vector.Fori(0, TURNS) as i:
                    turn = nc.vector.snap(i + g * TURNS)
                    for s in range(2):
                        wait(sem("z_used"), nc.vector.snap(ended(turn, s)))
                        wait(sem(f"x1_{s}"), nc.vector.snap(turn * 16 + 16))
                        wait(sem(f"stored{s}"), nc.vector.snap(turn * 16))
                        nc.vector.scalar_tensor_tensor(out=x2[:, s], in0=ps[s][:], scalar=t["mod"][:, 0, bass.ds(2 * i + (s + 40), 1)],
                                                       in1=x1[:, s], op0=ALU.mult, op1=ALU.add).then_inc(sem(f"x2_{s}"), 1)
def attention(nc, d, t):
    NT = 4
    QT = SEQ // P
    FOX, SB = 4, 2
    W_POOL = ((2, 4), (8, 16))
    RIM = 16
    cols = lambda g: slice(BANK * g, BANK * (g + 1))
    with ExitStack() as st:
        sem = Sems(nc, st, "g_")
        sb = lambda n, s, dt=F32: st.enter_context(nc.sbuf_tensor("g_" + n, s, dt))
        raw = sb("raw", [P, NT, KD, P])
        w_hi, w_lo = sb("w_hi", [P, NT, KD, P], F32R), sb("w_lo", [P, NT, KD, P], F32R)
        q, k, v = sb("q", [P, SEQ]), sb("k", [P, SEQ]), sb("v", [P, SEQ])
        sq, rstd = sb("sq", [P, 2, SEQ]), sb("rstd", [P, 2, SEQ])
        vt = sb("vt", [P, QT, P])
        gs = sb("gs", [P, SEQ])
        out = sb("out", [P, SEQ])
        qz = sb("qz", [P, 2, SEQ])
        negc = sq
        sc = sb("sc", [P, 2, SEQ])
        logf, cum = sc[0:8], rstd[0:8, 1]
        s2 = sb("s2", [P, 2, SEQ])
        pt = sb("pt", [P, 2, QT, P])
        mx, den, rden = sb("mx", [P, 2]), sb("den", [P, 4]), sb("rden", [P, 4])
        ot = sb("ot", [P, 2, P])
        qg8 = sb("qg8", [P, 1])
        wpool = sb("wpool", [P, 2, P])
        ps = [st.enter_context(nc.psum_tensor(f"g_ps{n}", [P, BANK], F32)) for n in range(2)]
        pb = [st.enter_context(nc.psum_tensor(f"g_pb{n}", [P, 2 * BANK], F32)) for n in range(3)]
        gate = {n: sem("passed_" + n) for n in ("pe", "sp", "act", "dve", "pool")}
        h_hi, h_lo, ident = t["h3_hi"], t["h3_lo"], t["c_ident"]
        TURNS = 2 + FOX + SB
        block = st.enter_context(nc.Block())
        full = {n: sem("full_" + n) for n in ("pb0", "pb1", "pb2", "ps0", "ps1")}
        free = {n: sem("free_" + n) for n in ("pb0", "pb1", "pb2", "ps0", "ps1")}
        buf = {"pb0": pb[0], "pb1": pb[1], "pb2": pb[2], "ps0": ps[0], "ps1": ps[1]}
        UNITS = 2 * QT
        USES_POOL = {"pb0": 2, "pb1": 2, "pb2": 2, "ps0": 1, "ps1": 1}
        USES_FOX = {"pb0": 2 + QT, "pb1": 2 + QT, "pb2": 2 + UNITS, "ps0": 1 + UNITS, "ps1": 1 + QT}
        USES_SB = {"pb0": 1 + QT, "pb1": 1 + QT, "pb2": 2 + UNITS, "ps0": 1 + UNITS, "ps1": 1 + QT}
        unit = lambda u: (u // 2, u % 2, P * (u // 2 + 1))

        def bases(eng, i, sbr):
            if not sbr:
                return {n: eng.snap(i * USES_FOX[n] + USES_POOL[n]) for n in full}
            return {n: eng.snap(i * USES_SB[n] + (USES_POOL[n] + FOX * USES_FOX[n])) for n in full}

        @block.sync
        def _(sp):
            def wait(s, value):
                hold(sp, gate["sp"], s, value)

            def load(n):
                for tl in range(NT):
                    wait(sem(f"lo{tl}"), n)
                sp.dma_start(raw[:], d["w2"][n]).then_inc(sem("raw"), 16)

            def store(n, tile):
                wait(sem("out"), held(nc.sync, n + 1))
                sp.dma_start(d["mix2"][:, tile], out[:]).then_inc(sem("stored"), 16)

            sp.dma_start(raw[:], d["w2"][0]).then_inc(sem("raw"), 16)
            sp.wait_ge(sem("wpool0"), 1)
            for g in range(4):
                half = slice(HEAD * (g % 2), HEAD * (g % 2) + HEAD)
                sp.dma_start(wpool[half, g // 2, half], d["w_pool"][g]).then_inc(sem("wpool"), 16)
            def load_sums(i):
                wait(full["pb1"], held(nc.sync, i * USES_FOX["pb1"] + (USES_POOL["pb1"] + 2)))
                sp.dma_start(negc[:], d["cums"][bass.ds(2 * i, 2)].unsqueeze(0).broadcast_to([P, 2, SEQ])).then_inc(sem("negc"), 16)

            sp.wait_ge(sem("cum"), 1)
            sp.dma_start(d["cums"], cum).then_inc(sem("cums"), 16)
            for j in range(2):
                load(j + 1)
                store(j, FOX + j)
            sp.wait_ge(sem("cums"), 16)
            with nc.sync.Fori(0, FOX) as i:
                load(nc.sync.snap(i + 3))
                load_sums(i)
                store(nc.sync.snap(i + 2), i)
            load(7)
            store(2 + FOX, FOX + 2)
            store(3 + FOX, FOX + 3)
            sp.wait_ge(sem("stored"), 16 * TURNS)

        @block.tensor
        def _(pe):
            def wait(s, value):
                hold(pe, gate["pe"], s, value)

            def tile(n, tl, outs):
                wait(sem(f"hi{tl}"), n + 1)
                wait(sem(f"lo{tl}"), n + 1)
                for g, (o, name, reads) in enumerate(outs):
                    wait(free[name], reads)
                    mm = product(nc, o, w_hi[:, tl], w_lo[:, tl], h_hi, h_lo, KD, cols(g))
                    if g or outs[1][1] != name:
                        mm.then_inc(full[name], 1)

            def both(name, reads):
                return [(buf[name][:, cols(g)], name, reads) for g in range(2)]

            def pooled_turn(j):
                if j == 0:
                    tile(0, 0, [(ps[0][:], "ps0", 0), (ps[1][:], "ps1", 0)])
                    pe.wait_ge(sem("wpool"), 64)
                tile(j, 1 - j, both("pb0", j))
                tile(j, 2 - j, both("pb1", j))
                pe.wait_ge(sem("pooled"), j + 1)
                wait(free["pb2"], j)
                for g in range(2):
                    mm = nc.tensor.matmul(pb[2][:, cols(g)], wpool[:, j], q[:, cols(g)], start=True, stop=True)
                mm.then_inc(full["pb2"], 1)

            def scores(u, first, base, mask):
                qt, h, keys = unit(u)
                name = f"pb{u % 2}"
                wait(free[name], base[name] + (first + u // 2))
                for at in range(0, keys, BANK):
                    to = min(keys, at + BANK)
                    mm = nc.tensor.matmul(buf[name][:, at:to], qz[:, h, P * qt:P * (qt + 1)], k[:, at:to], start=True,
                                          stop=(to < keys))
                mm = nc.tensor.matmul(buf[name][:, keys - P:keys], ident, mask, start=False, stop=True)
                mm.then_inc(full[name], 1)

            def turn_weights(u, base, sbr):
                qt, h, keys = unit(u)
                wait(sem(f"weights{u % 2}"), base[f"w{u % 2}"] + (u // 2 + 1))
                wait(free["pb2"], base["pb2"] + (2 + u))
                for b in range(qt + 1):
                    mm = nc.tensor.transpose(pb[2][:, P * b:P * (b + 1)], (sc if sbr else s2)[:, u % 2, P * b:P * (b + 1)], ident)
                mm.then_inc(full["pb2"], 1)

            def values(u, base):
                qt, h, keys = unit(u)
                wait(free["pb2"], base["pb2"] + (3 + u))
                wait(free["ps0"], base["ps0"] + (1 + u))
                for b in range(qt + 1):
                    mm = nc.tensor.matmul(ps[0][:, 0:HEAD], pt[:, u % 2, b], vt[:, b, HEAD * h:HEAD * (h + 1)],
                                          start=(b == 0), stop=(b == qt))
                mm.then_inc(full["ps0"], 1)

            def turn_output(qt, base):
                wait(free["ps0"], base["ps0"] + (1 + 2 * (qt + 1)))
                wait(free["ps1"], base["ps1"] + (1 + qt))
                nc.tensor.transpose(ps[1][:, 0:P], ot[:, qt % 2], ident).then_inc(full["ps1"], 1)

            def heads(n, i, sbr):
                base = bases(nc.tensor, i, sbr)
                w = nc.tensor.snap(i * QT + (FOX * QT if sbr else 0))
                base.update(w0=w, w1=w)
                tile(n, 0, both("pb0", base["pb0"]))
                tile(n, 1, both("pb1", base["pb1"]))
                tile(n, 2, both("pb2", base["pb2"]))
                tile(n, 3, [(ps[0][:], "ps0", base["ps0"]), (ps[1][:], "ps1", base["ps1"])])
                wait(free["pb2"], base["pb2"] + 1)
                for b in range(QT):
                    mm = nc.tensor.transpose(pb[2][:, P * b:P * (b + 1)], v[:, P * b:P * (b + 1)], ident)
                mm.then_inc(full["pb2"], 1)
                if not sbr:
                    for x, name in ((0, "pb0"), (1, "pb1")):
                        wait(sem("sq"), i * 2 + (x + 1))
                        wait(free[name], base[name] + 1)
                        for g in range(2):
                            mm = nc.tensor.matmul(buf[name][:, cols(g)], t["c_headones"], sq[:, x, cols(g)], start=True, stop=True)
                        mm.then_inc(full[name], 1)
                    wait(sem("qk"), i * 2 + 2)
                else:
                    for name in ("pb0", "pb1"):
                        wait(free[name], base[name] + 1)
                wait(free["pb2"], base["pb2"] + 2)
                first = 1 if sbr else 2
                mask = t["c_negstrict"] if sbr else t["c_negcausal"]
                scores(0, first, base, mask)
                scores(1, first, base, mask)
                for u in range(UNITS + 3):
                    if u < UNITS:
                        turn_weights(u, base, sbr)
                    if u + 2 < UNITS:
                        scores(u + 2, first, base, mask)
                    if 1 <= u <= UNITS:
                        values(u - 1, base)
                    if u >= 3 and u % 2:
                        turn_output((u - 3) // 2, base)

            for j in range(2):
                pooled_turn(j)
            with nc.tensor.Fori(0, FOX) as i:
                heads(nc.tensor.snap(i + 2), i, False)
            with nc.tensor.Fori(0, SB) as i:
                heads(nc.tensor.snap(i + (2 + FOX)), i, True)

        @block.scalar
        def _(act):
            def wait(s, value):
                hold(act, gate["act"], s, value)

            def split_hi(n, tl):
                wait(sem("raw"), n * 16 + 16)
                nc.scalar.activation(w_hi[:, tl], raw[:, tl], ACT.Copy).then_inc(sem(f"hi{tl}"), 1)

            def pooled_turn(j):
                if j == 0:
                    for g in range(2):
                        act.wait_ge(full[f"ps{g}"], 1)
                        nc.scalar.activation(logf[:, 0, cols(g)], ps[g][0:8, :], ACT.Abs, bias=t["v_b_f"][0:8]).then_inc(sem("ff"), 1)
                    act.wait_ge(sem("ff"), 2)
                    nc.scalar.activation(logf[:, 0], logf[:, 0], ACT.Exp, scale=-1.0).then_inc(sem("ff"), 1)
                    act.wait_ge(sem("ff"), 3)
                    nc.scalar.activation(logf[:, 0], logf[:, 0], ACT.Ln, bias=1.0).then_inc(sem("ff"), 1)
                act.wait_ge(full["pb0"], j + 1)
                act.wait_ge(sem("pooled"), j)
                nc.scalar.activation(v[:], pb[0][:], ACT.Copy).then_inc(free["pb0"], 1)
                act.wait_ge(full["pb1"], j + 1)
                act.wait_ge(sem("out"), j)
                nc.scalar.activation(gs[:], pb[1][:], ACT.Silu).then_inc(free["pb1"], 1)
                for tl in range(NT):
                    split_hi(j + 1, tl)

            def heads(n, i, sbr, last):
                base = bases(nc.scalar, i, sbr)
                for tl, name, dst in ((0, "pb0", q), (1, "pb1", k), (2, "pb2", v)):
                    wait(full[name], base[name] + 1)
                    if sbr and tl == 0:
                        for h in range(2):
                            rows = slice(HEAD * h, HEAD * h + HEAD)
                            a = nc.scalar.activation(qz[rows, h], buf[name][rows, :], ACT.Copy, scale=0.125)
                        a.then_inc(free[name], 1)
                    else:
                        nc.scalar.activation(dst[:], buf[name][:], ACT.Copy).then_inc(free[name], 1)
                    if not last:
                        split_hi(n + 1, tl)
                wait(full["pb2"], base["pb2"] + 2)
                nc.scalar.activation(vt[:].rearrange("p b c -> p (b c)"), pb[2][:], ACT.Copy).then_inc(free["pb2"], 1)
                wait(sem("out"), n)
                for g in range(2):
                    wait(full[f"ps{g}"], base[f"ps{g}"] + 1)
                    nc.scalar.activation(gs[:, cols(g)], ps[g][:], ACT.Silu).then_inc(free[f"ps{g}"], 1)
                if not last:
                    split_hi(n + 1, 3)
                if not sbr:
                    for x, name in ((0, "pb0"), (1, "pb1")):
                        wait(full[name], base[name] + 2)
                        nc.scalar.activation(rstd[:, x], buf[name][:], ACT.Sqrt, scale=1.0 / HEAD, bias=t["c_eps"]).then_inc(free[name], 1)
                    for u in range(UNITS):
                        qt, h, keys = unit(u)
                        wait(sem("mx"), i * UNITS + (u + 1))
                        if u >= 2:
                            wait(full["pb2"], base["pb2"] + (2 + u - 1))
                        nc.scalar.activation(s2[:, u % 2, 0:keys], sc[:, u % 2, 0:keys], ACT.Exp, bias=mx[:, u % 2:u % 2 + 1],
                                             accum_out=den[:, u % 4:u % 4 + 1]).then_inc(sem(f"weights{u % 2}"), 1)
                else:
                    for u in range(UNITS):
                        qt, h, keys = unit(u)
                        name = f"pb{u % 2}"
                        wait(full[name], base[name] + (2 + u // 2))
                        if u >= 2:
                            wait(full["pb2"], base["pb2"] + (2 + u - 1))
                        nc.scalar.activation(sc[:, u % 2, 0:keys], buf[name][:, 0:keys], ACT.Sigmoid)
                        nc.scalar.activation(s2[:, u % 2, 0:keys], buf[name][:, 0:keys], ACT.Sigmoid, scale=-1.0).then_inc(free[name], 1)

            for tl in range(NT):
                split_hi(0, tl)
            for j in range(2):
                pooled_turn(j)
            with nc.scalar.Fori(0, FOX) as i:
                heads(nc.scalar.snap(i + 2), i, False, False)
            with nc.scalar.Fori(0, 1) as i:
                heads(nc.scalar.snap(i + (2 + FOX)), i, True, False)
            with nc.scalar.Fori(1, 2) as i:
                heads(nc.scalar.snap(i + (2 + FOX)), i, True, True)

        @block.gpsimd
        def _(pool):
            nc.gpsimd.memset(wpool[:], 0.0).then_inc(sem("wpool0"), 1)
            with nc.gpsimd.Fori(0, TURNS) as n:
                for tl in range(NT):
                    hold(pool, gate["pool"], sem(f"hi{tl}"), n + 1)
                    nc.gpsimd.tensor_tensor(w_lo[:, tl], raw[:, tl], w_hi[:, tl].bitcast(F32), ALU.subtract).then_inc(sem(f"lo{tl}"), 1)

        @block.vector
        def _(dve):
            TT, TS, STT = nc.vector.tensor_tensor, nc.vector.tensor_scalar, nc.vector.scalar_tensor_tensor

            def wait(s, value):
                hold(dve, gate["dve"], s, value)

            def ones(n):
                return t["c_ones"][:, 0:1].broadcast_to([P, n])

            def forget_sums():
                for g in range(2):
                    dve.wait_ge(sem("ff"), 4)
                    TS(logf[:, 1, cols(g)], ps[g][0:8, :], t["v_b_f"][0:8], 0.0, ALU.add, ALU.min).then_inc(free[f"ps{g}"], 1)
                for g in range(2):
                    dve.wait_ge(free[f"ps{g}"], 1)
                TT(logf[:, 1], logf[:, 0], logf[:, 1], ALU.subtract).then_inc(sem("logf"), 1)
                dve.wait_ge(sem("logf"), 1)
                nc.vector.tensor_tensor_scan(cum, ones(SEQ)[0:8], logf[:, 1], 0.0, ALU.mult, ALU.add).then_inc(sem("cum"), 1)

            def pooled_turn(j):
                run = sq[:].rearrange("p x s -> p (x s)")
                dve.wait_ge(free["pb0"], j + 1)
                dve.wait_ge(sem("rim"), 1)
                nc.vector.tensor_tensor_scan(run[:, RIM:RIM + SEQ], ones(SEQ), v[:], 0.0, ALU.mult, ALU.add).then_inc(sem("run"), 1)
                dve.wait_ge(sem("run"), j + 1)
                mean = rstd[:, 0]
                for h, win in enumerate(W_POOL[j]):
                    rows = slice(HEAD * h, HEAD * h + HEAD)
                    TT(mean[rows], run[rows, RIM:RIM + SEQ], run[rows, RIM - win:RIM + SEQ - win], ALU.subtract).then_inc(sem("diff"), 1)
                dve.wait_ge(sem("diff"), 2 * j + 2)
                TT(mean[:, 0:RIM], mean[:, 0:RIM], t["c_invcount"][:, j], ALU.mult).then_inc(sem("mean"), 1)
                STT(out=q[:, RIM:SEQ], in0=mean[:, RIM:SEQ], scalar=t["c_invwin"][:, j:j + 1], in1=v[:, RIM:SEQ],
                    op0=ALU.mult, op1=ALU.subtract).then_inc(sem("rest"), 1)
                dve.wait_ge(sem("mean"), j + 1)
                dve.wait_ge(sem("rest"), j + 1)
                TT(q[:, 0:RIM], mean[:, 0:RIM], v[:, 0:RIM], ALU.subtract).then_inc(sem("pooled"), 1)
                dve.wait_ge(full["pb2"], j + 1)
                dve.wait_ge(free["pb1"], j + 1)
                dve.wait_ge(sem("stored"), 16 * j)
                STT(out=out[:], in0=pb[2][:], scalar=t["v_pool_scale"][:, j:j + 1], in1=gs[:], op0=ALU.mult,
                    op1=ALU.mult).then_inc(free["pb2"], 1)
                dve.wait_ge(free["pb2"], j + 1)
                dve.sem_inc(sem("out"), 1)

            def heads(n, i, sbr):
                base = bases(nc.vector, i, sbr)

                def mid_fox(u):
                    qt, h, keys = unit(u)
                    name = f"pb{u % 2}"
                    wait(full[name], base[name] + (3 + u // 2))
                    if u >= 2:
                        wait(sem(f"weights{u % 2}"), i * QT + u // 2)
                    nc.vector.tensor_tensor_reduce(out=sc[:, u % 2, 0:keys], in0=buf[name][:, 0:keys], in1=negc[:, h, 0:keys],
                                                   scale=1.0, scalar=-3.0e38, op0=ALU.add, op1=ALU.max,
                                                   accum_out=mx[:, u % 2:u % 2 + 1]).then_inc(free[name], 1)
                    wait(free[name], base[name] + (3 + u // 2))
                    TS(mx[:, u % 2:u % 2 + 1], mx[:, u % 2:u % 2 + 1], -1.0, None, ALU.mult).then_inc(sem("mx"), 1)

                def mid_sb(u):
                    qt, h, keys = unit(u)
                    name = f"pb{u % 2}"
                    x, y = sc[:, u % 2, 0:keys], s2[:, u % 2, 0:keys]
                    wait(free[name], base[name] + (2 + u // 2))
                    nc.vector.tensor_tensor_scan(y[:, ::-1], y[:, ::-1], ones(keys), 1.0, ALU.mult, ALU.mult).then_inc(sem("left"), 1)
                    wait(sem("left"), i * UNITS + (u + 1))
                    TT(x[:, 0:keys - 1], x[:, 0:keys - 1], y[:, 1:keys], ALU.mult).then_inc(sem(f"weights{u % 2}"), 1)

                def weights_out(u):
                    qt, h, keys = unit(u)
                    wait(full["pb2"], base["pb2"] + (3 + u))
                    if u >= 2:
                        wait(full["ps0"], base["ps0"] + (1 + u - 1))
                    nc.vector.tensor_copy(pt[:, u % 2, 0:qt + 1].rearrange("p b c -> p (b c)"), pb[2][:, 0:keys]).then_inc(free["pb2"], 1)

                def values_out(u):
                    qt, h, keys = unit(u)
                    dst = ot[:, qt % 2, HEAD * h:HEAD * (h + 1)]
                    if not sbr:
                        wait(sem(f"weights{u % 2}"), i * QT + (u // 2 + 1))
                        nc.vector.reciprocal(rden[:, u % 4:u % 4 + 1], den[:, u % 4:u % 4 + 1]).then_inc(sem("rden"), 1)
                        wait(sem("rden"), i * UNITS + (u + 1))
                    wait(full["ps0"], base["ps0"] + (2 + u))
                    if qt >= 2:
                        wait(full["ps1"], base["ps1"] + (1 + qt - 1))
                    if sbr:
                        nc.vector.tensor_copy(dst, ps[0][:, 0:HEAD]).then_inc(free["ps0"], 1)
                    else:
                        TS(dst, ps[0][:, 0:HEAD], rden[:, u % 4:u % 4 + 1], None, ALU.mult).then_inc(free["ps0"], 1)

                def gated(qt):
                    wait(full["ps1"], base["ps1"] + (2 + qt))
                    TT(out[:, P * qt:P * (qt + 1)], ps[1][:, 0:P], gs[:, P * qt:P * (qt + 1)], ALU.mult).then_inc(free["ps1"], 1)

                if not sbr:
                    for x, name, src in ((0, "pb0", q), (1, "pb1", k)):
                        wait(free[name], base[name] + 1)
                        TT(sq[:, x], src[:], src[:], ALU.mult).then_inc(sem("sq"), 1)
                    for x, name, src, g in ((0, "pb0", q, qg8[:]), (1, "pb1", k, t["v_kg"])):
                        wait(free[name], base[name] + 2)
                        nc.vector.reciprocal(rstd[:, x], rstd[:, x]).then_inc(sem("rstd"), 1)
                        wait(sem("rstd"), i * 2 + (x + 1))
                        if x == 0:
                            for h in range(2):
                                rows = slice(HEAD * h, HEAD * h + HEAD)
                                a = STT(out=qz[rows, h], in0=q[rows], scalar=g[rows], in1=rstd[rows, 0], op0=ALU.mult, op1=ALU.mult)
                        else:
                            a = STT(out=k[:], in0=k[:], scalar=g, in1=rstd[:, 1], op0=ALU.mult, op1=ALU.mult)
                        a.then_inc(sem("qk"), 1)
                    wait(sem("negc"), i * 16 + 16)
                wait(sem("stored"), n * 16)
                mid = mid_sb if sbr else mid_fox
                mid(0)
                mid(1)
                for u in range(UNITS + 3):
                    if u < UNITS:
                        weights_out(u)
                    if u + 2 < UNITS:
                        mid(u + 2)
                    if 1 <= u <= UNITS:
                        values_out(u - 1)
                    if u >= 3 and u % 2:
                        gated((u - 3) // 2)
                wait(free["ps1"], base["ps1"] + (1 + QT))
                dve.sem_inc(sem("out"), 1)

            nc.vector.memset(sq[:, 0, 0:RIM], 0.0).then_inc(sem("rim"), 1)
            nc.vector.memset(qz[:], 0.0).then_inc(sem("rim"), 1)
            TS(qg8[:], t["v_qg"], 0.125, None, ALU.mult).then_inc(sem("qg8"), 1)
            forget_sums()
            for j in range(2):
                pooled_turn(j)
            dve.wait_ge(sem("cum"), 1)
            dve.wait_ge(sem("qg8"), 1)
            with nc.vector.Fori(0, FOX) as i:
                heads(nc.vector.snap(i + 2), i, False)
            with nc.vector.Fori(0, SB) as i:
                heads(nc.vector.snap(i + (2 + FOX)), i, True)


def output(nc, d, t):
    G = range(2)
    cols = lambda g: slice(BANK * g, BANK * (g + 1))
    with ExitStack() as st:
        sem = Sems(nc, st, "h_")
        sb = lambda n, s, dt=F32: st.enter_context(nc.sbuf_tensor("h_" + n, s, dt))
        mix, x3 = sb("mix", [P, KD, SEQ]), sb("x3", [P, KD, SEQ])
        m_hi, m_lo = sb("m_hi", [P, KD, SEQ], F32R), sb("m_lo", [P, KD, SEQ], F32R)
        raw = sb("raw", [P, 2, KD, P])
        w_hi, w_lo = sb("w_hi", [P, 2, KD, P], F32R), sb("w_lo", [P, 2, KD, P], F32R)
        ps = [st.enter_context(nc.psum_tensor(f"h_ps{n}", [P, BANK], F32)) for n in range(4)]
        full = [sem(f"psum_full{b}") for b in range(4)]
        free = [sem(f"psum_free{b}") for b in range(4)]
        gate = {n: sem("passed_" + n) for n in ("pe", "sp", "act", "dve", "pool")}
        block = st.enter_context(nc.Block())

        @block.sync
        def _(sp):
            sp.dma_start(raw[:], d["w_out_2"][0]).then_inc(sem("raw"), 16)
            for k in range(KD):
                sp.dma_start(mix[:, k], d["mix2"][:, k]).then_inc(sem("mix"), 16)
            sp.dma_start(x3[:], d["x3s"]).then_inc(sem("x3"), 16)

            def store(i):
                for s in range(2):
                    for g in G:
                        hold(sp, gate["sp"], free[2 * s + g], held(nc.sync, i + 1))
                    sp.dma_start(d["out"][2 * i + s], x3[:, 2 * i + s]).then_inc(sem("stored"), 16)

            with nc.sync.Fori(0, 3) as i:
                n = nc.sync.snap(i + 1)
                for s in range(2):
                    hold(sp, gate["sp"], sem(f"lo{s}"), n)
                sp.dma_start(raw[:], d["w_out_2"][n]).then_inc(sem("raw"), 16)
                store(nc.sync.snap(i + 0))
            store(3)
            sp.wait_ge(sem("stored"), 16 * KD)

        @block.tensor
        def _(pe):
            pe.wait_ge(sem("mix_lo"), KD)
            with nc.tensor.Fori(0, 4) as i:
                n = nc.tensor.snap(i + 1)
                for s in range(2):
                    hold(pe, gate["pe"], sem(f"hi{s}"), n)
                    hold(pe, gate["pe"], sem(f"lo{s}"), n)
                    for g in G:
                        b = 2 * s + g
                        hold(pe, gate["pe"], free[b], i)
                        product(nc, ps[b][:], w_hi[:, s], w_lo[:, s], m_hi, m_lo, KD, cols(g)).then_inc(full[b], 1)

        @block.scalar
        def _(act):
            def split_hi(n, s):
                hold(act, gate["act"], sem("raw"), n * 16 + 16)
                if not isinstance(n, int):
                    hold(act, gate["act"], full[2 * s + 1], n)
                nc.scalar.activation(w_hi[:, s], raw[:, s], ACT.Copy).then_inc(sem(f"hi{s}"), 1)

            for s in range(2):
                split_hi(0, s)
            for k in range(KD):
                act.wait_ge(sem("mix"), 16 * KD)
                nc.scalar.activation(m_hi[:, k], mix[:, k], ACT.Copy).then_inc(sem("mix_hi"), 1)
            with nc.scalar.Fori(1, 4) as n:
                for s in range(2):
                    split_hi(n, s)

        @block.gpsimd
        def _(pool):
            with nc.gpsimd.Fori(0, 4) as n:
                for s in range(2):
                    hold(pool, gate["pool"], sem(f"hi{s}"), n + 1)
                    nc.gpsimd.tensor_tensor(w_lo[:, s], raw[:, s], w_hi[:, s].bitcast(F32), ALU.subtract).then_inc(sem(f"lo{s}"), 1)

        @block.vector
        def _(dve):
            for k in range(KD):
                dve.wait_ge(sem("mix_hi"), k + 1)
                nc.vector.tensor_tensor(m_lo[:, k], mix[:, k], m_hi[:, k].bitcast(F32), ALU.subtract).then_inc(sem("mix_lo"), 1)
            dve.wait_ge(sem("x3"), 16)
            with nc.vector.Fori(0, 4) as i:
                n = nc.vector.snap(i + 1)
                for s in range(2):
                    for g in G:
                        b = 2 * s + g
                        hold(dve, gate["dve"], full[b], n)
                        xs = x3[:, bass.ds(2 * i + s, 1), cols(g)]
                        nc.vector.tensor_tensor(xs, ps[b][:].unsqueeze(1), xs, ALU.add).then_inc(free[b], 1)


DRAM_IN = {"vecs": [P, NVEC], "consts": [P, NCON], "xT": [P, KD, SEQ], "ctxT": [P, KD, CTX], "ada": [24, P, 2, KD, P],
           "w1": [26, P, KD, P], "lora": [PAIRS, P, 2, P], "g_up": [P, CH], "w_out": [4, P, 2, KD, P],
           "w_ffn": [NFF, P, 2, KD, P], "w_down": [KD, P, NFF, P], "w2": [8, P, 4, KD, P], "w_pool": [4, HEAD, HEAD],
           "w_out_2": [4, P, 2, KD, P]}
SCRATCH = {"ops": [2, 4, PAIRS, P, SLOTS * C], "vts": [SLOTS, P, PAIRS, C], "mixd": [P, KD, SEQ], "sgs": [P, SEQ],
           "ys": [2, SLOTS, P, PAIRS, C], "x1s": [P, KD, SEQ], "zs": [NFF, P, SEQ],
           "x2s": [P, KD, SEQ], "x3s": [P, KD, SEQ], "mix2": [P, KD, SEQ], "cums": [8, SEQ]}


def program(nc):
    d = {n: nc.dram_tensor(n, s, F32, kind="ExternalInput").ap() for n, s in DRAM_IN.items()}
    d.update({n: nc.dram_tensor(n, s, F32, kind="Internal").ap() for n, s in SCRATCH.items()})
    d["out"] = nc.dram_tensor("out", [KD, P, SEQ], F32, kind="ExternalOutput").ap()
    with ExitStack() as whole:
        keep = lambda st, n, s, dt=F32, **k: st.enter_context(nc.sbuf_tensor(n, s, dt, **k))[:]
        t = {"vec": keep(whole, "vec", [P, NVEC]), "con": keep(whole, "con", [P, NCON]),
             "mod": keep(whole, "mod", [P, 2, 48]), "silu_c": keep(whole, "silu_c", [P, KD, 2]),
             "c_eps": keep(whole, "eps", [P, 1]), "c_gneps": keep(whole, "gneps", [P, 1])}
        for n, (at, m) in VECS.items():
            t["v_" + n] = t["vec"][:, at:at + m]
        for n, (at, m) in CONS.items():
            t["c_" + n] = t["con"][:, at:at + m]
        t["c_strict"] = t["c_strict"].rearrange("p (x h c) -> p x h c", x=2, h=2)
        for n in ("incl", "mask_u1", "reset", "invcount"):
            t["c_" + n] = t["c_" + n].rearrange("p (x c) -> p x c", x=2)
        t["c_mask_lev"] = t["c_mask_lev"].rearrange("p (x l c) -> p x l c", x=2, l=LEVELS)
        with ExitStack() as mixer:
            t["pend"] = keep(mixer, "pend", [P, 2, SLOTS, PAIRS], side="right")
            with ExitStack() as st:
                t["h_hi"], t["h_lo"] = keep(st, "h_hi", [P, KD, TOK], F32R), keep(st, "h_lo", [P, KD, TOK], F32R)
                prologue(nc, d, t)
                projections(nc, d, t)
            scan(nc, d, t)
            ffn = whole.enter_context(ExitStack())
            t["h2_hi"], t["h2_lo"] = keep(ffn, "h2_hi", [P, KD, SEQ], F32R), keep(ffn, "h2_lo", [P, KD, SEQ], F32R)
            with ExitStack() as st:
                t["x1"] = keep(st, "x1", [P, KD, SEQ])
                mixer_out(nc, d, t)
                norm_x1(nc, d, t)
        ffn_up(nc, d, t)
        ffn.close()
        ffn_down(nc, d, t)
        with ExitStack() as st:
            t["h3_hi"], t["h3_lo"] = keep(st, "h3_hi", [P, KD, SEQ], F32R), keep(st, "h3_lo", [P, KD, SEQ], F32R)
            with ExitStack() as inner:
                t["x3"] = keep(inner, "x3", [P, KD, SEQ])
                norm_x3(nc, d, t)
            attention(nc, d, t)
        output(nc, d, t)


def norm_x1(nc, d, t):
    with ExitStack() as st:
        stored = Sems(nc, st, "n1_")("stored")
        with nc.Block() as block:
            @block.sync
            def _(sp):
                sp.dma_start(d["x1s"], t["x1"]).then_inc(stored, 16)
                sp.wait_ge(stored, 16)
        gain = lambda g: nc.vector.scalar_tensor_tensor(out=g, in0=t["mod"][:, 0, 32:40], scalar=1.0, in1=t["v_norm2_g"],
                                                        op0=ALU.add, op1=ALU.mult)
        rms(nc, t, "n1", t["x1"], t["x1"], (t["h2_hi"], t["h2_lo"]), gain, t["mod"][:, 0, 24:32])


def norm_x3(nc, d, t):
    with ExitStack() as st:
        loaded = Sems(nc, st, "n2_")("loaded")
        with nc.Block() as block:
            @block.sync
            def _(sp):
                sp.dma_start(t["x3"], d["x2s"]).then_inc(loaded, 16)
                sp.wait_ge(loaded, 16)
        rms(nc, t, "n2", t["x3"], t["x3"], None, lambda g: nc.vector.tensor_copy(g, t["v_final_g"]), None, d["x3s"])
        rms(nc, t, "n3", t["x3"], t["x3"], (t["h3_hi"], t["h3_lo"]), lambda g: nc.vector.tensor_copy(g, t["v_norm_g_2"]), None)


def constants():
    row, col = np.arange(P)[:, None], np.arange(P)[None, :]
    s, u = (np.arange(P) % C)[:, None], np.arange(C)[None, :]
    tri = lambda keep: keep.astype(np.float32)
    parts = {"ident": np.eye(P), "ones": np.ones((P, P)), "headones": tri(row // HEAD == col // HEAD), "identc": tri(s == u),
             "negcausal": -1e30 * tri(col > row), "negstrict": -1e30 * tri(col >= row)}
    before = [s < u, s > u]
    after = [s > u, s < u]
    head = row // HEAD
    parts["strict"] = np.concatenate([tri(b & (head == h)) for b in before for h in range(2)], 1)
    parts["incl"] = np.concatenate([tri(b | (s == u)) for b in before], 1)
    block = lambda m: s // m == u // m
    parts["mask_u1"] = np.concatenate([-tri(b & block(2)) for b in before], 1)
    parts["mask_lev"] = np.concatenate([tri(a & block(2 ** (l + 2)) & ~block(2 ** (l + 1))) for a in after for l in range(LEVELS)], 1)
    first = np.tile(np.arange(C), BANK // C)[None, :]
    parts["reset"] = np.concatenate([np.repeat(tri(first != e), P, 0) for e in (0, C - 1)], 1)
    win = np.array([[2] * HEAD + [4] * HEAD, [8] * HEAD + [16] * HEAD]).T[:, :, None]
    parts["invcount"] = (1.0 / np.minimum(np.arange(16)[None, None, :] + 1, win)).reshape(P, 32)
    parts["invwin"] = (1.0 / win).reshape(P, 2)
    return np.concatenate([parts[n].astype(np.float32) for n in CONS], 1)


def kernel(**a):
    import concourse.bacc as bacc
    from concourse.bass_utils import run_bass_kernel_spmd

    a = {n: np.asarray(x) for n, x in a.items()}

    def tiles(w):
        return w.reshape(w.shape[0] // P, P, w.shape[1] // P, P).transpose(2, 1, 0, 3)

    def turns(w, order):
        w = tiles(w)
        return np.ascontiguousarray(w[np.array(order)].transpose(0, 2, 1, 3, 4))

    def column(v):
        return v.reshape(-1, P).T

    def featmajor(x):
        return np.ascontiguousarray(x.T.reshape(KD, P, x.shape[0]).transpose(1, 0, 2))

    w0a0 = np.stack([a["rw_w0"][0], a["rw_a0"][0]], 1)
    vec = {"norm1_g": column(a["norm1_g"][0]), "norm2_g": column(a["norm2_g"][0]), "final_g": column(a["final_g"]),
           "norm_g_2": column(a["norm_g_2"][0]), "ada_b": column(a["ada_b"][0]), "conv_a_w": column(a["conv_a_w"][0]),
           "w0a0": column(w0a0), "k_k": column(a["rw_k_k"][0]), "k_a": column(a["rw_k_a"][0]), "r_k": column(a["rw_r_k"][0]),
           "ln_g": column(a["rw_ln_g"][0]), "ln_b": column(a["rw_ln_b"][0]), "ffn_conv_w": column(a["ffn_conv_w"][0]),
           "ffn_conv_b": column(a["ffn_conv_b"][0]), "pool_scale": column(a["pool_scale_2"][0]),
           "cc": np.stack([column(a["c"][0]), column(a["c_ctx"])], 2).reshape(P, 16),
           "qg": np.tile(a["q_norm_g_2"][0], 2)[:, None], "kg": np.tile(a["k_norm_g_2"][0], 2)[:, None],
           "b_f": np.pad(a["b_f_2"][0], (0, P - 8))[:, None]}
    w_in = a["w_in"][0]
    w2 = a["w_in_2"][0]
    at = 4 * CH
    ff = np.pad(w2[:, at:at + 8], ((0, 0), (0, P - 8)))
    w2 = np.concatenate([w2[:, 0:at], w2[:, at + 8:], ff], 1)
    FF, Z = 28, 28
    given = {
        "vecs": np.concatenate([vec[n] for n in VECS], 1), "consts": constants(),
        "xT": featmajor(a["x"][0]), "ctxT": featmajor(a["ctx"][0]),
        "ada": turns(a["ada_w"][0], np.arange(48).reshape(24, 2)),
        "w1": np.ascontiguousarray(tiles(w_in)[np.array([24, 25] + [n + j for j in range(PAIRS) for n in (20, 16, 12)]
                                                        + [n + j for j in range(4) for n in (4, 8, 0)])]),
        "lora": np.concatenate([a["rw_w_up"][0], a["rw_a_up"][0]], 1).reshape(2, P, PAIRS, P).transpose(2, 1, 0, 3),
        "g_up": a["rw_g_up"][0],
        "w_out": turns(a["w_out"][0], np.arange(8).reshape(4, 2)),
        "w_ffn": turns(a["ffn_w_up"][0], [[i, NFF + i] for i in range(NFF)]),
        "w_down": tiles(a["ffn_w_down"][0]),
        "w2": turns(w2, [[FF, 16, 18, Z], [17, 19, Z, Z]] + [[p, 4 + p, 8 + p, 12 + p] for p in range(4)]
                    + [[20 + p, 22 + p, 24 + p, 26 + p] for p in range(2)]),
        "w_pool": a["w_pool_2"][0], "w_out_2": turns(a["w_out_2"][0], np.arange(8).reshape(4, 2)),
    }
    nc = bacc.Bacc("TRN2", target_bir_lowering=False, num_devices=1)
    program(nc)
    got = run_bass_kernel_spmd(nc, [{n: np.ascontiguousarray(x) for n, x in given.items()}], core_ids=[0])
    out = got.results[0]["out"]
    return np.ascontiguousarray(out.reshape(D, SEQ).T)[None]
```

```python
import numpy as np
import concourse.bass as bass
import concourse.mybir as mybir
from contextlib import ExitStack

F32 = mybir.dt.float32
F32R = mybir.dt.float32r
ALU = mybir.AluOpType
ACT = mybir.ActivationFunctionType

P = 128
D = 1024
KD = D // P
SEQ, CTX = 1024, 256
TOK = CTX + SEQ
HEAD = 64
CH = 512
PAIRS = CH // P
NFF = 22
GRID_W = 64
GRID_H = SEQ // GRID_W
C = 64
NCTX, NSEQ = CTX // C, SEQ // C
STEPS = NCTX + NSEQ
SLOTS = STEPS + NCTX
LEVELS = 5
DECAY_SCALE = float(np.exp(-0.5))
RMS_EPS, GN_EPS = 1e-6, 64e-5
BANK = 512

VECS = {}
_at = 0
for _name, _n in (("norm1_g", 8), ("norm2_g", 8), ("final_g", 8), ("norm_g_2", 8), ("ada_b", 48),
                  ("conv_a_w", 12), ("w0a0", 16), ("k_k", 4), ("k_a", 4), ("r_k", 4), ("ln_g", 4),
                  ("ln_b", 4), ("ffn_conv_w", 9 * NFF), ("ffn_conv_b", NFF), ("pool_scale", 2),
                  ("cc", 16), ("qg", 1), ("kg", 1), ("b_f", 1)):
    VECS[_name] = (_at, _n)
    _at += _n
NVEC = _at

CONS = {}
_at = 0
for _name, _n in (("ident", P), ("ones", P), ("headones", P), ("negcausal", P),
                  ("negstrict", P), ("strict", 2 * 2 * C), ("incl", 2 * C),
                  ("mask_u1", 2 * 2 * C), ("mask_lev", 2 * LEVELS * C), ("reset", 2 * BANK),
                  ("invcount", 2 * 16), ("invwin", 2)):
    CONS[_name] = (_at, _n)
    _at += _n
NCON = _at


def bc(ap, axis, n):
    shape = list(ap.shape)
    return ap.unsqueeze(axis).broadcast_to(shape[:axis] + [n] + shape[axis:])


class Sems:

    def __init__(self, nc, stack, prefix):
        self.nc, self.prefix, self.known = nc, prefix, {}
        stack.callback(self.close)

    def __call__(self, name):
        if name not in self.known:
            self.known[name] = self.nc.alloc_semaphore(name=self.prefix + name)
        return self.known[name]

    def close(self):
        self.nc.clear_and_free_semaphores(list(self.known.values()))
        self.nc.all_engine_barrier()


def hold(eng, gate, sem, value):
    if isinstance(value, int) and value <= 0:
        return
    eng.wait_ge(sem, value)
    if not isinstance(value, int):
        eng.sem_inc(gate, 1)


def held(eng, value):
    return value if isinstance(value, int) else eng.snap(value)


def product(nc, out, w_hi, w_lo, x_hi, x_lo, nk, cols):
    for k in range(nk):
        for n, (w, x) in enumerate(((w_hi, x_hi), (w_hi, x_lo), (w_lo, x_hi))):
            last = nc.tensor.matmul(out, w[:, k, :], x[:, k, cols], start=(k == 0 and n == 0),
                                    stop=(k == nk - 1 and n == 2))
    return last


def prologue(nc, d, t):
    groups = [(0, CTX, 1), (CTX, BANK, 0), (CTX + BANK, BANK, 0)]
    NADA = 2
    GADA = 16 // NADA
    SLOTS_ADA = 3
    KPOOL = 3
    with ExitStack() as st:
        sem = Sems(nc, st, "a_")
        sb = lambda n, s, dt=F32: st.enter_context(nc.sbuf_tensor("a_" + n, s, dt))
        xin = sb("xin", [P, KD, TOK])
        tmp = sb("tmp", [P, KD, TOK])
        rstd = sb("rstd", [P, TOK])
        adaw = sb("adaw", [P, SLOTS_ADA, NADA, KD, P])
        silu_c = t["silu_c"]
        gain = sb("gain", [P, 2, KD])
        ps = [st.enter_context(nc.psum_tensor(f"a_ps{n}", [P, BANK], F32)) for n in range(4)]
        modps = ps[3][:, 0:32].rearrange("p (n c) -> p n c", c=2)
        vec, con = t["vec"], t["con"]
        block = st.enter_context(nc.Block())

        @block.sync
        def _(sp):
            sp.dma_start(vec, d["vecs"]).then_inc(sem("vecs"), 16)
            sp.dma_start(con, d["consts"]).then_inc(sem("consts"), 16)
            sp.dma_start(xin[:, :, 0:CTX], d["ctxT"]).then_inc(sem("x0"), 16)

            def load_ada(i):
                if i >= SLOTS_ADA:
                    sp.wait_ge(sem(f"ada_used{i % SLOTS_ADA}"), i // SLOTS_ADA)
                sp.dma_start(adaw[:, i % SLOTS_ADA], d["ada"][i]).then_inc(sem(f"ada{i % SLOTS_ADA}"), 16)

            for i in range(GADA):
                load_ada(i)
                if i in (1, 2):
                    sp.dma_start(xin[:, :, CTX + BANK * (i - 1):CTX + BANK * i],
                                 d["xT"][:, :, BANK * (i - 1):BANK * i]).then_inc(sem(f"x{i}"), 16)
            sp.dma_start(t["raw_in"], d["w1"][0]).then_inc(t["ahead"]("in"), 16)

        @block.tensor
        def _(pe):
            pe.wait_ge(sem("consts"), 16)
            pe.wait_ge(sem("silu_c"), 1)

            def sums(g):
                at, n, _ = groups[g]
                pe.wait_ge(sem("squares"), g + 1)
                for k in range(KD):
                    mm = nc.tensor.matmul(ps[g][:, 0:n], t["c_ones"], tmp[:, k, at:at + n],
                                          start=(k == 0), stop=(k == KD - 1))
                mm.then_inc(sem("sumsq"), 1)

            for i in range(GADA):
                pe.wait_ge(sem(f"ada{i % SLOTS_ADA}"), 16 * (i // SLOTS_ADA + 1))
                for m in range(NADA):
                    for k in range(KD):
                        mm = nc.tensor.matmul(modps[:, i * NADA + m, :], adaw[:, i % SLOTS_ADA, m, k, :],
                                              silu_c[:, k, :], start=(k == 0), stop=(k == KD - 1))
                mm.then_inc(sem(f"ada_used{i % SLOTS_ADA}"), 1)
                if i in (1, 3, 5):
                    sums(i // 2)

        @block.scalar
        def _(act):
            act.wait_ge(sem("vecs"), 16)
            nc.scalar.activation(silu_c, t["v_cc"].rearrange("p (k c) -> p k c", c=2),
                                 ACT.Silu).then_inc(sem("silu_c"), 1)
            for g, (at, n, _) in enumerate(groups):
                act.wait_ge(sem(f"x{g}"), 16)
                nc.scalar.activation(tmp[:, :, at:at + n], xin[:, :, at:at + n],
                                     ACT.Square).then_inc(sem("squares"), 1)
            act.wait_ge(sem("eps"), 2)
            for g, (at, n, _) in enumerate(groups):
                act.wait_ge(sem("sumsq"), g + 1)
                nc.scalar.activation(rstd[:, at:at + n], ps[g][:, 0:n], ACT.Sqrt, scale=1.0 / D,
                                     bias=t["c_eps"]).then_inc(sem("std"), 1)
            for g, (at, n, c) in enumerate(groups):
                act.wait_ge(sem("full"), g + 1)
                nc.scalar.activation(t["h_hi"][:, :, at:at + n], tmp[:, :, at:at + n],
                                     ACT.Copy).then_inc(sem("hi"), 1)

        @block.vector
        def _(dve):
            nc.vector.memset(t["c_eps"], RMS_EPS).then_inc(sem("eps"), 1)
            nc.vector.memset(t["c_gneps"], GN_EPS).then_inc(sem("eps"), 1)
            for g, (at, n, _) in enumerate(groups):
                dve.wait_ge(sem("std"), g + 1)
                nc.vector.reciprocal(rstd[:, at:at + n], rstd[:, at:at + n]).then_inc(sem("rstd"), 1)
                dve.wait_ge(sem("rstd"), g + 1)
                nc.vector.tensor_tensor(tmp[:, :, at:at + n], xin[:, :, at:at + n], bc(rstd[:, at:at + n], 1, KD),
                                        ALU.mult).then_inc(sem("normed"), 1)
            last = GADA - 1
            dve.wait_ge(sem(f"ada_used{last % SLOTS_ADA}"), last // SLOTS_ADA + 1)
            for c in range(2):
                nc.vector.tensor_tensor(t["mod"][:, c, 0:16], modps[:, :, c], t["v_ada_b"][:, 0:16],
                                        ALU.add).then_inc(sem("mod"), 1)
            dve.wait_ge(sem("mod"), 2)
            for c in range(2):
                g = nc.vector.scalar_tensor_tensor(out=gain[:, c], in0=t["mod"][:, c, 8:16], scalar=1.0,
                                                   in1=t["v_norm1_g"], op0=ALU.add, op1=ALU.mult)
            g.then_inc(sem("gain"), 1)
            dve.wait_ge(sem("gain"), 1)
            dve.wait_ge(sem("normed"), len(groups))

            def full(g):
                at, n, c = groups[g]
                for k in range(KD):
                    a = nc.vector.tensor_scalar(tmp[:, k, at:at + n], tmp[:, k, at:at + n], gain[:, c, k:k + 1], t["mod"][:, c, k:k + 1],
                                                ALU.mult, ALU.add)
                a.then_inc(sem("full"), 1)

            full(0)
            for g, (at, n, _) in enumerate(groups):
                if g + 1 < len(groups):
                    full(g + 1)
                dve.wait_ge(sem("hi"), g + 1)
                nc.vector.tensor_tensor(t["h_lo"][:, KPOOL:KD, at:at + n], tmp[:, KPOOL:KD, at:at + n],
                                        t["h_hi"][:, KPOOL:KD, at:at + n].bitcast(F32), ALU.subtract).then_inc(sem("lo"), 1)

        @block.gpsimd
        def _(pool):
            for g, (at, n, _) in enumerate(groups):
                pool.wait_ge(sem("hi"), g + 1)
                nc.gpsimd.tensor_tensor(t["h_lo"][:, 0:KPOOL, at:at + n], tmp[:, 0:KPOOL, at:at + n],
                                        t["h_hi"][:, 0:KPOOL, at:at + n].bitcast(F32), ALU.subtract).then_inc(sem("lo_pool"), 1)


def projections(nc, d, t):
    NADA = 2
    GROUPS = [(0, CTX), (CTX, BANK), (CTX + BANK, BANK)]
    JOBS = [(g, x) for g in range(3) for x in range(2)]
    NJ = len(JOBS)
    FIRST, PER_TURN = 5, 8
    CC, CX, CB = 0, 1, 2
    V, K, R = 0, 1, 2
    ADA_TURN = 2
    with ExitStack() as st:
        sem = Sems(nc, st, "b_")
        sb = lambda n, s, dt=F32: st.enter_context(nc.sbuf_tensor("b_" + n, s, dt))
        raw = t["raw_in"]
        w_hi, w_lo = sb("w_hi", [P, 3, KD, P], F32R), sb("w_lo", [P, 3, KD, P], F32R)
        adaw = sb("adaw", [P, NADA, KD, P])
        wa = sb("wa", [P, TOK])
        lora = sb("lora", [P, 2, P])
        bias = sb("bias", [P, 4])
        ka1 = sb("ka1", [P, PAIRS])
        r, k, v, kk, sq = (sb(n, [P, TOK]) for n in ("r", "k", "v", "kk", "sq"))
        rn = sq
        rkk = sb("rkk", [P, SEQ])
        vt = sb("vt", [P, TOK // P, P])
        th = sb("th", [P, 2, 2, BANK])
        cum = sb("cum", [P, 2, BANK])
        pinv = sb("pinv", [P, 2, BANK])
        kd = sb("kd", [P, 2, BANK])
        ops = sb("ops", [P, 2, 4, BANK])
        gcc, u, y = v[:, 0:SEQ], sq[:, 0:SEQ + 2], r[:, 0:SEQ]
        ps = [st.enter_context(nc.psum_tensor(f"b_ps{n}", [P, BANK], F32)) for n in range(8)]
        PS_HEADS, PS_W, PS_A, PS_ADA = 4, 5, 6, 7
        PS_BONUS = (PS_HEADS, (FIRST + PER_TURN - 1) % 4)
        PS_CC, PS_CX, PS_CB = (1, 2), (3, PS_BONUS[1]), (PS_HEADS, PS_W)
        gate = {n: sem("passed_" + n) for n in ("pe", "sp", "act", "dve", "pool")}
        h_hi, h_lo = t["h_hi"], t["h_lo"]
        conv_w, k_k, r_k, k_a = t["v_conv_a_w"], t["v_k_k"], t["v_r_k"], t["v_k_a"]
        cols = lambda g: slice(GROUPS[g][0], GROUPS[g][0] + GROUPS[g][1])
        seq = lambda g: slice(BANK * (g - 1), BANK * g)
        dense_at = lambda n, j: n * PER_TURN + (FIRST + j)
        bank_of = lambda j: (FIRST + j) % 4
        DENSE = [(V, 0), (V, 1), (V, 2), (K, 0), (K, 1), (K, 2), (R, 1), (R, 2)]
        ALL = FIRST + PAIRS * PER_TURN
        block = st.enter_context(nc.Block())

        tanh_before = lambda m, j: m * NJ + (j + 1)
        made_at = lambda m, j: m * NJ + (j + 3)
        job = lambda m, j: m * NJ + (j + 1)

        @block.sync
        def _(sp):
            def wait(s, value):
                hold(sp, gate["sp"], s, value)

            def load_w(tile):
                wait(sem("lo"), tile)
                sp.dma_start(raw, d["w1"][tile]).then_inc(sem("raw"), 16)

            def store_job(m, j):
                g, x = JOBS[j]
                at, n = GROUPS[g]
                s0 = at // C if g or x == 0 else STEPS
                wait(sem("made"), made_at(m, j))
                sp.dma_start(d["ops"][x, :, m, :, s0 * C:s0 * C + n].rearrange("a p c -> p a c"),
                             ops[:, j % 2, :, 0:n]).then_inc(sem(f"ops_stored{j % 2}"), 16)

            def store_bonus(m):
                wait(sem("bonus"), m * 2 + 2)
                sp.dma_start(d["mixd"][:, m + PAIRS], rkk[:]).then_inc(sem("bonus_stored"), 16)

            def store_vt(m):
                wait(sem("vt"), m * 3 + 3)
                for c in range(2):
                    for h in range(2):
                        rows, heads = slice(C * c, C * c + C), slice(HEAD * h, HEAD * h + HEAD)
                        for s0, n in ((0, STEPS), (STEPS, NCTX)):
                            dst = d["vts"][s0:s0 + n, heads, m, :].rearrange("(j c) s v -> c s j v", c=2)[c]
                            sp.dma_start(dst, vt[rows, 0:n // 2, heads]).then_inc(sem("vt_stored"), 16)

            def store_conv(c):
                wait(sem("conv_out"), c * 2 + 2)
                sp.dma_start(d["mixd"][:, c], y).then_inc(sem("conv_stored"), 16)

            def pair_turn(n, jobs):
                m = held(nc.sync, n - 1)
                load_w(n * 3 + 5)
                if jobs:
                    store_bonus(m)
                if jobs:
                    for j in range(4):
                        store_job(m, j)
                load_w(n * 3 + 6)
                if jobs:
                    for j in range(4, NJ):
                        store_job(m, j)
                store_vt(n)
                wait(sem("p_lora"), n * NJ)
                sp.dma_start(lora[:], d["lora"][n]).then_inc(sem("lora"), 16)
                load_w(n * 3 + 7)

            for tile in range(1, 5):
                load_w(tile)
                if tile == 3:
                    sp.wait_ge(sem("sg"), 2)
                    sp.dma_start(d["sgs"], sq[:, 0:SEQ]).then_inc(sem("sg_stored"), 16)
            pair_turn(0, False)
            with nc.sync.Fori(1, PAIRS) as n:
                pair_turn(n, True)
            tile = 2 + 3 * (PAIRS + 1)
            load_w(tile)
            store_bonus(PAIRS - 1)
            for j in range(3):
                store_job(PAIRS - 1, j)
            load_w(tile + 1)
            for j in range(3, NJ):
                store_job(PAIRS - 1, j)
            load_w(tile + 2)
            store_conv(0)
            with nc.sync.Fori(1, 3) as c:
                for i in range(3):
                    load_w(held(nc.sync, c * 3 + (tile + i)))
                store_conv(c)
            store_conv(3)
            sp.wait_ge(sem("sg_stored"), 16)
            for j in range(2):
                sp.wait_ge(sem(f"ops_stored{j}"), 16 + 16 * NJ // 2 * PAIRS)
            sp.wait_ge(sem("vt_stored"), 128 * PAIRS)
            sp.wait_ge(sem("bonus_stored"), 16 * PAIRS)
            sp.wait_ge(sem("conv_stored"), 16 * 4)

        @block.tensor
        def _(pe):
            def wait(s, value):
                hold(pe, gate["pe"], s, value)

            def weights(slot, tile):
                wait(sem("hi"), tile + 1)
                wait(sem("lo"), tile + 1)

            def dense(bank, slot, g, done):
                at, n = GROUPS[g]
                return product(nc, ps[bank][:, 0:n], w_hi[:, slot], w_lo[:, slot], h_hi, h_lo, KD,
                               cols(g)).then_inc(done, 1)

            def modulation(n):
                wait(sem("ada"), n * 16 + 16)
                wait(sem("ada_read"), n)
                for m in range(NADA):
                    for q in range(KD):
                        mm = nc.tensor.matmul(ps[PS_ADA][:, 2 * m:2 * m + 2], adaw[:, m, q, :], t["silu_c"][:, q, :],
                                              start=(q == 0), stop=(q == KD - 1))
                mm.then_inc(sem("ada_used"), 1)

            def low_rank(m, j):
                g, x = JOBS[j]
                n = GROUPS[g][1]
                wait(sem("lora"), m * 16 + 16)
                wait(sem("tanh"), tanh_before(m, j))
                if j == 0:
                    wait(sem("norm"), m * 3 + 3)
                nc.tensor.matmul(ps[PS_W][:, 0:n], lora[0:C, x], wa[0:C, cols(g)], start=True, stop=True)
                nc.tensor.matmul(ps[PS_A][:, 0:n], lora[C:P, x], wa[C:P, cols(g)], start=True,
                                 stop=True).then_inc(sem("p_lora"), 1)

            def bonus_sums(n):
                wait(sem("rkk"), n + 1)
                wait(sem("norm"), n * 3 + 1)
                for g in range(2):
                    nc.tensor.matmul(ps[PS_BONUS[g]][:], t["c_headones"], rkk[:, BANK * g:BANK * (g + 1)], start=True,
                                     stop=True).then_inc(sem("p_bonus"), 1)

            def turn_v(n, g):
                wait(sem("dense_read"), dense_at(n, g + 1))
                wait(sem("bonus"), n * 2)
                wait(sem("vt"), n * 3 + g)
                at, m = GROUPS[g]
                for b in range(m // P):
                    mm = nc.tensor.transpose(ps[PS_HEADS][:, P * b:P * (b + 1)], v[:, at + P * b:at + P * (b + 1)],
                                             t["c_ident"])
                mm.then_inc(sem("p_vt"), 1)

            def norm_sums(n):
                wait(sem("sq"), n + 1)
                wait(sem("vt"), n * 3 + 3)
                wait(sem("tanh"), tanh_before(n, 0))
                for g, (at, m) in enumerate(GROUPS):
                    nc.tensor.matmul(ps[PS_HEADS + g][:, 0:m], t["c_headones"], sq[:, cols(g)], start=True,
                                     stop=True).then_inc(sem("p_norms"), 1)

            def pair_turn(n, jobs):
                m = held(nc.tensor, n - 1)
                for j, (slot, g) in enumerate(DENSE):
                    if jobs and j < NJ:
                        low_rank(m, j)
                    weights(slot, n * 3 + (2 + slot))
                    wait(sem("dense_read"), dense_at(n, j - 3))
                    if jobs and j == 3:
                        wait(sem("bonus"), n * 2)
                    dense(bank_of(j), slot, g, sem("dense"))
                    if j in (3, 7):
                        modulation(n * ADA_TURN + j // 4)
                    if 3 <= j < 6:
                        turn_v(n, j - 3)
                    if j == 6:
                        norm_sums(n)
                bonus_sums(n)

            def conv_turn(c, jobs):
                for slot, g, banks, read in ((CC, 1, PS_CC[0], "cc_read"), (CC, 2, PS_CC[1], "cc_read"),
                                             (CX, 1, PS_CX[0], "cx_read"), (CX, 2, PS_CX[1], "cx_read"), (CB, 1, PS_CB[0], "conv_out"), (CB, 2, PS_CB[1], "conv_out")):
                    if jobs:
                        low_rank(PAIRS - 1, 2 * slot + g - 1)
                    weights(slot, c * 3 + (2 + 3 * PAIRS + slot))
                    wait(sem(read), c * 2 - (2 - g))
                    if jobs and (slot, g) == (CX, 2):
                        wait(sem("bonus"), PAIRS * 2)
                    if jobs and (slot, g) == (CB, 2):
                        wait(sem("tanh"), tanh_before(PAIRS, 0))
                    dense(banks, slot, g, sem(("p_cc", "p_cx", "p_cb")[slot]))
                    if g == 2 and slot != CX:
                        modulation((c + PAIRS) * ADA_TURN + slot // 2)

            for j, (slot, g) in enumerate(((0, 0), (0, 1), (0, 2), (1, 1), (1, 2))):
                weights(slot, slot)
                wait(sem("dense_read"), j - 3)
                dense(j % 4, slot, g, sem("dense"))
            pe.wait_ge(sem("wa"), 4)
            pair_turn(0, False)
            with nc.tensor.Fori(1, PAIRS) as n:
                pair_turn(n, True)
            pe.wait_ge(sem("dense_read"), ALL)
            conv_turn(0, True)
            with nc.tensor.Fori(1, 4) as c:
                conv_turn(c, False)

        @block.scalar
        def _(act):
            def wait(s, value):
                hold(act, gate["act"], s, value)

            def hi(slot, tile):
                if isinstance(tile, int) and tile == 0:
                    act.wait_ge(t["ahead"]("in"), 16)
                else:
                    wait(sem("raw"), tile * 16)
                nc.scalar.activation(w_hi[:, slot], raw, ACT.Copy).then_inc(sem("hi"), 1)

            def read(n, j):
                slot, g = DENSE[j]
                wait(sem("dense"), dense_at(n, j + 1))
                nc.scalar.activation((v, k, r)[slot][:, cols(g)], ps[bank_of(j)][:, 0:GROUPS[g][1]],
                                     ACT.Copy).then_inc(sem("dense_read"), 1)

            def read_vt(n, g):
                at, m = GROUPS[g]
                wait(sem("p_vt"), n * 3 + (g + 1))
                nc.scalar.activation(vt[:, at // P:(at + m) // P].rearrange("p j c -> p (j c)"), ps[PS_HEADS][:, 0:m],
                                     ACT.Copy).then_inc(sem("vt"), 1)

            def tanhs(m, j):
                g, x = JOBS[j]
                n = GROUPS[g][1]
                wait(sem("p_lora"), job(m, j))
                wait(sem("bias"), m + 1)
                wait(sem("made"), made_at(m, j - 2))
                for w, bank in ((0, PS_W), (1, PS_A)):
                    a = nc.scalar.activation(th[:, j % 2, w, 0:n], ps[bank][:, 0:n], ACT.Tanh, scale=0.5,
                                             bias=bias[:, 2 * x + w:2 * x + w + 1])
                a.then_inc(sem("tanh"), 1)

            def powers(m, j):
                g, x = JOBS[j]
                s, n = j % 2, GROUPS[g][1]
                wait(sem("cum"), job(m, j))
                nc.scalar.activation(pinv[:, s, 0:n], cum[:, s, 0:n], ACT.Exp, scale=DECAY_SCALE)
                wait(sem("cex"), job(m, j))
                nc.scalar.activation(cum[:, s, 0:n], cum[:, s, 0:n], ACT.Exp, scale=-DECAY_SCALE)
                nc.scalar.activation(th[:, s, 0, 0:n], th[:, s, 0, 0:n], ACT.Exp, scale=-DECAY_SCALE).then_inc(sem("powers"), 1)

            def load_ada(n):
                wait(sem("ada_used"), n)
                nc.scalar.dma_start(adaw[:], d["ada"][held(nc.scalar, n + 8)]).then_inc(sem("ada"), 16)

            def pair_turn(n, jobs):
                m = held(nc.scalar, n - 1)
                if jobs:
                    tanhs(m, 0)
                for j in range(6):
                    if j == 0 and jobs:
                        wait(sem("bonus"), n * 2)
                    if j == 0:
                        wait(sem("vt_stored"), n * 128)
                    if j >= 4:
                        read_vt(n, j - 4)
                    if jobs and j + 1 < NJ:
                        tanhs(m, j + 1)
                    if jobs:
                        powers(m, j)
                    if j >= 3 and jobs:
                        wait(sem("made"), made_at(m, 2 * j - 5))
                    read(n, j)
                    if j == 2:
                        hi(V, n * 3 + 5)
                    if j == 4:
                        load_ada(n * ADA_TURN + 1)
                read_vt(n, 2)
                hi(K, n * 3 + 6)
                read(n, 6)
                for g in range(3):
                    wait(sem("p_norms"), n * 3 + (g + 1))
                    nc.scalar.activation(rn[:, cols(g)], ps[PS_HEADS + g][:, 0:GROUPS[g][1]], ACT.Sqrt).then_inc(sem("norm"), 1)
                read(n, 7)
                hi(R, n * 3 + 7)
                load_ada(n * ADA_TURN + 2)

            def conv_turn(c, last):
                wait(sem("cx_read"), c * 2)
                for g in (1, 2):
                    wait(sem("p_cc"), c * 2 + g)
                    nc.scalar.activation(gcc[:, seq(g)], ps[PS_CC[g - 1]][:], ACT.Copy).then_inc(sem("cc_read"), 1)
                for slot, done in () if last == "alone" else ((CC, "p_cc"), (CX, "p_cx"), (CB, "p_cb")):
                    wait(sem(done), c * 2 + 2)
                    if slot == CX:
                        load_ada((c + PAIRS) * ADA_TURN + 1)
                    if not last:
                        hi(slot, c * 3 + (5 + 3 * PAIRS + slot))
                if not last:
                    load_ada((c + PAIRS) * ADA_TURN + 2)

            act.sem_inc(sem("tanh"), 1)
            load_ada(0)
            for tile in range(2):
                hi(tile, tile)
            for g, (at, n) in enumerate(GROUPS):
                act.wait_ge(sem("dense"), g + 1)
                nc.scalar.activation(wa[0:C, cols(g)], ps[g][0:C, 0:n], ACT.Tanh)
                nc.scalar.activation(wa[C:P, cols(g)], ps[g][C:P, 0:n], ACT.Copy).then_inc(sem("dense_read"), 1)
            act.sem_inc(sem("wa"), 1)
            hi(V, 2)
            for g, bank in ((1, 3), (2, 0)):
                act.wait_ge(sem("dense"), 3 + g)
                nc.scalar.activation(sq[:, seq(g)], ps[bank][:], ACT.Sigmoid).then_inc(sem("dense_read"), 1)
            act.wait_ge(sem("dense_read"), FIRST)
            act.sem_inc(sem("sg"), 2)
            act.sem_inc(sem("wa"), 3)
            hi(K, 3)
            hi(R, 4)
            pair_turn(0, False)
            with nc.scalar.Fori(1, PAIRS) as n:
                pair_turn(n, True)
            m = PAIRS - 1
            tanhs(m, 0)
            tanhs(m, 1)
            powers(m, 0)
            tanhs(m, 2)
            powers(m, 1)
            act.wait_ge(sem("bonus"), 2 * PAIRS)
            act.wait_ge(sem("vt_stored"), 128 * PAIRS)
            for j in range(2, NJ):
                if j + 1 < NJ:
                    tanhs(m, j + 1)
                powers(m, j)
                if j == 3:
                    conv_turn(0, "alone")
            for slot, done in ((CC, "p_cc"), (CX, "p_cx"), (CB, "p_cb")):
                act.wait_ge(sem(done), 2)
                if slot == CX:
                    load_ada(PAIRS * ADA_TURN + 1)
                hi(slot, 5 + 3 * PAIRS + slot)
            load_ada(PAIRS * ADA_TURN + 2)
            with nc.scalar.Fori(1, 3) as c:
                conv_turn(c, False)
            conv_turn(3, True)

        @block.gpsimd
        def _(pool):
            TT, TS = nc.gpsimd.tensor_tensor, nc.gpsimd.tensor_scalar

            def wait(s, value):
                hold(pool, gate["pool"], s, value)

            def lo(slot, tile):
                wait(sem("hi"), tile + 1)
                TT(w_lo[:, slot], raw, w_hi[:, slot].bitcast(F32), ALU.subtract).then_inc(sem("lo"), 1)

            def sigmoids(m, j):
                s, n = j % 2, GROUPS[JOBS[j][0]][1]
                wait(sem("tanh"), tanh_before(m, j + 1))
                TS(th[:, s, :, 0:n], th[:, s, :, 0:n], 0.5, 0.5, ALU.mult, ALU.add).then_inc(sem("sig"), 1)

            def parts(m, j):
                g, x = JOBS[j]
                s, (at, n) = j % 2, GROUPS[g]
                wait(sem("cum"), job(m, j))
                TT(th[:, s, 0, 0:n], cum[:, s, 0:n], th[:, s, 0, 0:n], ALU.subtract).then_inc(sem("cex"), 1)
                wait(sem("kk"), m * 3 + (g + 1))
                wait(sem("km"), job(m, j))
                TT(th[:, s, 1, 0:n], th[:, s, 1, 0:n], kk[:, cols(g)], ALU.mult).then_inc(sem("b"), 1)

            def jobs_of(m, splits):
                sigmoids(m, 0)
                for j in range(NJ):
                    if j + 1 < NJ:
                        sigmoids(m, j + 1)
                    parts(m, j)
                    if j in splits:
                        lo(*splits[j])

            for slot, tile in ((0, 0), (1, 1), (V, 2), (K, 3), (R, 4), (V, 5), (K, 6), (R, 7)):
                lo(slot, tile)
            with nc.gpsimd.Fori(1, PAIRS) as n:
                jobs_of(nc.gpsimd.snap(n - 1), {3: (V, n * 3 + 5)})
                lo(K, n * 3 + 6)
                lo(R, n * 3 + 7)
            jobs_of(PAIRS - 1, {})
            with nc.gpsimd.Fori(0, 3) as c:
                for slot in range(3):
                    lo(slot, c * 3 + (5 + 3 * PAIRS + slot))

        @block.vector
        def _(dve):
            TT, TS, STT = nc.vector.tensor_tensor, nc.vector.tensor_scalar, nc.vector.scalar_tensor_tensor

            def wait(s, value):
                hold(dve, gate["dve"], s, value)

            def modulation(n):
                wait(sem("ada_used"), n + 1)
                at = held(nc.vector, n * NADA + 16)
                TT(t["mod"][:, 0, bass.ds(at, NADA)], ps[PS_ADA][:, 0:2 * NADA].rearrange("p (n c) -> p n c", c=2)[:, :, 0],
                   t["v_ada_b"][:, bass.ds(at, NADA)], ALU.add).then_inc(sem("ada_read"), 1)

            def biases(m):
                wait(sem("tanh"), tanh_before(m, 0))
                TS(bias[:].unsqueeze(2), t["v_w0a0"].rearrange("p (w q) -> p w q", q=PAIRS)[:, :, bass.ds(m, 1)], 0.5, None,
                   ALU.mult).then_inc(sem("bias"), 1)

            def bonus(m):
                for g in (1, 2):
                    wait(sem("p_bonus"), m * 2 + g)
                    TT(rkk[:, seq(g)], ps[PS_BONUS[g - 1]][:], v[:, cols(g)], ALU.mult).then_inc(sem("bonus"), 1)

            def sums(m, j):
                g, x = JOBS[j]
                s, n = j % 2, GROUPS[g][1]
                wait(sem("sig"), job(m, j))
                flat = [cum[:, s, 0:n], t["c_reset"][:, x, 0:n], th[:, s, 0, 0:n]]
                out, reset, data = flat if x == 0 else [a[:, ::-1] for a in flat]
                nc.vector.tensor_tensor_scan(out, reset, data, 0.0, ALU.mult, ALU.add).then_inc(sem("cum"), 1)
                TS(kd[:, s, 0:n], th[:, s, 1, 0:n], k_a[:, bass.ds(m, 1)], ka1[:, bass.ds(m, 1)], ALU.mult,
                   ALU.add).then_inc(sem("km"), 1)

            def products(m, j):
                g, x = JOBS[j]
                s, (at, n) = j % 2, GROUPS[g]
                wait(sem("km"), job(m, j))
                TT(kd[:, s, 0:n], kd[:, s, 0:n], k[:, cols(g)], ALU.mult).then_inc(sem("kd"), 1)
                wait(sem(f"ops_stored{j % 2}"), (m * (NJ // 2) + (j // 2 + 1)) * 16)
                wait(sem("powers"), job(m, j))
                s0 = at // C if g or x == 0 else STEPS
                TS(t["pend"][:, x, s0:s0 + n // C, bass.ds(m, 1)], cum[:, s, (C - 1, 0)[x]:n:C].unsqueeze(2), 1.0, None, ALU.mult)
                TT(ops[:, s, 0, 0:n], r[:, cols(g)], cum[:, s, 0:n], ALU.mult)
                wait(sem("kk"), m * 3 + (g + 1))
                TT(ops[:, s, 1, 0:n], kk[:, cols(g)], th[:, s, 0, 0:n], ALU.mult)
                wait(sem("b"), job(m, j))
                TT(ops[:, s, 2, 0:n], th[:, s, 1, 0:n], pinv[:, s, 0:n], ALU.mult)
                wait(sem("kd"), job(m, j))
                TT(ops[:, s, 3, 0:n], kd[:, s, 0:n], pinv[:, s, 0:n], ALU.mult).then_inc(sem("made"), 1)

            def norms(n):
                wait(sem("dense_read"), dense_at(n, 6))
                wait(sem("b"), n * NJ)
                TS(kk[:], k[:], k_k[:, bass.ds(n, 1)], None, ALU.mult).then_inc(sem("kk_raw"), 1)
                wait(sem("kk_raw"), n + 1)
                TT(sq[:], kk[:], kk[:], ALU.mult).then_inc(sem("sq"), 1)
                for g in range(3):
                    if g == 2:
                        wait(sem("dense_read"), dense_at(n, 8))
                        wait(sem("bonus_stored"), n * 16)
                        STT(out=rkk[:], in0=r[:, CTX:TOK], scalar=r_k[:, bass.ds(n, 1)], in1=k[:, CTX:TOK], op0=ALU.mult,
                            op1=ALU.mult).then_inc(sem("rkk"), 1)
                    wait(sem("norm"), n * 3 + (g + 1))
                    TS(rn[:, cols(g)], rn[:, cols(g)], 1e-12, None, ALU.max).then_inc(sem("guarded"), 1)
                    wait(sem("guarded"), n * 3 + (g + 1))
                    nc.vector.reciprocal(rn[:, cols(g)], rn[:, cols(g)]).then_inc(sem("rnorm"), 1)
                    wait(sem("rnorm"), n * 3 + (g + 1))
                    TT(kk[:, cols(g)], kk[:, cols(g)], rn[:, cols(g)], ALU.mult).then_inc(sem("kk"), 1)
                bonus(n)

            def jobs_of(m, n):
                biases(m)
                sums(m, 0)
                for j in range(NJ):
                    if j + 1 < NJ:
                        sums(m, j + 1)
                    products(m, j)
                    if j == 3:
                        modulation(n * ADA_TURN)

            def conv_turn(c):
                wait(sem("conv"), c * 3)
                for g in (1, 2):
                    wait(sem("cc_read"), c * 2 + g)
                    wait(sem("p_cx"), c * 2 + g)
                    TT(u[:, 1 + BANK * (g - 1):1 + BANK * g], ps[PS_CX[g - 1]][:], gcc[:, seq(g)], ALU.mult).then_inc(sem("cx_read"), 1)
                wait(sem("cx_read"), c * 2 + 2)
                wait(sem("conv_stored"), c * 16)
                for tap in range(3):
                    wait(sem("conv"), c * 3 + tap)
                    w = conv_w[:, bass.ds(c + 4 * tap, 1)]
                    if tap == 0:
                        a = TS(y, u[:, 0:SEQ], w, None, ALU.mult)
                    else:
                        a = STT(out=y, in0=u[:, tap:tap + SEQ], scalar=w, in1=y, op0=ALU.mult, op1=ALU.add)
                    a.then_inc(sem("conv"), 1)
                wait(sem("conv"), c * 3 + 3)
                if not isinstance(c, int):
                    modulation((c + PAIRS) * ADA_TURN)
                for g in (1, 2):
                    wait(sem("p_cb"), c * 2 + g)
                    TT(y[:, seq(g)], ps[PS_CB[g - 1]][:], y[:, seq(g)], ALU.mult).then_inc(sem("conv_out"), 1)
                modulation((c + PAIRS) * ADA_TURN + 1)

            dve.sem_inc(sem("made"), 2)
            for j in range(2):
                dve.sem_inc(sem(f"ops_stored{j}"), 16)
            TS(ka1[:], k_a, -1.0, 1.0, ALU.mult, ALU.add).then_inc(sem("ka1"), 1)
            nc.vector.memset(r[:, 0:CTX], 0.0).then_inc(sem("ka1"), 1)
            dve.wait_ge(sem("ka1"), 2)
            modulation(0)
            dve.wait_ge(sem("sg_stored"), 16)
            norms(0)
            modulation(1)
            with nc.vector.Fori(1, PAIRS) as n:
                jobs_of(nc.vector.snap(n - 1), n)
                norms(n)
                modulation(n * ADA_TURN + 1)
            jobs_of(PAIRS - 1, PAIRS)
            nc.vector.memset(u[:, 0:1], 0.0)
            nc.vector.memset(u[:, SEQ + 1:SEQ + 2], 0.0).then_inc(sem("u0"), 1)
            dve.wait_ge(sem("u0"), 1)
            conv_turn(0)
            with nc.vector.Fori(1, 4) as c:
                conv_turn(c)


def scan(nc, d, t):
    DIRS, HEADS = range(2), range(2)
    ROWS = [slice(HEAD * h, HEAD * h + HEAD) for h in HEADS]
    LOADS = 6 * 16
    with ExitStack() as st:
        sem = Sems(nc, st, "c_")
        sb = lambda n, s, dt=F32: st.enter_context(nc.sbuf_tensor("c_" + n, s, dt))
        two = lambda n, s: [sb(f"{n}{x}", s) for x in DIRS]
        four = lambda n, s: [[sb(f"{n}{x}{par}", s) for par in range(2)] for x in DIRS]
        rk = four("rk", [P, 2, PAIRS, C])
        kbk = four("kbk", [P, 3, PAIRS, 2, C])
        vc = four("vc", [P, PAIRS, C])
        vd = four("vd", [P, PAIRS, 2, C])
        bk = four("bk", [P, 2, PAIRS, 2, C])
        lr = four("lr", [P, PAIRS, C])
        mr = four("mr", [P, PAIRS, C])
        md = four("md", [P, PAIRS, 2, C])
        uend = four("uend", [P, PAIRS, 2, C])
        ld = two("ld", [P, PAIRS, 2, C])
        td = two("td", [P, PAIRS, 2, C])
        ud = two("ud", [P, PAIRS, 2, C])
        yd = two("yd", [P, PAIRS, 2, C])
        gg = two("gg", [P, PAIRS, C])
        zc = two("zc", [P, PAIRS, C])
        zd = two("zd", [P, PAIRS, 2, C])
        s1 = two("s1", [P, PAIRS, C])
        sc = two("sc", [P, PAIRS, C])
        sd = two("sd", [P, PAIRS, 2, C])
        yo = four("yo", [P, PAIRS, C])
        bank = [[st.enter_context(nc.psum_tensor(f"c_ps{x}{n}", [P, BANK], F32)) for n in range(4)] for x in DIRS]
        gate = {n: sem("passed_" + n) for n in ("pe", "sp", "act", "dve", "pool")}
        S = lambda name, x: sem(f"{name}{x}")
        half = lambda ap, w=0: ap[:, PAIRS * C * w:PAIRS * C * (w + 1)].rearrange("p (q c) -> p q c", q=PAIRS)
        quad = lambda ap: ap.rearrange("p (q w c) -> p q w c", q=PAIRS, w=2)
        whole = lambda ap: ap.rearrange("p (q c) -> p q c", q=PAIRS)
        flat = lambda ap: ap.rearrange("p q h c -> p q (h c)")
        slot_of = lambda x, s: (s + 0, SLOTS - 1 - s)[x]
        has_y = lambda s: not isinstance(s, int) or s >= NCTX
        LEVEL = lambda u, lev: u * LEVELS + (lev + 1)
        block = st.enter_context(nc.Block())

        def steps(eng, inverse, both, chain):
            inverse(0, 0, 0)
            for s in range(NCTX):
                both(s, s % 2, s // 2, (s + 1) // 2)
            with eng.Fori(NCTX // 2, STEPS // 2 - 1) as j:
                both(eng.snap(j * 2), 0, j, j)
                both(eng.snap(j * 2 + 1), 1, j, eng.snap(j + 1))
            both(STEPS - 2, 0, STEPS // 2 - 1, STEPS // 2 - 1)
            chain(STEPS - 1, 1, STEPS // 2 - 1)

        @block.sync
        def _(sp):
            def load(x, slot, par):
                ld_ = S(f"loaded{par}_", x)
                at = bass.ds(slot * C, C)
                part = lambda a0, a1, rows: d["ops"][x, a0:a1, :, rows, at].rearrange("a q p c -> p (a q) c")
                sp.dma_start(rk[x][par][:].rearrange("p a q c -> p (a q) c"), part(0, 2, slice(0, P))).then_inc(ld_, 16)
                sp.dma_start(vc[x][par][:], d["vts"][slot]).then_inc(ld_, 16)
                for h, rows in enumerate(ROWS):
                    sp.dma_start(kbk[x][par][rows, :, :, h].rearrange("p a q c -> p (a q) c"),
                                 part(1, 4, rows)).then_inc(ld_, 16)
                    sp.dma_start(vd[x][par][rows, :, h], d["vts"][slot, rows]).then_inc(ld_, 16)

            def step(s, par, more):
                for x in DIRS:
                    if more:
                        if has_y(s):
                            hold(sp, gate["sp"], S("p_y", x), held(nc.sync, s + (1 - NCTX)))
                        else:
                            sp.wait_ge(S("p_s", x), s + 1)
                        load(x, held(nc.sync, slot_of(x, s + 2)), par)
                for x in DIRS if has_y(s) else ():
                    hold(sp, gate["sp"], S("yo", x), held(nc.sync, s + (2 - NCTX)))
                    sp.dma_start(d["ys"][x, :, :, bass.ds(held(nc.sync, slot_of(x, s) * C), C)].rearrange("q p c -> p q c"), yo[x][par][:]).then_inc(S(f"stored{par}_", x), 16)

            for x in DIRS:
                for par in range(2):
                    sp.sem_inc(S(f"stored{par}_", x), 16)
            for par in range(2):
                for x in DIRS:
                    sp.wait_ge(sem("zeros"), 2 * par + x + 1)
                    load(x, slot_of(x, par), par)
            for s in range(NCTX):
                step(s, s % 2, True)
            with nc.sync.Fori(NCTX // 2, STEPS // 2 - 1) as j:
                step(nc.sync.snap(j * 2), 0, True)
                step(nc.sync.snap(j * 2 + 1), 1, True)
            step(STEPS - 2, 0, False)
            step(STEPS - 1, 1, False)
            for x in DIRS:
                for par in range(2):
                    sp.wait_ge(S(f"stored{par}_", x), 16 + 16 * NSEQ // 2)

        @block.tensor
        def _(pe):
            def heads(out, *pairs):
                for q in range(PAIRS):
                    for n, (still, moving) in enumerate(pairs):
                        last = nc.tensor.matmul(out[:, q], still[:, q].rearrange("p h c -> p (h c)"), moving(q),
                                                start=(n == 0), stop=(n == len(pairs) - 1))
                return last

            at = lambda buf: (lambda q: buf[:, q])
            diag = lambda buf: (lambda q: buf[:, q].rearrange("p h c -> p (h c)"))

            def turned(out, src):
                for q in range(PAIRS):
                    last = nc.tensor.transpose(out[:, q], diag(src)(q), t["c_ident"])
                return last

            def wait(name, x, value):
                hold(pe, gate["pe"], S(name, x), value)

            def token_major(x, u, par, u2, a):
                wait(f"loaded{par}_", x, u2 * LOADS + LOADS)
                wait(("yd", "t")[a], x, u * (LEVELS, LEVELS - 1)[a])
                for q in range(PAIRS):
                    mm = nc.tensor.transpose(bank[x][a][:, P * q:P * (q + 1)],
                                             kbk[x][par][:, 1 + a, q].rearrange("p h c -> p (h c)"), t["c_ident"])
                mm.then_inc(S(("p_bet", "p_khat")[a], x), 1)

            def triangles(x, u, par, a):
                wait(("bet", "khat")[a], x, u + 1)
                heads(quad(bank[x][a]), (kbk[x][par][:, 1 + a], lambda q: rk[x][par][:, :, q])).then_inc(S(("p_l", "p_m")[a], x), 1)

            def first_t(x, u):
                wait("u0", x, u + 1)
                wait("lr", x, u + 1)
                turned(whole(bank[x][0]), ud[x]).then_inc(S("p_t0", x), 1)

            def level_y(x, u, lev):
                if lev == 0:
                    wait("t0", x, u + 1)
                else:
                    wait("t", x, u * (LEVELS - 1) + lev)
                heads(whole(bank[x][0]), (ld[x], diag(td[x]))).then_inc(S("p_yd", x), 1)

            def level_t(x, u, lev):
                wait("yd", x, LEVEL(u, lev))
                if lev == 0:
                    wait("mr", x, u + 1)
                else:
                    wait("u", x, u * (LEVELS - 1) + lev)
                heads(whole(bank[x][1]), (ud[x], diag(yd[x]))).then_inc(S("p_t", x), 1)

            def level_u(x, u, lev):
                if lev == 0:
                    wait("uend", x, u)
                wait("t", x, u * (LEVELS - 1) + (lev + 1))
                turned(whole(bank[x][3]), td[x]).then_inc(S("p_u", x), 1)

            def last_u(x, u):
                wait("yd", x, LEVEL(u, LEVELS - 1))
                wait("u", x, u * (LEVELS - 1) + (LEVELS - 1))
                heads(whole(bank[x][3]), (yd[x], diag(ud[x]))).then_inc(S("p_uend", x), 1)

            def chain_g(x, s, par):
                wait("mr", x, s + 1)
                wait("sc", x, s + 1)
                if has_y(s):
                    wait("yo", x, held(nc.tensor, s + (1 - NCTX)))
                heads(half(bank[x][2]), (md[x][par], at(vc[x][par])), (kbk[x][par][:, 0], at(sc[x]))).then_inc(S("p_g", x), 1)

            def chain_z(x, s, par):
                wait("uend", x, s + 1)
                wait("gg", x, s + 1)
                heads(half(bank[x][2], 1), (uend[x][par], at(gg[x]))).then_inc(S("p_z", x), 1)

            def chain_s(x, s, par):
                wait("zc", x, s + 1)
                heads(half(bank[x][2]), (bk[x][par][:, 1], at(vc[x][par])), (bk[x][par][:, 0], at(zc[x]))).then_inc(S("p_s", x), 1)

            def chain_y(x, s, par):
                wait("s1", x, s + 1)
                wait("zd", x, held(nc.tensor, s + (1 - NCTX)))
                wait("sd", x, held(nc.tensor, s + (2 - NCTX)))
                heads(half(bank[x][2], 1), (sd[x], lambda q: rk[x][par][:, 0, q]), (vd[x][par], at(mr[x][par])),
                      (zd[x], at(lr[x][par]))).then_inc(S("p_y", x), 1)

            def levels(u, y):
                for lev in range(LEVELS):
                    for x in DIRS:
                        level_y(x, u, lev)
                    if lev:
                        for x in DIRS:
                            level_u(x, u, lev - 1)
                    for x in DIRS:
                        if lev < LEVELS - 1:
                            level_t(x, u, lev)
                        else:
                            last_u(x, u)
                    if lev == 0:
                        for x in DIRS:
                            y(x)

            def inverse(u, par, u2):
                for part in (token_major, triangles):
                    for a in range(2):
                        for x in DIRS:
                            part(x, u, par, *((u2,) if part is token_major else ()), a)
                for x in DIRS:
                    first_t(x, u)
                levels(u, lambda x: None)

            def both(s, par, s2, u2):
                u, other = held(nc.tensor, s + 1), 1 - par
                for a in range(2):
                    for x in DIRS:
                        token_major(x, u, other, u2, a)
                for x in DIRS:
                    chain_g(x, s, par)
                for x in DIRS:
                    triangles(x, u, other, 0)
                for x in DIRS:
                    chain_z(x, s, par)
                for x in DIRS:
                    triangles(x, u, other, 1)
                for x in DIRS:
                    first_t(x, u)
                for x in DIRS:
                    chain_s(x, s, par)
                levels(u, lambda x: chain_y(x, s, par) if has_y(s) else None)

            def chain(s, par, s2):
                for part in (chain_g, chain_z, chain_s, chain_y):
                    for x in DIRS:
                        part(x, s, par)

            steps(nc.tensor, inverse, both, chain)

        @block.scalar
        def _(act):
            def wait(name, x, value):
                hold(act, gate["act"], S(name, x), value)

            def copy(out, src, scale=1.0):
                return nc.scalar.activation(out, src, ACT.Copy, scale=scale)

            def token_major(u, par):
                for a, name in ((0, "bet"), (1, "khat")):
                    for x in DIRS:
                        wait("p_" + name, x, u + 1)
                        copy(flat(bk[x][par][:, a]), whole(bank[x][a])).then_inc(S(name, x), 1)

            def first_t(x, u):
                wait("p_t0", x, u + 1)
                copy(flat(td[x]), whole(bank[x][0])).then_inc(S("t0", x), 1)

            def diag(out, src, name, x):
                for h, rows in enumerate(ROWS):
                    a = copy(out[rows, :, h], src[rows])
                a.then_inc(S(name, x), 1)

            def level(u, lev):
                for x in DIRS:
                    wait("p_u", x, u * (LEVELS - 1) + (lev + 1))
                    copy(flat(ud[x]), whole(bank[x][3])).then_inc(S("u", x), 1)

            def chain_g(x, s):
                wait("p_g", x, s + 1)
                copy(gg[x][:], half(bank[x][2])).then_inc(S("gg", x), 1)

            def chain_z(x, s):
                wait("p_z", x, s + 1)
                copy(zc[x][:], half(bank[x][2], 1), -1.0).then_inc(S("zc", x), 1)

            def chain_zd(x, s):
                wait("zc", x, s + 1)
                diag(zd[x], zc[x], "zd", x)

            def chain_y(x, s, par, s2):
                wait("p_y", x, held(nc.scalar, s + (1 - NCTX)))
                wait(f"stored{par}_", x, held(nc.scalar, s2 * 16 + (16 - NCTX // 2 * 16)))
                copy(yo[x][par][:], half(bank[x][2], 1)).then_inc(S("yo", x), 1)

            def inverse(u, par, u2):
                token_major(u, par)
                for x in DIRS:
                    first_t(x, u)
                for lev in range(LEVELS - 1):
                    level(u, lev)

            def both(s, par, s2, u2):
                u = held(nc.scalar, s + 1)
                token_major(u, 1 - par)
                for x in DIRS:
                    chain_g(x, s)
                for x in DIRS:
                    chain_z(x, s)
                for x in DIRS:
                    first_t(x, u)
                if has_y(s):
                    for x in DIRS:
                        chain_zd(x, s)
                    for x in DIRS:
                        chain_y(x, s, par, s2)
                for lev in range(LEVELS - 1):
                    level(u, lev)

            def chain(s, par, s2):
                for x in DIRS:
                    chain_g(x, s)
                for x in DIRS:
                    chain_z(x, s)
                for x in DIRS:
                    chain_zd(x, s)
                for x in DIRS:
                    chain_y(x, s, par, s2)

            for x in DIRS:
                act.sem_inc(S("yo", x), 1)
                wait("sd", x, 1)
            steps(nc.scalar, inverse, both, chain)

        @block.vector
        def _(dve):
            TT = nc.vector.tensor_tensor

            def wait(name, x, value):
                hold(dve, gate["dve"], S(name, x), value)

            strict, incl = t["c_strict"], t["c_incl"]

            def triangles_l(x, u, par):
                wait("p_l", x, u + 1)
                wait("uend", x, u)
                b = quad(bank[x][0])
                TT(ud[x][:], bc(b[:, :, 1], 2, 2), bc(t["c_mask_u1"][:, x], 1, PAIRS), ALU.mult).then_inc(S("u_raw", x), 1)
                wait("u_raw", x, u + 1)
                TT(flat(ud[x]), flat(ud[x]), bc(t["c_ident"], 1, PAIRS), ALU.add).then_inc(S("u0", x), 1)
                TT(ld[x][:], bc(b[:, :, 1], 2, 2), bc(strict[:, x], 1, PAIRS), ALU.mult)
                TT(lr[x][par][:], b[:, :, 0], bc(incl[:, x], 1, PAIRS), ALU.mult).then_inc(S("lr", x), 1)

            def triangles_m(x, u, par):
                wait("p_m", x, u + 1)
                b = quad(bank[x][1])
                TT(md[x][par][:], bc(b[:, :, 1], 2, 2), bc(strict[:, x], 1, PAIRS), ALU.mult)
                TT(mr[x][par][:], b[:, :, 0], bc(incl[:, x], 1, PAIRS), ALU.mult).then_inc(S("mr", x), 1)

            def level_y(x, u, lev):
                wait("p_yd", x, LEVEL(u, lev))
                TT(yd[x][:], quad(bank[x][0]), bc(bc(t["c_mask_lev"][:, x, lev], 1, 2), 1, PAIRS), ALU.mult).then_inc(S("yd", x), 1)

            def level_t(x, u, lev):
                wait("p_t", x, u * (LEVELS - 1) + (lev + 1))
                TT(flat(td[x]), flat(td[x]), whole(bank[x][1]), ALU.subtract).then_inc(S("t", x), 1)

            def last_u(x, u, par):
                wait("p_uend", x, u + 1)
                TT(flat(uend[x][par]), flat(ud[x]), whole(bank[x][3]), ALU.subtract).then_inc(S("uend", x), 1)

            def levels(u, par):
                for lev in range(LEVELS):
                    for x in DIRS:
                        level_y(x, u, lev)
                    for x in DIRS:
                        if lev < LEVELS - 1:
                            level_t(x, u, lev)
                        else:
                            last_u(x, u, par)

            def chain_s(x, s):
                wait("p_s", x, s + 1)
                if has_y(s):
                    wait("sd", x, held(nc.vector, s + (2 - NCTX)))
                TT(s1[x][:], sc[x][:], half(bank[x][2]), ALU.add).then_inc(S("s1", x), 1)
                wait("s1", x, s + 1)
                end = t["pend"][:, x, bass.ds(held(nc.vector, slot_of(x, s)), 1)].rearrange("p o q -> p (o q)")
                TT(sc[x][:], s1[x][:], bc(end, 2, C), ALU.mult).then_inc(S("sc", x), 1)

            def inverse(u, par, u2):
                for part in (triangles_l, triangles_m):
                    for x in DIRS:
                        part(x, u, par)
                levels(u, par)

            def both(s, par, s2, u2):
                u, other = held(nc.vector, s + 1), 1 - par
                for part in (triangles_l, triangles_m):
                    for x in DIRS:
                        part(x, u, other)
                for x in DIRS:
                    chain_s(x, s)
                levels(u, other)

            def chain(s, par, s2):
                for x in DIRS:
                    chain_s(x, s)

            for par in range(2):
                for x in DIRS:
                    nc.vector.memset(kbk[x][par][:], 0.0)
                    nc.vector.memset(vd[x][par][:], 0.0).then_inc(sem("zeros"), 1)
                    if par == 0:
                        nc.vector.memset(sc[x][:], 0.0).then_inc(S("sc", x), 1)
            steps(nc.vector, inverse, both, chain)

        @block.gpsimd
        def _(pool):
            TS = nc.gpsimd.tensor_scalar

            def wait(name, x, value):
                hold(pool, gate["pool"], S(name, x), value)

            def state(s, par, s2, u2):
                for x in DIRS if has_y(s) or s == NCTX - 1 else ():
                    wait("sc", x, held(nc.gpsimd, s + 2))
                    if has_y(s):
                        wait("p_y", x, held(nc.gpsimd, s + (1 - NCTX)))
                    for h in HEADS:
                        a = TS(sd[x][:, :, h], sc[x][:], t["c_headones"][:, HEAD * h:HEAD * h + 1], None, ALU.mult)
                    a.then_inc(S("sd", x), 1)

            for x in DIRS:
                nc.gpsimd.memset(zd[x][:], 0.0)
                nc.gpsimd.memset(sd[x][:], 0.0).then_inc(S("sd", x), 1)
            steps(nc.gpsimd, lambda u, par, u2: None, state, lambda s, par, s2: None)


def mixer_out(nc, d, t):
    G = range(2)
    cols = lambda g: slice(BANK * g, BANK * (g + 1))
    with ExitStack() as st:
        sem = Sems(nc, st, "d_")
        sb = lambda n, s, dt=F32: st.enter_context(nc.sbuf_tensor("d_" + n, s, dt))
        y, yr = sb("y", [P, PAIRS, SEQ]), sb("yr", [P, 2, SEQ])
        sq, rstd = sb("sq", [P, SEQ]), sb("rstd", [P, 2, SEQ])
        g_up = sb("g_up", [P, CH])
        raw = sb("raw", [P, 2, KD, P])
        w_hi, w_lo = sb("w_hi", [P, 2, KD, P], F32R), sb("w_lo", [P, 2, KD, P], F32R)
        ps = [st.enter_context(nc.psum_tensor(f"d_ps{n}", [P, BANK], F32)) for n in range(8)]
        mix, sg = sb("mix", [P, KD, SEQ]), sb("sg", [P, SEQ])
        x1, hi, lo = t["x"], t["h2_hi"], t["h2_lo"]
        full = [sem(f"psum_full{b}") for b in range(4)]
        free = [sem(f"psum_free{b}") for b in range(4)]
        gate = {n: sem("passed_" + n) for n in ("pe", "sp", "act", "dve", "pool")}
        block = st.enter_context(nc.Block())

        @block.sync
        def _(sp):
            for j in range(PAIRS):
                if j >= 2:
                    sp.wait_ge(sem("summed"), j - 1)
                for x, buf in ((0, y[:, j]), (1, yr[:, j % 2])):
                    sp.dma_start(buf, d["ys"][x, j, :, CTX:TOK]).then_inc(sem(f"y{j % 2}"), 16)
                if j == 1:
                    sp.dma_start(sg[:], d["sgs"]).then_inc(sem("g_up"), 16)
                    sp.dma_start(g_up[:], d["g_up"]).then_inc(sem("g_up"), 16)
                if j == 2:
                    sp.dma_start(mix[:, PAIRS:KD], d["mixd"][:, PAIRS:KD]).then_inc(sem("mix_r"), 16)
                if j == 3:
                    sp.dma_start(mix[:, 0:PAIRS], d["mixd"][:, 0:PAIRS]).then_inc(sem("mix_c"), 16)
                    sp.dma_start(raw[:], d["w_out"][0]).then_inc(sem("raw"), 16)
            sp.dma_start(x1[:], d["xT"]).then_inc(sem("x"), 16)
            with nc.sync.Fori(0, 3) as i:
                for s in range(2):
                    hold(sp, gate["sp"], sem(f"lo{s}"), nc.sync.snap(i + 1))
                sp.dma_start(raw[:], d["w_out"][i + 1]).then_inc(sem("raw"), 16)

        @block.tensor
        def _(pe):
            def means(j):
                pe.wait_ge(sem("summed"), j + 1)
                if j:
                    pe.wait_ge(sem("centred"), j)
                for g in G:
                    mm = nc.tensor.matmul(ps[g][:], t["c_headones"], y[:, j, cols(g)], start=True, stop=True)
                mm.then_inc(sem("p_mean"), 1)

            means(0)
            for j in range(PAIRS):
                if j + 1 < PAIRS:
                    means(j + 1)
                pe.wait_ge(sem("sq"), j + 1)
                if j:
                    pe.wait_ge(sem("std"), j)
                for g in G:
                    mm = nc.tensor.matmul(ps[2 + g][:], t["c_headones"], sq[:, cols(g)], start=True, stop=True)
                mm.then_inc(sem("p_var"), 1)
                if j == 0:
                    pe.wait_ge(sem("g_up"), 32)
                if j >= 2:
                    pe.wait_ge(sem("gated"), j - 1)
                for g in G:
                    mm = nc.tensor.matmul(ps[4 + 2 * (j % 2) + g][:], g_up[:, P * j:P * (j + 1)], sg[:, cols(g)], start=True, stop=True)
                mm.then_inc(sem("p_gate"), 1)
            pe.wait_ge(sem("centred"), PAIRS)
            pe.wait_ge(sem("std"), PAIRS)

            def there(k):
                if k < KD - 1:
                    pe.wait_ge(sem("mix_lo"), max(1, k - PAIRS + 2))
                else:
                    pe.wait_ge(sem("mix_last"), 1)

            def tile(n, s):
                hold(pe, gate["pe"], sem(f"hi{s}"), n)
                hold(pe, gate["pe"], sem(f"lo{s}"), n)
                for g in G:
                    b = 2 * s + g
                    hold(pe, gate["pe"], free[b], n)
                    product(nc, ps[b][:], w_hi[:, s], w_lo[:, s], hi, lo, KD, cols(g)).then_inc(full[b], 1)

            pe.wait_ge(sem("lo0"), 1)
            for k in range(KD):
                there(k)
                for g in G:
                    for m, (w, x) in enumerate(((w_hi, hi), (w_hi, lo), (w_lo, hi))):
                        mm = nc.tensor.matmul(ps[g][:], w[:, 0, k], x[:, k, cols(g)], start=(k == 0 and m == 0),
                                              stop=(k == KD - 1 and m == 2))
                    if k == KD - 1:
                        mm.then_inc(full[g], 1)
            tile(1, 1)
            with nc.tensor.Fori(2, 5) as n:
                for s in range(2):
                    tile(n, s)

        @block.scalar
        def _(act):
            def split_hi(n, first):
                hold(act, gate["act"], sem("raw"), n * 16 + 16)
                for s in range(2):
                    if not first:
                        hold(act, gate["act"], full[2 * s + 1], n)
                    nc.scalar.activation(w_hi[:, s], raw[:, s], ACT.Copy).then_inc(sem(f"hi{s}"), 1)

            def squares(j):
                act.wait_ge(sem("centred"), j + 1)
                if j:
                    act.wait_ge(sem("p_var"), j)
                nc.scalar.activation(sq[:], y[:, j], ACT.Square).then_inc(sem("sq"), 1)

            def std(j):
                act.wait_ge(sem("p_var"), j + 1)
                if j >= 2:
                    act.wait_ge(sem("yn"), j - 1)
                for g in G:
                    a = nc.scalar.activation(rstd[:, j % 2, cols(g)], ps[2 + g][:], ACT.Sqrt, scale=1.0 / HEAD, bias=t["c_gneps"])
                a.then_inc(sem("std"), 1)

            def gained(j):
                act.wait_ge(sem("yn"), j + 1)
                nc.scalar.activation(y[:, j], y[:, j], ACT.Identity, scale=t["v_ln_g"][:, j:j + 1],
                                     bias=t["v_ln_b"][:, j:j + 1]).then_inc(sem("scaled"), 1)

            def mix_hi(j):
                act.wait_ge(sem("gated"), j + 1)
                nc.scalar.activation(hi[:, PAIRS + j], mix[:, PAIRS + j], ACT.Copy).then_inc(sem("mix_hi"), 1)

            for j in range(2):
                squares(j)
                std(j)
            for j in range(PAIRS):
                if j + 2 < PAIRS:
                    squares(j + 2)
                gained(j)
                if j + 2 < PAIRS:
                    std(j + 2)
                if j == 0:
                    act.wait_ge(sem("mix_c"), 16)
                    nc.scalar.activation(hi[:, 0:PAIRS], mix[:, 0:PAIRS], ACT.Copy).then_inc(sem("mix_hi"), 1)
                    split_hi(0, True)
                if j:
                    mix_hi(j - 1)
            mix_hi(PAIRS - 1)
            with nc.scalar.Fori(0, 3) as i:
                split_hi(nc.scalar.snap(i + 1), False)
        @block.gpsimd
        def _(pool):
            def split_lo(n):
                for s in range(2):
                    hold(pool, gate["pool"], sem(f"hi{s}"), n + 1)
                    nc.gpsimd.tensor_tensor(w_lo[:, s], raw[:, s], w_hi[:, s].bitcast(F32),
                                            ALU.subtract).then_inc(sem(f"lo{s}"), 1)

            def summed(j):
                pool.wait_ge(sem(f"y{j % 2}"), 32 * (j // 2 + 1))
                nc.gpsimd.tensor_tensor(y[:, j], y[:, j], yr[:, j % 2], ALU.add).then_inc(sem("summed"), 1)

            def mix_lo(j):
                k = slice(PAIRS + j, PAIRS + j + 1)
                pool.wait_ge(sem("mix_hi"), j + 2)
                nc.gpsimd.tensor_tensor(lo[:, k], mix[:, k], hi[:, k].bitcast(F32), ALU.subtract).then_inc(sem("mix_lo"), 1)

            for j in range(PAIRS):
                summed(j)
            pool.wait_ge(sem("mix_hi"), 1)
            k = slice(0, PAIRS)
            nc.gpsimd.tensor_tensor(lo[:, k], mix[:, k], hi[:, k].bitcast(F32), ALU.subtract).then_inc(sem("mix_lo"), 1)
            split_lo(0)
            for j in range(PAIRS - 1):
                mix_lo(j)
            with nc.gpsimd.Fori(1, 4) as i:
                split_lo(i)

        @block.vector
        def _(dve):
            TT, TS, STT = nc.vector.tensor_tensor, nc.vector.tensor_scalar, nc.vector.scalar_tensor_tensor
            def centred(j):
                dve.wait_ge(sem("p_mean"), j + 1)
                for g in G:
                    a = STT(out=y[:, j, cols(g)], in0=ps[g][:], scalar=-1.0 / HEAD, in1=y[:, j, cols(g)], op0=ALU.mult, op1=ALU.add)
                a.then_inc(sem("centred"), 1)

            def normed(j):
                r = rstd[:, j % 2]
                dve.wait_ge(sem("std"), j + 1)
                nc.vector.reciprocal(r, r).then_inc(sem("rstd"), 1)
                dve.wait_ge(sem("rstd"), j + 1)
                TT(y[:, j], y[:, j], r, ALU.mult).then_inc(sem("yn"), 1)

            def gated(j):
                dve.wait_ge(sem("scaled"), j + 1)
                dve.wait_ge(sem("mix_r"), 16)
                TT(y[:, j], y[:, j], mix[:, PAIRS + j], ALU.add).then_inc(sem("bonus"), 1)
                dve.wait_ge(sem("bonus"), j + 1)
                dve.wait_ge(sem("p_gate"), j + 1)
                for g in G:
                    a = TT(mix[:, PAIRS + j, cols(g)], y[:, j, cols(g)], ps[4 + 2 * (j % 2) + g][:], ALU.mult)
                a.then_inc(sem("gated"), 1)

            for b in range(4):
                dve.sem_inc(free[b], 1)
            centred(0)
            centred(1)
            normed(0)
            for j in range(PAIRS):
                if j + 2 < PAIRS:
                    centred(j + 2)
                if j + 1 < PAIRS:
                    normed(j + 1)
                gated(j)
            k = slice(KD - 1, KD)
            dve.wait_ge(sem("mix_hi"), 1 + PAIRS)
            TT(lo[:, k], mix[:, k], hi[:, k].bitcast(F32), ALU.subtract).then_inc(sem("mix_last"), 1)
            dve.wait_ge(sem("x"), 16)
            with nc.vector.Fori(0, 4) as i:
                n = nc.vector.snap(i + 1)
                for s in range(2):
                    tile = nc.vector.snap(i * 2 + s)
                    for g in G:
                        b = 2 * s + g
                        hold(dve, gate["dve"], full[b], n)
                        xs = x1[:, bass.ds(tile, 1), cols(g)]
                        STT(out=xs, in0=ps[b][:].unsqueeze(1), scalar=t["mod"][:, 0, bass.ds(tile + 16, 1)], in1=xs,
                            op0=ALU.mult, op1=ALU.add).then_inc(free[b], 1)


def norm_x1(nc, d, t):
    N, HALF = 256, KD // 2
    groups = [slice(N * g, N * (g + 1)) for g in range(SEQ // N)]
    x, hi, lo = t["x"], t["h2_hi"], t["h2_lo"]
    shift = t["mod"][:, 0, 24:32]
    with ExitStack() as st:
        sem = Sems(nc, st, "n1_")
        sq = st.enter_context(nc.sbuf_tensor("n1_sq", [P, 2, KD, N], F32))
        whole = st.enter_context(nc.sbuf_tensor("n1_whole", [P, 2, KD, N], F32))
        rstd = st.enter_context(nc.sbuf_tensor("n1_rstd", [P, 2, N], F32))
        gain = st.enter_context(nc.sbuf_tensor("n1_gain", [P, KD], F32))
        ps = [st.enter_context(nc.psum_tensor(f"n1_ps{n}", [P, BANK], F32)) for n in range(2)]
        block = st.enter_context(nc.Block())

        @block.scalar
        def _(act):
            def squares(g):
                if g >= 2:
                    act.wait_ge(sem("sums"), g - 1)
                nc.scalar.activation(sq[:, g % 2], x[:, :, groups[g]], ACT.Square).then_inc(sem("squares"), 1)

            def std(g):
                act.wait_ge(sem("sums"), g + 1)
                if g >= 2:
                    act.wait_ge(sem("normed"), g - 1)
                nc.scalar.activation(rstd[:, g % 2], ps[g % 2][:, 0:N], ACT.Sqrt, scale=1.0 / D,
                                     bias=t["c_eps"]).then_inc(sem("std"), 1)

            squares(0)
            squares(1)
            std(0)
            for g, cols in enumerate(groups):
                if g + 2 < len(groups):
                    squares(g + 2)
                if g + 1 < len(groups):
                    std(g + 1)
                act.wait_ge(sem("normed"), g + 1)
                for k in range(KD):
                    a = nc.scalar.activation(whole[:, g % 2, k], whole[:, g % 2, k], ACT.Identity,
                                             bias=shift[:, k:k + 1])
                a.then_inc(sem("full"), 1)
                act.wait_ge(sem("full"), g + 1)
                nc.scalar.activation(hi[:, :, cols], whole[:, g % 2], ACT.Copy).then_inc(sem("hi"), 1)

        @block.tensor
        def _(pe):
            pe.wait_ge(sem("squares"), 1)
            for g in range(len(groups)):
                pe.wait_ge(sem("squares"), g + 1)
                if g >= 2:
                    pe.wait_ge(sem("std"), g - 1)
                for k in range(KD):
                    mm = nc.tensor.matmul(ps[g % 2][:, 0:N], t["c_ones"], sq[:, g % 2, k], start=(k == 0), stop=(k == KD - 1))
                mm.then_inc(sem("sums"), 1)

        @block.vector
        def _(dve):
            def normed(g):
                dve.wait_ge(sem("std"), g + 1)
                nc.vector.reciprocal(rstd[:, g % 2], rstd[:, g % 2]).then_inc(sem("rstd"), 1)
                dve.wait_ge(sem("rstd"), g + 1)
                if g >= 2:
                    for half in range(2):
                        dve.wait_ge(sem(f"lo{half}"), g - 1)
                for k in range(KD):
                    a = nc.vector.scalar_tensor_tensor(out=whole[:, g % 2, k], in0=x[:, k, groups[g]], scalar=gain[:, k:k + 1],
                                                       in1=rstd[:, g % 2], op0=ALU.mult, op1=ALU.mult)
                a.then_inc(sem("normed"), 1)

            nc.vector.scalar_tensor_tensor(out=gain[:], in0=t["mod"][:, 0, 32:40], scalar=1.0, in1=t["v_norm2_g"],
                                           op0=ALU.add, op1=ALU.mult).then_inc(sem("gain"), 1)
            dve.wait_ge(sem("gain"), 1)
            normed(0)
            for g, cols in enumerate(groups):
                if g + 1 < len(groups):
                    normed(g + 1)
                dve.wait_ge(sem("hi"), g + 1)
                nc.vector.tensor_tensor(lo[:, HALF:KD, cols], whole[:, g % 2, HALF:KD], hi[:, HALF:KD, cols].bitcast(F32),
                                        ALU.subtract).then_inc(sem("lo1"), 1)

        @block.sync
        def _(sp):
            sp.dma_start(t["raw_up"], d["w_ffn"][0]).then_inc(t["ahead"]("up"), 16)

        @block.gpsimd
        def _(pool):
            for g, cols in enumerate(groups):
                pool.wait_ge(sem("hi"), g + 1)
                nc.gpsimd.tensor_tensor(lo[:, 0:HALF, cols], whole[:, g % 2, 0:HALF], hi[:, 0:HALF, cols].bitcast(F32),
                                        ALU.subtract).then_inc(sem("lo0"), 1)


def norm_x3(nc, d, t):
    N, HALF = 256, KD // 2
    groups = [slice(N * g, N * (g + 1)) for g in range(SEQ // N)]
    x, hi, lo = t["x"], t["h3_hi"], t["h3_lo"]
    final_g, norm_g = t["v_final_g"], t["v_norm_g_2"]
    with ExitStack() as st:
        sem = Sems(nc, st, "n3_")
        sb = lambda n, shape: st.enter_context(nc.sbuf_tensor("n3_" + n, shape, F32))
        sq = sb("sq", [P, 2, KD, N])
        whole = sb("whole", [P, 2, KD, N])
        r1, r3, mean = sb("r1", [P, 2, N]), sb("r3", [P, 2, N]), sb("mean", [P, 2, N])
        ps = [st.enter_context(nc.psum_tensor(f"n3_ps{n}", [P, BANK], F32)) for n in range(4)]
        block = st.enter_context(nc.Block())

        @block.scalar
        def _(act):
            def squares(g):
                for w in range(2):
                    if g >= 1:
                        act.wait_ge(sem(f"sums{w}"), g)
                    if w == 0:
                        a = nc.scalar.activation(sq[:, 0], x[:, :, groups[g]], ACT.Square)
                    else:
                        for k in range(KD):
                            a = nc.scalar.activation(sq[:, 1, k], x[:, k, groups[g]], ACT.Square, scale=final_g[:, k:k + 1])
                    a.then_inc(sem(f"squares{w}"), 1)

            def std1(g):
                act.wait_ge(sem("sums0"), g + 1)
                if g >= 2:
                    act.wait_ge(sem("x3"), g - 1)
                nc.scalar.activation(r1[:, g % 2], ps[g % 2][:, 0:N], ACT.Sqrt, scale=1.0 / D, bias=t["c_eps"]).then_inc(sem("std1"), 1)

            def std3(g):
                act.wait_ge(sem("mean"), g + 1)
                if g >= 2:
                    act.wait_ge(sem("h3"), g - 1)
                nc.scalar.activation(r3[:, g % 2], mean[:, g % 2], ACT.Sqrt, scale=1.0 / D, bias=t["c_eps"]).then_inc(sem("std3"), 1)

            for g in range(2):
                squares(g)
                std1(g)
            for g, cols in enumerate(groups):
                std3(g)
                if g + 2 < len(groups):
                    squares(g + 2)
                    std1(g + 2)
                act.wait_ge(sem("h3"), g + 1)
                nc.scalar.activation(hi[:, :, cols], whole[:, g % 2], ACT.Copy).then_inc(sem("hi"), 1)

        @block.tensor
        def _(pe):
            for g in range(len(groups)):
                for w in range(2):
                    pe.wait_ge(sem(f"squares{w}"), g + 1)
                    if g >= 2:
                        pe.wait_ge(sem(("std1", "mean")[w]), g - 1)
                    for k in range(KD):
                        mm = nc.tensor.matmul(ps[2 * w + g % 2][:, 0:N], t["c_ones"], sq[:, w, k], start=(k == 0), stop=(k == KD - 1))
                    mm.then_inc(sem(f"sums{w}"), 1)

        @block.vector
        def _(dve):
            TT, STT = nc.vector.tensor_tensor, nc.vector.scalar_tensor_tensor

            def scaled(out, cols, gain, r):
                for k in range(KD):
                    a = STT(out=out[:, k], in0=x[:, k, cols], scalar=gain[:, k:k + 1], in1=r, op0=ALU.mult, op1=ALU.mult)
                return a

            def first(g):
                p = g % 2
                dve.wait_ge(sem("std1"), g + 1)
                nc.vector.reciprocal(r1[:, p], r1[:, p]).then_inc(sem("r1"), 1)
                dve.wait_ge(sem("r1"), g + 1)
                if g >= 2:
                    dve.wait_ge(sem("std3"), g - 1)
                TT(mean[:, p], r1[:, p], r1[:, p], ALU.mult).then_inc(sem("r1_sq"), 1)
                dve.wait_ge(sem("r1_sq"), g + 1)
                dve.wait_ge(sem("sums1"), g + 1)
                TT(mean[:, p], mean[:, p], ps[2 + p][:, 0:N], ALU.mult).then_inc(sem("mean"), 1)
                dve.wait_ge(sem("squares1"), g + 1)
                scaled(x[:, :, groups[g]], groups[g], final_g, r1[:, p]).then_inc(sem("x3"), 1)

            def second(g):
                p = g % 2
                dve.wait_ge(sem("std3"), g + 1)
                nc.vector.reciprocal(r3[:, p], r3[:, p]).then_inc(sem("r3"), 1)
                dve.wait_ge(sem("r3"), g + 1)
                dve.wait_ge(sem("x3"), g + 1)
                if g >= 2:
                    dve.wait_ge(sem("lo"), g - 1)
                scaled(whole[:, p], groups[g], norm_g, r3[:, p]).then_inc(sem("h3"), 1)

            first(0)
            for g, cols in enumerate(groups):
                if g + 1 < len(groups):
                    first(g + 1)
                second(g)
            for g, cols in list(enumerate(groups))[-1:]:
                dve.wait_ge(sem("hi"), g + 1)
                TT(lo[:, HALF:KD, cols], whole[:, g % 2, HALF:KD], hi[:, HALF:KD, cols].bitcast(F32),
                   ALU.subtract).then_inc(sem("last_lo"), 1)

        @block.gpsimd
        def _(pool):
            for g, cols in enumerate(groups):
                n = HALF if g == len(groups) - 1 else KD
                pool.wait_ge(sem("hi"), g + 1)
                nc.gpsimd.tensor_tensor(lo[:, 0:n, cols], whole[:, g % 2, 0:n], hi[:, 0:n, cols].bitcast(F32),
                                        ALU.subtract).then_inc(sem("lo"), 1)

        @block.sync
        def _(sp):
            sp.dma_start(t["raw_2"], d["w2"][0]).then_inc(t["ahead"]("w2"), 16)
            for g, cols in enumerate(groups):
                sp.wait_ge(sem("x3"), g + 1)
                sp.dma_start(d["x3s"][:, :, cols], x[:, :, cols]).then_inc(sem("stored"), 16)
            sp.wait_ge(sem("stored"), 16 * len(groups))


def ffn_up(nc, d, t):
    with ExitStack() as st:
        sem = Sems(nc, st, "e_")
        sb = lambda n, s, dt=F32: st.enter_context(nc.sbuf_tensor("e_" + n, s, dt))
        raw = t["raw_up"]
        w_hi, w_lo = sb("w_hi", [P, 2, KD, P], F32R), sb("w_lo", [P, 2, KD, P], F32R)
        grid = sb("grid", [P, GRID_H + 2, GRID_W + 2])
        acc = sb("acc", [P, GRID_H, GRID_W])
        act_g = sb("act_g", [P, SEQ])
        z = sb("z", [P, SEQ])
        ps = [st.enter_context(nc.psum_tensor(f"e_ps{n}", [P, BANK], F32)) for n in range(4)]
        full = [sem(f"psum_full{b}") for b in range(4)]
        free = [sem(f"psum_free{b}") for b in range(4)]
        gate = {n: sem("passed_" + n) for n in ("pe", "sp", "act", "dve", "pool")}
        hi, lo = t["h2_hi"], t["h2_lo"]
        ROWS = GRID_H // 2
        cols = lambda g: slice(BANK * g, BANK * (g + 1))
        block = st.enter_context(nc.Block())

        @block.sync
        def _(sp):
            def store(i):
                hold(sp, gate["sp"], sem("z"), i * 2 + 4)
                sp.dma_start(d["zs"][i], z[:]).then_inc(sem("stored"), 16)

            with nc.sync.Fori(0, NFF - 1) as i:
                n = nc.sync.snap(i + 1)
                for s in range(2):
                    hold(sp, gate["sp"], sem(f"lo{s}"), n)
                sp.dma_start(raw[:], d["w_ffn"][n]).then_inc(sem("raw"), 16)
                store(nc.sync.snap(i + 0))
            for s in range(2):
                sp.dma_start(t["raw_down"][:, s], d["w_down"][s]).then_inc(t["ahead"](f"down{s}"), 16)
            store(NFF - 1)
            sp.wait_ge(sem("stored"), 16 + 16 * NFF)

        @block.tensor
        def _(pe):
            with nc.tensor.Fori(0, NFF) as i:
                n = nc.tensor.snap(i + 1)
                for s in range(2):
                    hold(pe, gate["pe"], sem(f"hi{s}"), n)
                    hold(pe, gate["pe"], sem(f"lo{s}"), n)
                    for g in range(2):
                        b = 2 * s + g
                        hold(pe, gate["pe"], free[b], n)
                        product(nc, ps[b][:], w_hi[:, s], w_lo[:, s], hi, lo, KD, cols(g)).then_inc(full[b], 1)

        @block.scalar
        def _(act):
            def split_hi(n, s):
                if isinstance(n, int):
                    act.wait_ge(t["ahead"]("up"), 16)
                else:
                    hold(act, gate["act"], sem("raw"), n * 16)
                    hold(act, gate["act"], full[2 * s + 1], n)
                nc.scalar.activation(w_hi[:, s], raw[:, s], ACT.Copy).then_inc(sem(f"hi{s}"), 1)

            def step(i, n, last):
                hold(act, gate["act"], sem("conv"), i * 9 + 9)
                for g in range(2):
                    hold(act, gate["act"], full[g], n)
                    nc.scalar.activation(grid[:, 1 + ROWS * g:1 + ROWS * (g + 1), 1:1 + GRID_W],
                                         ps[g][:].rearrange("p (h w) -> p h w", w=GRID_W), ACT.Copy).then_inc(free[g], 1)
                if not last:
                    split_hi(n, 0)
                hold(act, gate["act"], sem("conv"), i * 9 + 18)
                hold(act, gate["act"], sem("z"), i * 2 + 2)
                nc.scalar.activation(act_g[:], acc[:].rearrange("p h w -> p (h w)"), ACT.Silu).then_inc(sem("silu"), 1)
                if not last:
                    split_hi(n, 1)

            act.wait_ge(sem("rim"), 1)
            for s in range(2):
                split_hi(0, s)
            with nc.scalar.Fori(0, NFF - 1) as i:
                step(nc.scalar.snap(i + 0), nc.scalar.snap(i + 1), False)
            step(NFF - 1, NFF, True)

        @block.gpsimd
        def _(pool):
            with nc.gpsimd.Fori(0, NFF) as i:
                n = nc.gpsimd.snap(i + 1)
                for s in range(2):
                    hold(pool, gate["pool"], sem(f"hi{s}"), n)
                    nc.gpsimd.tensor_tensor(w_lo[:, s], raw[:, s], w_hi[:, s].bitcast(F32), ALU.subtract).then_inc(sem(f"lo{s}"), 1)

        @block.vector
        def _(dve):
            for b in range(4):
                dve.sem_inc(free[b], 1)
            dve.sem_inc(sem("conv"), 9)
            dve.sem_inc(sem("silu"), 1)
            dve.sem_inc(sem("z"), 2)
            dve.sem_inc(sem("stored"), 16)
            nc.vector.memset(grid[:], 0.0).then_inc(sem("rim"), 1)
            w = t["v_ffn_conv_w"]
            with nc.vector.Fori(0, NFF) as i:
                n = nc.vector.snap(i + 1)
                for g in range(2):
                    hold(dve, gate["dve"], free[g], nc.vector.snap(n + 1))
                hold(dve, gate["dve"], sem("silu"), n)
                for tap in range(9):
                    dy, dx = tap // 3, tap % 3
                    view = grid[:, dy:dy + GRID_H, dx:dx + GRID_W]
                    wt = w[:, bass.ds(i + tap * NFF, 1)]
                    if tap:
                        hold(dve, gate["dve"], sem("conv"), nc.vector.snap(i * 9 + (tap + 9)))
                        a = nc.vector.scalar_tensor_tensor(out=acc[:], in0=view, scalar=wt, in1=acc[:], op0=ALU.mult, op1=ALU.add)
                    else:
                        a = nc.vector.tensor_scalar(acc[:], view, wt, t["v_ffn_conv_b"][:, bass.ds(i, 1)], ALU.mult, ALU.add)
                    a.then_inc(sem("conv"), 1)
                hold(dve, gate["dve"], sem("silu"), nc.vector.snap(n + 1))
                hold(dve, gate["dve"], sem("stored"), n * 16)
                for g in range(2):
                    hold(dve, gate["dve"], full[2 + g], n)
                    nc.vector.tensor_tensor(z[:, cols(g)], act_g[:, cols(g)], ps[2 + g][:], ALU.mult).then_inc(free[2 + g], 1)
                for g in range(2):
                    hold(dve, gate["dve"], free[2 + g], nc.vector.snap(n + 1))
                dve.sem_inc(sem("z"), 2)


def ffn_down(nc, d, t):
    HALVES, TURNS = 2, KD // 2
    ZT, ZS = NFF // 2, 2
    with ExitStack() as st:
        sem = Sems(nc, st, "f_")
        sb = lambda n, s, dt=F32: st.enter_context(nc.sbuf_tensor("f_" + n, s, dt))
        z_hi, z_lo = sb("z_hi", [P, NFF, BANK], F32R), sb("z_lo", [P, NFF, BANK], F32R)
        z_raw = sb("z_raw", [P, ZS, 2, BANK])
        raw = t["raw_down"]
        w_hi, w_lo = sb("w_hi", [P, 2, NFF, P], F32R), sb("w_lo", [P, 2, NFF, P], F32R)
        x = t["x"]
        ps = [st.enter_context(nc.psum_tensor(f"f_ps{n}", [P, BANK], F32)) for n in range(2)]
        gate = {n: sem("passed_" + n) for n in ("pe", "sp", "act", "dve", "pool")}
        cols = lambda g: slice(BANK * g, BANK * (g + 1))
        slot = lambda g, j: (g * ZT + j) % ZS
        uses = lambda g, j: (g * ZT + j) // ZS
        block = st.enter_context(nc.Block())

        @block.sync
        def _(sp):
            def load_w(tile, turn, s):
                hold(sp, gate["sp"], sem(f"lo{s}"), turn)
                sp.dma_start(raw[:, s], d["w_down"][tile]).then_inc(sem(f"raw{s}"), 16)

            for g in range(HALVES):
                for s in range(2 if g else 0):
                    load_w(s, g * TURNS, s)
                for j in range(ZT):
                    if uses(g, j):
                        sp.wait_ge(sem(f"z_lo{slot(g, j)}"), uses(g, j))
                    sp.dma_start(z_raw[:, slot(g, j)], d["zs"][2 * j:2 * j + 2, :, cols(g)].rearrange("n p c -> p n c")
                                 ).then_inc(sem(f"z_raw{slot(g, j)}"), 16)
                with nc.sync.Fori(1, TURNS) as i:
                    for s in range(2):
                        load_w(held(nc.sync, 2 * i + s), nc.sync.snap(i + g * TURNS), s)

        @block.gpsimd
        def _(pool):
            def split_w(turn, s):
                hold(pool, gate["pool"], sem(f"hi{s}"), turn + 1)
                nc.gpsimd.tensor_tensor(w_lo[:, s], raw[:, s], w_hi[:, s].bitcast(F32), ALU.subtract).then_inc(sem(f"lo{s}"), 1)

            split_w(0, 0)
            with nc.gpsimd.Fori(1, HALVES * TURNS) as turn:
                for s in range(2):
                    split_w(turn, s)

        @block.scalar
        def _(act):
            def wait(s, value):
                hold(act, gate["act"], s, value)

            def split_z(g, j):
                act.wait_ge(sem(f"z_raw{slot(g, j)}"), 16 * (uses(g, j) + 1))
                if g:
                    if j + 1 < ZT:
                        act.wait_ge(sem("z_used"), 2 * j + 2 + (2 * TURNS - 1) * (NFF - 1))
                    else:
                        act.wait_ge(sem("ended1"), TURNS)
                nc.scalar.activation(z_hi[:, 2 * j:2 * j + 2], z_raw[:, slot(g, j)], ACT.Copy).then_inc(sem(f"z_hi{slot(g, j)}"), 1)

            def split_w(turn, s):
                if isinstance(turn, int) and turn == 0:
                    act.wait_ge(t["ahead"](f"down{s}"), 16)
                else:
                    wait(sem(f"raw{s}"), turn * 16)
                    wait(sem(f"ended{s}"), turn)
                nc.scalar.activation(w_hi[:, s], raw[:, s], ACT.Copy).then_inc(sem(f"hi{s}"), 1)

            for g in range(HALVES):
                split_w(g * TURNS, 0)
                if g == 0:
                    split_w(0, 1)
                for j in range(ZT):
                    split_z(g, j)
                    if g and j == ZT - 3:
                        split_w(g * TURNS, 1)
                with nc.scalar.Fori(1, TURNS) as i:
                    for s in range(2):
                        split_w(nc.scalar.snap(i + g * TURNS), s)

        @block.tensor
        def _(pe):
            def sums(s, k):
                for n, (w, y) in enumerate(((w_hi, z_hi), (w_hi, z_lo), (w_lo, z_hi))):
                    mm = nc.tensor.matmul(ps[s][:], w[:, s, k], y[:, k], start=(k == 0 and n == 0), stop=(k == NFF - 1 and n == 2))
                mm.then_inc(sem("z_used" if k < NFF - 1 else f"ended{s}"), 1)

            def there(g, k):
                pe.wait_ge(sem(f"z_lo{slot(g, k // 2)}"), uses(g, k // 2) + 1)

            def ready(turn, s):
                hold(pe, gate["pe"], sem(f"lo{s}"), turn + 1)
                hold(pe, gate["pe"], sem(f"x2_{s}"), turn)

            for g in range(HALVES):
                if g == 0:
                    for s in range(2):
                        ready(0, s)
                    for k in range(NFF):
                        there(g, k)
                        for s in range(2):
                            sums(s, k)
                else:
                    for s in range(2):
                        ready(g * TURNS, s)
                        for k in range(NFF):
                            there(g, k)
                            sums(s, k)
                with nc.tensor.Fori(1, TURNS) as i:
                    for s in range(2):
                        ready(nc.tensor.snap(i + g * TURNS), s)
                        for k in range(NFF):
                            sums(s, k)

        @block.vector
        def _(dve):
            def add(g, i, turn, s):
                hold(dve, gate["dve"], sem(f"ended{s}"), held(nc.vector, turn + 1))
                tile = held(nc.vector, 2 * i + s)
                xs = x[:, bass.ds(tile, 1), cols(g)]
                nc.vector.scalar_tensor_tensor(out=xs, in0=ps[s][:].unsqueeze(1), scalar=t["mod"][:, 0, bass.ds(held(nc.vector, tile + 40), 1)],
                                               in1=xs, op0=ALU.mult, op1=ALU.add).then_inc(sem(f"x2_{s}"), 1)

            dve.wait_ge(sem("hi1"), 1)
            nc.vector.tensor_tensor(w_lo[:, 1], raw[:, 1], w_hi[:, 1].bitcast(F32), ALU.subtract).then_inc(sem("lo1"), 1)
            for g in range(HALVES):
                for j in range(ZT):
                    q = slot(g, j)
                    dve.wait_ge(sem(f"z_hi{q}"), uses(g, j) + 1)
                    k = slice(2 * j, 2 * j + 2)
                    nc.vector.tensor_tensor(z_lo[:, k], z_raw[:, q], z_hi[:, k].bitcast(F32), ALU.subtract).then_inc(sem(f"z_lo{q}"), 1)
                for s in range(2):
                    add(g, 0, g * TURNS, s)
                with nc.vector.Fori(1, TURNS) as i:
                    turn = nc.vector.snap(i + g * TURNS)
                    for s in range(2):
                        add(g, i, turn, s)


def attention(nc, d, t):
    NT = 4
    QT = SEQ // P
    FOX, SB = 4, 2
    W_POOL = ((2, 4), (8, 16))
    RIM = 16
    cols = lambda g: slice(BANK * g, BANK * (g + 1))
    with ExitStack() as st:
        sem = Sems(nc, st, "g_")
        sb = lambda n, s, dt=F32: st.enter_context(nc.sbuf_tensor("g_" + n, s, dt))
        raw = t["raw_2"]
        w_hi, w_lo = sb("w_hi", [P, NT, KD, P], F32R), sb("w_lo", [P, NT, KD, P], F32R)
        q, k, v = sb("q", [P, SEQ]), sb("k", [P, SEQ]), sb("v", [P, SEQ])
        sq, rstd = sb("sq", [P, 2, SEQ]), sb("rstd", [P, 2, SEQ])
        vt = sb("vt", [P, QT, P])
        gs = sb("gs", [P, SEQ])
        out = sb("out", [P, SEQ])
        qz = sb("qz", [P, 2, SEQ])
        negc = sq
        sc = sb("sc", [P, 2, SEQ])
        logf, cum = sc[0:8], rstd[0:8, 1]
        s2 = sb("s2", [P, 2, SEQ])
        pt = sb("pt", [P, 2, QT, P])
        mx, den, rden = sb("mx", [P, 2]), sb("den", [P, 4]), sb("rden", [P, 4])
        ot = sb("ot", [P, 2, P])
        qg8 = sb("qg8", [P, 1])
        wpool = sb("wpool", [P, 2, P])
        ps = [st.enter_context(nc.psum_tensor(f"g_ps{n}", [P, BANK], F32)) for n in range(2)]
        pb = [st.enter_context(nc.psum_tensor(f"g_pb{n}", [P, 2 * BANK], F32)) for n in range(3)]
        gate = {n: sem("passed_" + n) for n in ("pe", "sp", "act", "dve", "pool")}
        h_hi, h_lo, ident = t["h3_hi"], t["h3_lo"], t["c_ident"]
        TURNS = 2 + FOX + SB
        block = st.enter_context(nc.Block())
        full = {n: sem("full_" + n) for n in ("pb0", "pb1", "pb2", "ps0", "ps1")}
        free = {n: sem("free_" + n) for n in ("pb0", "pb1", "pb2", "ps0", "ps1")}
        buf = {"pb0": pb[0], "pb1": pb[1], "pb2": pb[2], "ps0": ps[0], "ps1": ps[1]}
        UNITS = 2 * QT
        USES_POOL = {"pb0": 2, "pb1": 2, "pb2": 2, "ps0": 1, "ps1": 1}
        USES_FOX = {"pb0": 2 + QT, "pb1": 2 + QT, "pb2": 2 + UNITS, "ps0": 1 + UNITS, "ps1": 1 + QT}
        USES_SB = {"pb0": 1 + QT, "pb1": 1 + QT, "pb2": 2 + UNITS, "ps0": 1 + UNITS, "ps1": 1 + QT}
        unit = lambda u: (u // 2, u % 2, P * (u // 2 + 1))

        def bases(eng, i, sbr):
            if not sbr:
                return {n: eng.snap(i * USES_FOX[n] + USES_POOL[n]) for n in full}
            return {n: eng.snap(i * USES_SB[n] + (USES_POOL[n] + FOX * USES_FOX[n])) for n in full}

        @block.sync
        def _(sp):
            def wait(s, value):
                hold(sp, gate["sp"], s, value)

            def load(n):
                for tl in range(NT):
                    wait(sem(f"lo{tl}"), n)
                sp.dma_start(raw, d["w2"][n]).then_inc(sem("raw"), 16)

            def store(n, tile):
                wait(sem("out"), held(nc.sync, n + 1))
                sp.dma_start(d["mix2"][:, tile], out[:]).then_inc(sem("stored"), 16)

            sp.wait_ge(sem("wpool0"), 1)
            for g in range(4):
                half = slice(HEAD * (g % 2), HEAD * (g % 2) + HEAD)
                sp.dma_start(wpool[half, g // 2, half], d["w_pool"][g]).then_inc(sem("wpool"), 16)
            def load_sums(i):
                wait(full["pb1"], held(nc.sync, i * USES_FOX["pb1"] + (USES_POOL["pb1"] + 2)))
                sp.dma_start(negc[:], d["cums"][bass.ds(2 * i, 2)].unsqueeze(0).broadcast_to([P, 2, SEQ])).then_inc(sem("negc"), 16)

            sp.wait_ge(sem("cum"), 1)
            sp.dma_start(d["cums"], cum).then_inc(sem("cums"), 16)
            for j in range(2):
                load(j + 1)
                store(j, FOX + j)
            sp.wait_ge(sem("cums"), 16)
            with nc.sync.Fori(0, FOX) as i:
                load(nc.sync.snap(i + 3))
                load_sums(i)
                store(nc.sync.snap(i + 2), i)
            load(7)
            store(2 + FOX, FOX + 2)
            store(3 + FOX, FOX + 3)
            sp.wait_ge(sem("stored"), 16 * TURNS)

        @block.tensor
        def _(pe):
            def wait(s, value):
                hold(pe, gate["pe"], s, value)

            def tile(n, tl, outs):
                wait(sem(f"hi{tl}"), n + 1)
                wait(sem(f"lo{tl}"), n + 1)
                for g, (o, name, reads) in enumerate(outs):
                    wait(free[name], reads)
                    mm = product(nc, o, w_hi[:, tl], w_lo[:, tl], h_hi, h_lo, KD, cols(g))
                    if g or outs[1][1] != name:
                        mm.then_inc(full[name], 1)

            def both(name, reads):
                return [(buf[name][:, cols(g)], name, reads) for g in range(2)]

            def pooled_turn(j):
                if j == 0:
                    tile(0, 0, [(ps[0][:], "ps0", 0), (ps[1][:], "ps1", 0)])
                    pe.wait_ge(sem("wpool"), 64)
                tile(j, 1 - j, both("pb0", j))
                tile(j, 2 - j, both("pb1", j))
                pe.wait_ge(sem("pooled"), j + 1)
                wait(free["pb2"], j)
                for g in range(2):
                    mm = nc.tensor.matmul(pb[2][:, cols(g)], wpool[:, j], q[:, cols(g)], start=True, stop=True)
                mm.then_inc(full["pb2"], 1)

            def scores(u, first, base, mask):
                qt, h, keys = unit(u)
                name = f"pb{u % 2}"
                wait(free[name], base[name] + (first + u // 2))
                for at in range(0, keys, BANK):
                    to = min(keys, at + BANK)
                    mm = nc.tensor.matmul(buf[name][:, at:to], qz[:, h, P * qt:P * (qt + 1)], k[:, at:to], start=True,
                                          stop=(to < keys))
                mm = nc.tensor.matmul(buf[name][:, keys - P:keys], ident, mask, start=False, stop=True)
                mm.then_inc(full[name], 1)

            def turn_weights(u, base, sbr):
                qt, h, keys = unit(u)
                wait(sem(f"weights{u % 2}"), base[f"w{u % 2}"] + (u // 2 + 1))
                wait(free["pb2"], base["pb2"] + (2 + u))
                for b in range(qt + 1):
                    mm = nc.tensor.transpose(pb[2][:, P * b:P * (b + 1)], (sc if sbr else s2)[:, u % 2, P * b:P * (b + 1)], ident)
                mm.then_inc(full["pb2"], 1)

            def values(u, base):
                qt, h, keys = unit(u)
                wait(free["pb2"], base["pb2"] + (3 + u))
                wait(free["ps0"], base["ps0"] + (1 + u))
                for b in range(qt + 1):
                    mm = nc.tensor.matmul(ps[0][:, 0:HEAD], pt[:, u % 2, b], vt[:, b, HEAD * h:HEAD * (h + 1)],
                                          start=(b == 0), stop=(b == qt))
                mm.then_inc(full["ps0"], 1)

            def turn_output(qt, base):
                wait(free["ps0"], base["ps0"] + (1 + 2 * (qt + 1)))
                wait(free["ps1"], base["ps1"] + (1 + qt))
                nc.tensor.transpose(ps[1][:, 0:P], ot[:, qt % 2], ident).then_inc(full["ps1"], 1)

            def heads(n, i, sbr):
                base = bases(nc.tensor, i, sbr)
                w = nc.tensor.snap(i * QT + (FOX * QT if sbr else 0))
                base.update(w0=w, w1=w)
                def norm_sums(x):
                    name = f"pb{x}"
                    wait(sem("sq"), i * 2 + (x + 1))
                    wait(free[name], base[name] + 1)
                    for g in range(2):
                        mm = nc.tensor.matmul(buf[name][:, cols(g)], t["c_headones"], sq[:, x, cols(g)], start=True, stop=True)
                    mm.then_inc(full[name], 1)

                tile(n, 0, both("pb0", base["pb0"]))
                tile(n, 1, both("pb1", base["pb1"]))
                if not sbr:
                    norm_sums(0)
                tile(n, 2, both("pb2", base["pb2"]))
                if not sbr:
                    norm_sums(1)
                tile(n, 3, [(ps[0][:], "ps0", base["ps0"]), (ps[1][:], "ps1", base["ps1"])])
                wait(free["pb2"], base["pb2"] + 1)
                for b in range(QT):
                    mm = nc.tensor.transpose(pb[2][:, P * b:P * (b + 1)], v[:, P * b:P * (b + 1)], ident)
                mm.then_inc(full["pb2"], 1)
                if not sbr:
                    wait(sem("qk"), i * 2 + 2)
                else:
                    for name in ("pb0", "pb1"):
                        wait(free[name], base[name] + 1)
                wait(free["pb2"], base["pb2"] + 2)
                first = 1 if sbr else 2
                mask = t["c_negstrict"] if sbr else t["c_negcausal"]
                scores(0, first, base, mask)
                scores(1, first, base, mask)
                for u in range(UNITS + 3):
                    if u < UNITS:
                        turn_weights(u, base, sbr)
                    if u + 2 < UNITS:
                        scores(u + 2, first, base, mask)
                    if 1 <= u <= UNITS:
                        values(u - 1, base)
                    if u >= 3 and u % 2:
                        turn_output((u - 3) // 2, base)

            for j in range(2):
                pooled_turn(j)
            with nc.tensor.Fori(0, FOX) as i:
                heads(nc.tensor.snap(i + 2), i, False)
            with nc.tensor.Fori(0, SB) as i:
                heads(nc.tensor.snap(i + (2 + FOX)), i, True)

        @block.scalar
        def _(act):
            def wait(s, value):
                hold(act, gate["act"], s, value)

            def split_hi(n, tl):
                if isinstance(n, int) and n == 0:
                    act.wait_ge(t["ahead"]("w2"), 16)
                else:
                    wait(sem("raw"), n * 16)
                nc.scalar.activation(w_hi[:, tl], raw[:, tl], ACT.Copy).then_inc(sem(f"hi{tl}"), 1)

            def pooled_turn(j):
                if j == 0:
                    for g in range(2):
                        act.wait_ge(full[f"ps{g}"], 1)
                        nc.scalar.activation(logf[:, 0, cols(g)], ps[g][0:8, :], ACT.Abs, bias=t["v_b_f"][0:8]).then_inc(sem("ff"), 1)
                    act.wait_ge(sem("ff"), 2)
                    nc.scalar.activation(logf[:, 0], logf[:, 0], ACT.Exp, scale=-1.0).then_inc(sem("ff"), 1)
                    act.wait_ge(sem("ff"), 3)
                    nc.scalar.activation(logf[:, 0], logf[:, 0], ACT.Ln, bias=1.0).then_inc(sem("ff"), 1)
                act.wait_ge(full["pb0"], j + 1)
                act.wait_ge(sem("pooled"), j)
                nc.scalar.activation(v[:], pb[0][:], ACT.Copy).then_inc(free["pb0"], 1)
                act.wait_ge(full["pb1"], j + 1)
                act.wait_ge(sem("out"), j)
                nc.scalar.activation(gs[:], pb[1][:], ACT.Silu).then_inc(free["pb1"], 1)
                for tl in range(NT):
                    split_hi(j + 1, tl)

            def heads(n, i, sbr, last):
                base = bases(nc.scalar, i, sbr)
                for tl, name, dst in ((0, "pb0", q), (1, "pb1", k), (2, "pb2", v)):
                    wait(full[name], base[name] + 1)
                    if sbr and tl == 0:
                        for h in range(2):
                            rows = slice(HEAD * h, HEAD * h + HEAD)
                            a = nc.scalar.activation(qz[rows, h], buf[name][rows, :], ACT.Copy, scale=0.125)
                        a.then_inc(free[name], 1)
                    else:
                        nc.scalar.activation(dst[:], buf[name][:], ACT.Copy).then_inc(free[name], 1)
                    if not last:
                        split_hi(n + 1, tl)
                    if not sbr and tl:
                        x, norms = tl - 1, f"pb{tl - 1}"
                        wait(full[norms], base[norms] + 2)
                        nc.scalar.activation(rstd[:, x], buf[norms][:], ACT.Sqrt, scale=1.0 / HEAD, bias=t["c_eps"]).then_inc(free[norms], 1)
                wait(sem("out"), n)
                for g in range(2):
                    wait(full[f"ps{g}"], base[f"ps{g}"] + 1)
                    nc.scalar.activation(gs[:, cols(g)], ps[g][:], ACT.Silu).then_inc(free[f"ps{g}"], 1)
                if not last:
                    split_hi(n + 1, 3)
                wait(full["pb2"], base["pb2"] + 2)
                nc.scalar.activation(vt[:].rearrange("p b c -> p (b c)"), pb[2][:], ACT.Copy).then_inc(free["pb2"], 1)
                if not sbr:
                    for u in range(UNITS):
                        qt, h, keys = unit(u)
                        wait(sem("mx"), i * UNITS + (u + 1))
                        if u >= 2:
                            wait(full["pb2"], base["pb2"] + (2 + u - 1))
                        nc.scalar.activation(s2[:, u % 2, 0:keys], sc[:, u % 2, 0:keys], ACT.Exp, bias=mx[:, u % 2:u % 2 + 1],
                                             accum_out=den[:, u % 4:u % 4 + 1]).then_inc(sem(f"weights{u % 2}"), 1)
                else:
                    for u in range(UNITS):
                        qt, h, keys = unit(u)
                        name = f"pb{u % 2}"
                        wait(full[name], base[name] + (2 + u // 2))
                        if u >= 2:
                            wait(full["pb2"], base["pb2"] + (2 + u - 1))
                        nc.scalar.activation(sc[:, u % 2, 0:keys], buf[name][:, 0:keys], ACT.Sigmoid)
                        nc.scalar.activation(s2[:, u % 2, 0:keys], buf[name][:, 0:keys], ACT.Sigmoid, scale=-1.0).then_inc(free[name], 1)

            for tl in range(NT):
                split_hi(0, tl)
            for j in range(2):
                pooled_turn(j)
            with nc.scalar.Fori(0, FOX) as i:
                heads(nc.scalar.snap(i + 2), i, False, False)
            with nc.scalar.Fori(0, 1) as i:
                heads(nc.scalar.snap(i + (2 + FOX)), i, True, False)
            with nc.scalar.Fori(1, 2) as i:
                heads(nc.scalar.snap(i + (2 + FOX)), i, True, True)

        @block.gpsimd
        def _(pool):
            nc.gpsimd.memset(wpool[:], 0.0).then_inc(sem("wpool0"), 1)
            with nc.gpsimd.Fori(0, TURNS) as n:
                for tl in range(NT):
                    hold(pool, gate["pool"], sem(f"hi{tl}"), n + 1)
                    nc.gpsimd.tensor_tensor(w_lo[:, tl], raw[:, tl], w_hi[:, tl].bitcast(F32), ALU.subtract).then_inc(sem(f"lo{tl}"), 1)

        @block.vector
        def _(dve):
            TT, TS, STT = nc.vector.tensor_tensor, nc.vector.tensor_scalar, nc.vector.scalar_tensor_tensor

            def wait(s, value):
                hold(dve, gate["dve"], s, value)

            def ones(n):
                return t["c_ones"][:, 0:1].broadcast_to([P, n])

            def forget_sums():
                for g in range(2):
                    dve.wait_ge(sem("ff"), 4)
                    TS(logf[:, 1, cols(g)], ps[g][0:8, :], t["v_b_f"][0:8], 0.0, ALU.add, ALU.min).then_inc(free[f"ps{g}"], 1)
                for g in range(2):
                    dve.wait_ge(free[f"ps{g}"], 1)
                TT(logf[:, 1], logf[:, 0], logf[:, 1], ALU.subtract).then_inc(sem("logf"), 1)
                dve.wait_ge(sem("logf"), 1)
                nc.vector.tensor_tensor_scan(cum, ones(SEQ)[0:8], logf[:, 1], 0.0, ALU.mult, ALU.add).then_inc(sem("cum"), 1)

            def pooled_turn(j):
                run = sq[:].rearrange("p x s -> p (x s)")
                dve.wait_ge(free["pb0"], j + 1)
                dve.wait_ge(sem("rim"), 1)
                nc.vector.tensor_tensor_scan(run[:, RIM:RIM + SEQ], ones(SEQ), v[:], 0.0, ALU.mult, ALU.add).then_inc(sem("run"), 1)
                dve.wait_ge(sem("run"), j + 1)
                mean = rstd[:, 0]
                for h, win in enumerate(W_POOL[j]):
                    rows = slice(HEAD * h, HEAD * h + HEAD)
                    TT(mean[rows], run[rows, RIM:RIM + SEQ], run[rows, RIM - win:RIM + SEQ - win], ALU.subtract).then_inc(sem("diff"), 1)
                dve.wait_ge(sem("diff"), 2 * j + 2)
                TT(mean[:, 0:RIM], mean[:, 0:RIM], t["c_invcount"][:, j], ALU.mult).then_inc(sem("mean"), 1)
                STT(out=q[:, RIM:SEQ], in0=mean[:, RIM:SEQ], scalar=t["c_invwin"][:, j:j + 1], in1=v[:, RIM:SEQ],
                    op0=ALU.mult, op1=ALU.subtract).then_inc(sem("rest"), 1)
                dve.wait_ge(sem("mean"), j + 1)
                dve.wait_ge(sem("rest"), j + 1)
                TT(q[:, 0:RIM], mean[:, 0:RIM], v[:, 0:RIM], ALU.subtract).then_inc(sem("pooled"), 1)
                dve.wait_ge(full["pb2"], j + 1)
                dve.wait_ge(free["pb1"], j + 1)
                dve.wait_ge(sem("stored"), 16 * j)
                STT(out=out[:], in0=pb[2][:], scalar=t["v_pool_scale"][:, j:j + 1], in1=gs[:], op0=ALU.mult,
                    op1=ALU.mult).then_inc(free["pb2"], 1)
                dve.wait_ge(free["pb2"], j + 1)
                dve.sem_inc(sem("out"), 1)

            def heads(n, i, sbr):
                base = bases(nc.vector, i, sbr)

                def mid_fox(u):
                    qt, h, keys = unit(u)
                    name = f"pb{u % 2}"
                    wait(full[name], base[name] + (3 + u // 2))
                    if u >= 2:
                        wait(sem(f"weights{u % 2}"), i * QT + u // 2)
                    nc.vector.tensor_tensor_reduce(out=sc[:, u % 2, 0:keys], in0=buf[name][:, 0:keys], in1=negc[:, h, 0:keys],
                                                   scale=1.0, scalar=-3.0e38, op0=ALU.add, op1=ALU.max,
                                                   accum_out=mx[:, u % 2:u % 2 + 1]).then_inc(free[name], 1)
                    wait(free[name], base[name] + (3 + u // 2))
                    TS(mx[:, u % 2:u % 2 + 1], mx[:, u % 2:u % 2 + 1], -1.0, None, ALU.mult).then_inc(sem("mx"), 1)

                def mid_sb(u):
                    qt, h, keys = unit(u)
                    name = f"pb{u % 2}"
                    x, y = sc[:, u % 2, 0:keys], s2[:, u % 2, 0:keys]
                    wait(free[name], base[name] + (2 + u // 2))
                    nc.vector.tensor_tensor_scan(y[:, ::-1], y[:, ::-1], ones(keys), 1.0, ALU.mult, ALU.mult).then_inc(sem("left"), 1)
                    wait(sem("left"), i * UNITS + (u + 1))
                    TT(x[:, 0:keys - 1], x[:, 0:keys - 1], y[:, 1:keys], ALU.mult).then_inc(sem(f"weights{u % 2}"), 1)

                def weights_out(u):
                    qt, h, keys = unit(u)
                    wait(full["pb2"], base["pb2"] + (3 + u))
                    if u >= 2:
                        wait(full["ps0"], base["ps0"] + (1 + u - 1))
                    nc.vector.tensor_copy(pt[:, u % 2, 0:qt + 1].rearrange("p b c -> p (b c)"), pb[2][:, 0:keys]).then_inc(free["pb2"], 1)

                def values_out(u):
                    qt, h, keys = unit(u)
                    dst = ot[:, qt % 2, HEAD * h:HEAD * (h + 1)]
                    if not sbr:
                        wait(sem(f"weights{u % 2}"), i * QT + (u // 2 + 1))
                        nc.vector.reciprocal(rden[:, u % 4:u % 4 + 1], den[:, u % 4:u % 4 + 1]).then_inc(sem("rden"), 1)
                        wait(sem("rden"), i * UNITS + (u + 1))
                    wait(full["ps0"], base["ps0"] + (2 + u))
                    if qt >= 2:
                        wait(full["ps1"], base["ps1"] + (1 + qt - 1))
                    if sbr:
                        nc.vector.tensor_copy(dst, ps[0][:, 0:HEAD]).then_inc(free["ps0"], 1)
                    else:
                        TS(dst, ps[0][:, 0:HEAD], rden[:, u % 4:u % 4 + 1], None, ALU.mult).then_inc(free["ps0"], 1)

                def gated(qt):
                    wait(full["ps1"], base["ps1"] + (2 + qt))
                    TT(out[:, P * qt:P * (qt + 1)], ps[1][:, 0:P], gs[:, P * qt:P * (qt + 1)], ALU.mult).then_inc(free["ps1"], 1)

                if not sbr:
                    for x, name, src in ((0, "pb0", q), (1, "pb1", k)):
                        wait(free[name], base[name] + 1)
                        TT(sq[:, x], src[:], src[:], ALU.mult).then_inc(sem("sq"), 1)
                    for x, name, src, g in ((0, "pb0", q, qg8[:]), (1, "pb1", k, t["v_kg"])):
                        wait(free[name], base[name] + 2)
                        nc.vector.reciprocal(rstd[:, x], rstd[:, x]).then_inc(sem("rstd"), 1)
                        wait(sem("rstd"), i * 2 + (x + 1))
                        if x == 0:
                            for h in range(2):
                                rows = slice(HEAD * h, HEAD * h + HEAD)
                                a = STT(out=qz[rows, h], in0=q[rows], scalar=g[rows], in1=rstd[rows, 0], op0=ALU.mult, op1=ALU.mult)
                        else:
                            a = STT(out=k[:], in0=k[:], scalar=g, in1=rstd[:, 1], op0=ALU.mult, op1=ALU.mult)
                        a.then_inc(sem("qk"), 1)
                    wait(sem("negc"), i * 16 + 16)
                wait(sem("stored"), n * 16)
                mid = mid_sb if sbr else mid_fox
                mid(0)
                mid(1)
                for u in range(UNITS + 3):
                    if u < UNITS:
                        weights_out(u)
                    if u + 2 < UNITS:
                        mid(u + 2)
                    if 1 <= u <= UNITS:
                        values_out(u - 1)
                    if u >= 3 and u % 2:
                        gated((u - 3) // 2)
                wait(free["ps1"], base["ps1"] + (1 + QT))
                dve.sem_inc(sem("out"), 1)

            nc.vector.memset(sq[:, 0, 0:RIM], 0.0).then_inc(sem("rim"), 1)
            nc.vector.memset(qz[:], 0.0).then_inc(sem("rim"), 1)
            TS(qg8[:], t["v_qg"], 0.125, None, ALU.mult).then_inc(sem("qg8"), 1)
            forget_sums()
            for j in range(2):
                pooled_turn(j)
            dve.wait_ge(sem("cum"), 1)
            dve.wait_ge(sem("qg8"), 1)
            with nc.vector.Fori(0, FOX) as i:
                heads(nc.vector.snap(i + 2), i, False)
            with nc.vector.Fori(0, SB) as i:
                heads(nc.vector.snap(i + (2 + FOX)), i, True)


def output(nc, d, t):
    G = range(2)
    cols = lambda g: slice(BANK * g, BANK * (g + 1))
    with ExitStack() as st:
        sem = Sems(nc, st, "h_")
        sb = lambda n, s, dt=F32: st.enter_context(nc.sbuf_tensor("h_" + n, s, dt))
        mix, x3 = sb("mix", [P, KD, SEQ]), sb("x3", [P, KD, SEQ])
        m_hi, m_lo = sb("m_hi", [P, KD, SEQ], F32R), sb("m_lo", [P, KD, SEQ], F32R)
        raw = sb("raw", [P, 2, KD, P])
        w_hi, w_lo = sb("w_hi", [P, 2, KD, P], F32R), sb("w_lo", [P, 2, KD, P], F32R)
        ps = [st.enter_context(nc.psum_tensor(f"h_ps{n}", [P, BANK], F32)) for n in range(4)]
        full = [sem(f"psum_full{b}") for b in range(4)]
        free = [sem(f"psum_free{b}") for b in range(4)]
        gate = {n: sem("passed_" + n) for n in ("pe", "sp", "act", "dve", "pool")}
        block = st.enter_context(nc.Block())

        @block.sync
        def _(sp):
            sp.dma_start(raw[:], d["w_out_2"][0]).then_inc(sem("raw"), 16)
            for k in range(KD):
                sp.dma_start(mix[:, k], d["mix2"][:, k]).then_inc(sem(f"mix{k}"), 16)
            sp.dma_start(x3[:], d["x3s"]).then_inc(sem("x3"), 16)

            def store(i):
                for s in range(2):
                    for g in G:
                        hold(sp, gate["sp"], free[2 * s + g], held(nc.sync, i + 2))
                    sp.dma_start(d["out"][2 * i + s], x3[:, 2 * i + s]).then_inc(sem("stored"), 16)

            with nc.sync.Fori(0, 3) as i:
                n = nc.sync.snap(i + 1)
                for s in range(2):
                    hold(sp, gate["sp"], sem(f"lo{s}"), n)
                sp.dma_start(raw[:], d["w_out_2"][n]).then_inc(sem("raw"), 16)
                store(nc.sync.snap(i + 0))
            store(3)
            sp.wait_ge(sem("stored"), 16 * KD)

        @block.tensor
        def _(pe):
            def turn(n, first):
                for s in range(2):
                    hold(pe, gate["pe"], sem(f"hi{s}"), n)
                    hold(pe, gate["pe"], sem(f"lo{s}"), n)
                    for g in G:
                        b = 2 * s + g
                        hold(pe, gate["pe"], free[b], n)
                        if first and s == 0:
                            if g == 0:
                                continue
                            for k in range(KD):
                                pe.wait_ge(sem("mix_lo"), k + 1)
                                for half in G:
                                    for m, (w, x) in enumerate(((w_hi, m_hi), (w_hi, m_lo), (w_lo, m_hi))):
                                        mm = nc.tensor.matmul(ps[half][:], w[:, 0, k], x[:, k, cols(half)], start=(k == 0 and m == 0),
                                                              stop=(k == KD - 1 and m == 2))
                                    if k == KD - 1:
                                        mm.then_inc(full[half], 1)
                        else:
                            product(nc, ps[b][:], w_hi[:, s], w_lo[:, s], m_hi, m_lo, KD, cols(g)).then_inc(full[b], 1)

            turn(1, True)
            with nc.tensor.Fori(2, 5) as n:
                turn(n, False)

        @block.scalar
        def _(act):
            def split_hi(n, s):
                hold(act, gate["act"], sem("raw"), n * 16 + 16)
                if not isinstance(n, int):
                    hold(act, gate["act"], full[2 * s + 1], n)
                nc.scalar.activation(w_hi[:, s], raw[:, s], ACT.Copy).then_inc(sem(f"hi{s}"), 1)

            for s in range(2):
                split_hi(0, s)
            for k in range(KD):
                act.wait_ge(sem(f"mix{k}"), 16)
                nc.scalar.activation(m_hi[:, k], mix[:, k], ACT.Copy).then_inc(sem("mix_hi"), 1)
            with nc.scalar.Fori(1, 4) as n:
                for s in range(2):
                    split_hi(n, s)

        @block.gpsimd
        def _(pool):
            with nc.gpsimd.Fori(0, 4) as n:
                for s in range(2):
                    hold(pool, gate["pool"], sem(f"hi{s}"), n + 1)
                    nc.gpsimd.tensor_tensor(w_lo[:, s], raw[:, s], w_hi[:, s].bitcast(F32), ALU.subtract).then_inc(sem(f"lo{s}"), 1)

        @block.vector
        def _(dve):
            for b in range(4):
                dve.sem_inc(free[b], 1)
            for k in range(KD):
                dve.wait_ge(sem("mix_hi"), k + 1)
                nc.vector.tensor_tensor(m_lo[:, k], mix[:, k], m_hi[:, k].bitcast(F32), ALU.subtract).then_inc(sem("mix_lo"), 1)
            dve.wait_ge(sem("x3"), 16)
            with nc.vector.Fori(0, 4) as i:
                n = nc.vector.snap(i + 1)
                for s in range(2):
                    for g in G:
                        b = 2 * s + g
                        hold(dve, gate["dve"], full[b], n)
                        xs = x3[:, bass.ds(2 * i + s, 1), cols(g)]
                        nc.vector.tensor_tensor(xs, ps[b][:].unsqueeze(1), xs, ALU.add).then_inc(free[b], 1)


DRAM_IN = {"vecs": [P, NVEC], "consts": [P, NCON], "xT": [P, KD, SEQ], "ctxT": [P, KD, CTX], "ada": [24, P, 2, KD, P],
           "w1": [26, P, KD, P], "lora": [PAIRS, P, 2, P], "g_up": [P, CH], "w_out": [4, P, 2, KD, P],
           "w_ffn": [NFF, P, 2, KD, P], "w_down": [KD, P, NFF, P], "w2": [8, P, 4, KD, P], "w_pool": [4, HEAD, HEAD],
           "w_out_2": [4, P, 2, KD, P]}
SCRATCH = {"ops": [2, 4, PAIRS, P, SLOTS * C], "vts": [SLOTS, P, PAIRS, C], "mixd": [P, KD, SEQ], "sgs": [P, SEQ],
           "ys": [2, PAIRS, P, SLOTS * C], "zs": [NFF, P, SEQ], "x3s": [P, KD, SEQ], "mix2": [P, KD, SEQ], "cums": [8, SEQ]}


def program(nc):
    d = {n: nc.dram_tensor(n, s, F32, kind="ExternalInput").ap() for n, s in DRAM_IN.items()}
    d.update({n: nc.dram_tensor(n, s, F32, kind="Internal").ap() for n, s in SCRATCH.items()})
    d["out"] = nc.dram_tensor("out", [KD, P, SEQ], F32, kind="ExternalOutput").ap()
    with ExitStack() as whole:
        ahead = Sems(nc, whole, "ahead_")
        keep = lambda st, n, s, dt=F32, **k: st.enter_context(nc.sbuf_tensor(n, s, dt, **k))[:]
        t = {"vec": keep(whole, "vec", [P, NVEC]), "con": keep(whole, "con", [P, NCON]),
             "mod": keep(whole, "mod", [P, 2, 48]), "silu_c": keep(whole, "silu_c", [P, KD, 2]),
             "c_eps": keep(whole, "eps", [P, 1]), "c_gneps": keep(whole, "gneps", [P, 1]),
             "ahead": ahead}
        for n, (at, m) in VECS.items():
            t["v_" + n] = t["vec"][:, at:at + m]
        for n, (at, m) in CONS.items():
            t["c_" + n] = t["con"][:, at:at + m]
        for n in ("strict", "mask_u1"):
            t["c_" + n] = t["c_" + n].rearrange("p (x h c) -> p x h c", x=2, h=2)
        for n in ("incl", "reset", "invcount"):
            t["c_" + n] = t["c_" + n].rearrange("p (x c) -> p x c", x=2)
        t["c_mask_lev"] = t["c_mask_lev"].rearrange("p (x l c) -> p x l c", x=2, l=LEVELS)
        with ExitStack() as mixer:
            t["pend"] = keep(mixer, "pend", [P, 2, SLOTS, PAIRS], side="right")
            with ExitStack() as st:
                t["raw_in"] = keep(st, "raw_in", [P, KD, P])
                t["h_hi"], t["h_lo"] = keep(st, "h_hi", [P, KD, TOK], F32R), keep(st, "h_lo", [P, KD, TOK], F32R)
                prologue(nc, d, t)
                projections(nc, d, t)
            scan(nc, d, t)
        with ExitStack() as rest:
            t["x"] = keep(rest, "x", [P, KD, SEQ], side="right")
            down = rest.enter_context(ExitStack())
            with ExitStack() as st:
                t["h2_hi"], t["h2_lo"] = keep(st, "h2_hi", [P, KD, SEQ], F32R), keep(st, "h2_lo", [P, KD, SEQ], F32R)
                mixer_out(nc, d, t)
                t["raw_down"] = keep(down, "raw_down", [P, 2, NFF, P], side="right")
                t["raw_up"] = keep(st, "raw_up", [P, 2, KD, P])
                norm_x1(nc, d, t)
                ffn_up(nc, d, t)
            ffn_down(nc, d, t)
            down.close()
            h3 = whole.enter_context(ExitStack())
            t["raw_2"] = keep(h3, "raw_2", [P, 4, KD, P])
            t["h3_hi"], t["h3_lo"] = keep(h3, "h3_hi", [P, KD, SEQ], F32R), keep(h3, "h3_lo", [P, KD, SEQ], F32R)
            norm_x3(nc, d, t)
        attention(nc, d, t)
        h3.close()
        output(nc, d, t)


def constants():
    row, col = np.arange(P)[:, None], np.arange(P)[None, :]
    s, u = (np.arange(P) % C)[:, None], np.arange(C)[None, :]
    tri = lambda keep: keep.astype(np.float32)
    parts = {"ident": np.eye(P), "ones": np.ones((P, P)), "headones": tri(row // HEAD == col // HEAD),
             "negcausal": -1e30 * tri(col > row), "negstrict": -1e30 * tri(col >= row)}
    before = [s < u, s > u]
    after = [s > u, s < u]
    head = row // HEAD
    parts["strict"] = np.concatenate([tri(b & (head == h)) for b in before for h in range(2)], 1)
    parts["incl"] = np.concatenate([tri(b | (s == u)) for b in before], 1)
    block = lambda m: s // m == u // m
    parts["mask_u1"] = np.concatenate([-tri(b & block(2) & (head == h)) for b in before for h in range(2)], 1)
    parts["mask_lev"] = np.concatenate([tri(a & block(2 ** (l + 2)) & ~block(2 ** (l + 1))) for a in after for l in range(LEVELS)], 1)
    first = np.tile(np.arange(C), BANK // C)[None, :]
    parts["reset"] = np.concatenate([np.repeat(tri(first != e), P, 0) for e in (0, C - 1)], 1)
    win = np.array([[2] * HEAD + [4] * HEAD, [8] * HEAD + [16] * HEAD]).T[:, :, None]
    parts["invcount"] = (1.0 / np.minimum(np.arange(16)[None, None, :] + 1, win)).reshape(P, 32)
    parts["invwin"] = (1.0 / win).reshape(P, 2)
    return np.concatenate([parts[n].astype(np.float32) for n in CONS], 1)


def kernel(**a):
    import concourse.bacc as bacc
    from concourse.bass_utils import run_bass_kernel_spmd

    a = {n: np.asarray(x) for n, x in a.items()}

    def tiles(w):
        return w.reshape(w.shape[0] // P, P, w.shape[1] // P, P).transpose(2, 1, 0, 3)

    def turns(w, order):
        w = tiles(w)
        return np.ascontiguousarray(w[np.array(order)].transpose(0, 2, 1, 3, 4))

    def column(v):
        return v.reshape(-1, P).T

    def featmajor(x):
        return np.ascontiguousarray(x.T.reshape(KD, P, x.shape[0]).transpose(1, 0, 2))

    w0a0 = np.stack([a["rw_w0"][0], a["rw_a0"][0]], 1)
    vec = {"norm1_g": column(a["norm1_g"][0]), "norm2_g": column(a["norm2_g"][0]), "final_g": column(a["final_g"]),
           "norm_g_2": column(a["norm_g_2"][0]), "ada_b": column(a["ada_b"][0]), "conv_a_w": column(a["conv_a_w"][0]),
           "w0a0": column(w0a0), "k_k": column(a["rw_k_k"][0]), "k_a": column(a["rw_k_a"][0]), "r_k": column(a["rw_r_k"][0]),
           "ln_g": column(a["rw_ln_g"][0]), "ln_b": column(a["rw_ln_b"][0]), "ffn_conv_w": column(a["ffn_conv_w"][0]),
           "ffn_conv_b": column(a["ffn_conv_b"][0]), "pool_scale": column(a["pool_scale_2"][0]),
           "cc": np.stack([column(a["c"][0]), column(a["c_ctx"])], 2).reshape(P, 16),
           "qg": np.tile(a["q_norm_g_2"][0], 2)[:, None], "kg": np.tile(a["k_norm_g_2"][0], 2)[:, None],
           "b_f": np.pad(a["b_f_2"][0], (0, P - 8))[:, None]}
    w_in = a["w_in"][0]
    w2 = a["w_in_2"][0]
    at = 4 * CH
    ff = np.pad(w2[:, at:at + 8], ((0, 0), (0, P - 8)))
    w2 = np.concatenate([w2[:, 0:at], w2[:, at + 8:], ff], 1)
    FF, Z = 28, 28
    given = {
        "vecs": np.concatenate([vec[n] for n in VECS], 1), "consts": constants(),
        "xT": featmajor(a["x"][0]), "ctxT": featmajor(a["ctx"][0]),
        "ada": turns(a["ada_w"][0], np.arange(48).reshape(24, 2)),
        "w1": np.ascontiguousarray(tiles(w_in)[np.array([24, 25] + [n + j for j in range(PAIRS) for n in (20, 16, 12)]
                                                        + [n + j for j in range(4) for n in (4, 8, 0)])]),
        "lora": np.concatenate([a["rw_w_up"][0], a["rw_a_up"][0]], 1).reshape(2, P, PAIRS, P).transpose(2, 1, 0, 3),
        "g_up": a["rw_g_up"][0],
        "w_out": turns(a["w_out"][0], np.arange(8).reshape(4, 2)),
        "w_ffn": turns(a["ffn_w_up"][0], [[i, NFF + i] for i in range(NFF)]),
        "w_down": tiles(a["ffn_w_down"][0]),
        "w2": turns(w2, [[FF, 16, 18, Z], [17, 19, Z, Z]] + [[p, 4 + p, 8 + p, 12 + p] for p in range(4)]
                    + [[20 + p, 22 + p, 24 + p, 26 + p] for p in range(2)]),
        "w_pool": a["w_pool_2"][0], "w_out_2": turns(a["w_out_2"][0], np.arange(8).reshape(4, 2)),
    }
    nc = bacc.Bacc("TRN2", target_bir_lowering=False, num_devices=1)
    program(nc)
    got = run_bass_kernel_spmd(nc, [{n: np.ascontiguousarray(x) for n, x in given.items()}], core_ids=[0])
    out = got.results[0]["out"]
    return np.ascontiguousarray(out.reshape(D, SEQ).T)[None]
```
